# Optimizing a Trainium2 kernel written in Bass

```python
import jax, jax.numpy as jnp
from jax import lax
import numpy as np
import math

D_MODEL = 1024
BATCH = 1
SEQ = 1024
DEPTH = 2

GRID_W = 64
D_GROUP = 256
N_GROUPS = 4
D_MIX = N_GROUPS * D_GROUP
HEAD_DIM = 64
CONV_A_WIDTH = 31
CONV_B_WIDTH = 3
SWA_Q_HEADS = D_GROUP // HEAD_DIM
SWA_KV_HEADS = 2
SWA_WINDOW = 128
SWA_BLOCK = 128
NA_HEADS = D_GROUP // HEAD_DIM
NA_KH_MAX = 8
NA_KW = 16
ROPE_THETA = 10000.0
EPS = 1e-6
NEG_INF = -1e30

SPLIT_SIZES = (
    D_GROUP, D_GROUP, D_GROUP,
    D_GROUP, D_GROUP, D_GROUP, D_GROUP,
    SWA_Q_HEADS * HEAD_DIM, SWA_KV_HEADS * HEAD_DIM,
    SWA_KV_HEADS * HEAD_DIM, D_GROUP,
    NA_HEADS * HEAD_DIM, NA_HEADS * HEAD_DIM,
    NA_HEADS * HEAD_DIM, D_GROUP,
)
D_IN = sum(SPLIT_SIZES)


def rmsnorm(x, g):
    x32 = x.astype(jnp.float32)
    y = x32 * lax.rsqrt(jnp.mean(x32 * x32, axis=-1, keepdims=True) + EPS)
    return y.astype(x.dtype) * g

def layernorm(x, g, b):
    x32 = x.astype(jnp.float32)
    mu = jnp.mean(x32, axis=-1, keepdims=True)
    xc = x32 - mu
    y = xc * lax.rsqrt(jnp.mean(xc * xc, axis=-1, keepdims=True) + EPS)
    return y.astype(x.dtype) * g + b

def depthwise_conv(x, w):
    width, ch = w.shape
    pad = (width - 1) // 2
    return lax.conv_general_dilated(
        x, w[:, None, :], window_strides=(1,), padding=[(pad, pad)],
        dimension_numbers=("NWC", "WIO", "NWC"), feature_group_count=ch)

def rope(x, pos):
    d = x.shape[-1]
    inv_freq = ROPE_THETA ** (-jnp.arange(0, d, 2, dtype=jnp.float32) / d)
    ang = pos[:, None] * inv_freq[None, :]
    cos = jnp.cos(ang)[None, :, None, :].astype(x.dtype)
    sin = jnp.sin(ang)[None, :, None, :].astype(x.dtype)
    x1, x2 = x[..., : d // 2], x[..., d // 2:]
    return jnp.concatenate([x1 * cos - x2 * sin, x2 * cos + x1 * sin], axis=-1)

def conformer_conv(u, v, conv_w, conv_b, ln_g, ln_b):
    h = u * jax.nn.sigmoid(v)
    h = depthwise_conv(h, conv_w) + conv_b
    h = layernorm(h, ln_g, ln_b)
    return jax.nn.silu(h)

def short_gated_conv(bg, cg, xv, conv_w):
    return bg * depthwise_conv(cg * xv, conv_w)

def window_gqa(q, k, v, sink):
    b, s, hq, d = q.shape
    hkv = k.shape[2]
    g = hq // hkv
    nb = s // SWA_BLOCK
    pos = jnp.arange(s, dtype=jnp.float32)
    q = rope(q, pos)
    k = rope(k, pos)
    qb = q.reshape(b, nb, SWA_BLOCK, hkv, g, d)
    pad = ((0, 0), (SWA_BLOCK, SWA_BLOCK), (0, 0), (0, 0))
    kp = jnp.pad(k, pad).reshape(b, nb + 2, SWA_BLOCK, hkv, d)
    vp = jnp.pad(v, pad).reshape(b, nb + 2, SWA_BLOCK, hkv, d)
    kw = jnp.concatenate([kp[:, :-2], kp[:, 1:-1], kp[:, 2:]], axis=2)
    vw = jnp.concatenate([vp[:, :-2], vp[:, 1:-1], vp[:, 2:]], axis=2)
    scores = jnp.einsum("bnqhgd,bnkhd->bnhgqk", qb, kw).astype(jnp.float32) * (d ** -0.5)
    blk = jnp.arange(nb)[:, None, None]
    qpos = blk * SWA_BLOCK + jnp.arange(SWA_BLOCK)[None, :, None]
    kpos = (blk - 1) * SWA_BLOCK + jnp.arange(3 * SWA_BLOCK)[None, None, :]
    valid = (jnp.abs(kpos - qpos) <= SWA_WINDOW) & (kpos >= 0) & (kpos < s)
    scores = jnp.where(valid[None, :, None, None], scores, NEG_INF)
    sink_col = jnp.broadcast_to(sink.astype(jnp.float32).reshape(1, 1, hkv, g, 1, 1),
                                scores.shape[:-1] + (1,))
    p = jax.nn.softmax(jnp.concatenate([scores, sink_col], axis=-1), axis=-1)[..., :-1]
    o = jnp.einsum("bnhgqk,bnkhd->bnqhgd", p.astype(v.dtype), vw)
    return o.reshape(b, s, hq * d)

def neighborhood_attn(q, k, v, rpb):
    b, s, h, d = q.shape
    rows = s // GRID_W
    kh = min(NA_KH_MAX, rows)
    r = jnp.arange(rows)
    r0 = jnp.clip(r - kh // 2, 0, rows - kh)
    row_idx = r0[:, None] + jnp.arange(kh)[None, :]
    qg = q.reshape(b, rows, GRID_W, h, d)
    kg = jnp.take(k.reshape(b, rows, GRID_W, h, d), row_idx, axis=1)
    vg = jnp.take(v.reshape(b, rows, GRID_W, h, d), row_idx, axis=1)
    scores = jnp.einsum("brqhd,brikhd->brhqik", qg, kg).astype(jnp.float32) * (d ** -0.5)
    c = jnp.arange(GRID_W)
    c0 = jnp.clip(c - NA_KW // 2, 0, GRID_W - NA_KW)
    col_ok = (c[None, :] >= c0[:, None]) & (c[None, :] < c0[:, None] + NA_KW)
    dr = row_idx - r[:, None] + (NA_KH_MAX - 1)
    dc = jnp.clip(c[None, :] - c[:, None], -(NA_KW - 1), NA_KW - 1) + (NA_KW - 1)
    bias = jnp.take(rpb[:, dr], dc, axis=-1)
    bias = bias.transpose(1, 0, 3, 2, 4).astype(jnp.float32)
    scores = jnp.where(col_ok[:, None, :], scores + bias[None], NEG_INF)
    p = jax.nn.softmax(scores.reshape(b, rows, h, GRID_W, kh * GRID_W), axis=-1)
    p = p.reshape(scores.shape).astype(v.dtype)
    o = jnp.einsum("brhqik,brikhd->brqhd", p, vg)
    return o.reshape(b, s, h * d)

def hybrid_layer(x, norm_g, w_in, w_out, conv_a_w, conv_a_b, ln_a_g, ln_a_b,
                 conv_b_w, swa_sink, na_rpb):
    b, s, _ = x.shape
    h = rmsnorm(x, norm_g)
    proj = jnp.einsum("bsd,de->bse", h, w_in)
    split_points = np.cumsum(SPLIT_SIZES)[:-1].tolist()
    (a_u, a_v, a_z,
     b_b, b_c, b_x, b_z,
     c_q, c_k, c_v, c_z,
     d_q, d_k, d_v, d_z) = jnp.split(proj, split_points, axis=-1)
    y_a = conformer_conv(a_u, a_v, conv_a_w, conv_a_b, ln_a_g, ln_a_b) * jax.nn.silu(a_z)
    y_b = short_gated_conv(b_b, b_c, b_x, conv_b_w) * jax.nn.silu(b_z)
    y_c = window_gqa(c_q.reshape(b, s, SWA_Q_HEADS, HEAD_DIM),
                     c_k.reshape(b, s, SWA_KV_HEADS, HEAD_DIM),
                     c_v.reshape(b, s, SWA_KV_HEADS, HEAD_DIM), swa_sink) * jax.nn.silu(c_z)
    y_d = neighborhood_attn(d_q.reshape(b, s, NA_HEADS, HEAD_DIM),
                            d_k.reshape(b, s, NA_HEADS, HEAD_DIM),
                            d_v.reshape(b, s, NA_HEADS, HEAD_DIM), na_rpb) * jax.nn.silu(d_z)
    y = jnp.concatenate([y_a, y_b, y_c, y_d], axis=-1)
    return x + jnp.einsum("bse,ed->bsd", y, w_out)

def first_inputs(seed: int = 0) -> dict:
    key = jax.random.key(seed)
    ks = jax.random.split(key, 12)
    f32 = jnp.float32
    x = jax.random.normal(ks[0], (BATCH, SEQ, D_MODEL), f32)
    norm_g = 1.0 + 0.05 * jax.random.normal(ks[1], (DEPTH, D_MODEL), f32)
    w_in = jax.random.normal(ks[2], (DEPTH, D_MODEL, D_IN), f32) * D_MODEL ** -0.5
    w_out = jax.random.normal(ks[3], (DEPTH, D_MIX, D_MODEL), f32) * D_MIX ** -0.5
    conv_a_w = jax.random.normal(ks[4], (DEPTH, CONV_A_WIDTH, D_GROUP), f32) * CONV_A_WIDTH ** -0.5
    conv_a_b = 0.02 * jax.random.normal(ks[5], (DEPTH, D_GROUP), f32)
    ln_a_g = 1.0 + 0.05 * jax.random.normal(ks[6], (DEPTH, D_GROUP), f32)
    ln_a_b = 0.02 * jax.random.normal(ks[7], (DEPTH, D_GROUP), f32)
    conv_b_w = jax.random.normal(ks[8], (DEPTH, CONV_B_WIDTH, D_GROUP), f32) * CONV_B_WIDTH ** -0.5
    swa_sink = jax.random.normal(ks[9], (DEPTH, SWA_Q_HEADS), f32)
    na_rpb = 0.1 * jax.random.normal(ks[10], (DEPTH, NA_HEADS, 2 * NA_KH_MAX - 1, 2 * NA_KW - 1), f32)
    final_norm_g = 1.0 + 0.05 * jax.random.normal(ks[11], (D_MODEL,), f32)
    return {"x": x, "norm_g": norm_g, "w_in": w_in, "w_out": w_out,
            "conv_a_w": conv_a_w, "conv_a_b": conv_a_b, "ln_a_g": ln_a_g, "ln_a_b": ln_a_b,
            "conv_b_w": conv_b_w, "swa_sink": swa_sink, "na_rpb": na_rpb,
            "final_norm_g": final_norm_g}

def first_block(x, norm_g, w_in, w_out, conv_a_w, conv_a_b, ln_a_g, ln_a_b,
              conv_b_w, swa_sink, na_rpb, final_norm_g):
    for l in range(DEPTH):
        x = hybrid_layer(x, norm_g[l], w_in[l], w_out[l], conv_a_w[l], conv_a_b[l],
                         ln_a_g[l], ln_a_b[l], conv_b_w[l], swa_sink[l], na_rpb[l])
    return rmsnorm(x, final_norm_g)


RET_HEADS = 4
RET_QK_DIM = 64
RET_V_DIM = 128
RET_CHUNK = 128
DIFF_HEADS = 4
DIFF_HEAD_DIM = 64
DIFF_V_DIM = 2 * DIFF_HEAD_DIM
Q_BLOCK = 128
FFN_HIDDEN = ((int(math.ceil(8 * D_MODEL / 3)) + 255) // 256) * 256
NORM_EPS = 1e-6

RET_Q_W = RET_HEADS * RET_QK_DIM
RET_V_W = RET_HEADS * RET_V_DIM
DIFF_QK_W = DIFF_HEADS * 2 * DIFF_HEAD_DIM
DIFF_V_W = DIFF_HEADS * DIFF_V_DIM
IN_SPLITS = [RET_Q_W, RET_Q_W, RET_V_W, RET_V_W, DIFF_QK_W, DIFF_QK_W, DIFF_V_W]
IN_WIDTH = sum(IN_SPLITS)
MIX_WIDTH = RET_V_W + DIFF_V_W


def rmsnorm_2(x, g):
    xf = x.astype(jnp.float32)
    y = xf * lax.rsqrt(jnp.mean(xf * xf, axis=-1, keepdims=True) + NORM_EPS)
    return (y * g.astype(jnp.float32)).astype(x.dtype)

def retention_gammas():
    return 1.0 - jnp.exp2(-5.0 - jnp.arange(RET_HEADS, dtype=jnp.float32))

def retention_chunkwise(q, k, v):
    B, S, H, dk = q.shape
    dv = v.shape[-1]
    C = RET_CHUNK
    N = S // C
    dt = q.dtype
    log_g = jnp.log(retention_gammas())
    k = k * jnp.asarray(dk ** -0.5, dt)
    q = q.reshape(B, N, C, H, dk)
    k = k.reshape(B, N, C, H, dk)
    v = v.reshape(B, N, C, H, dv)
    idx = jnp.arange(C, dtype=jnp.float32)
    rel = idx[:, None] - idx[None, :]
    decay = jnp.where(rel[None] >= 0,
                      jnp.exp(jnp.maximum(rel, 0.0)[None] * log_g[:, None, None]),
                      0.0).astype(dt)
    s = jnp.einsum('bnchd,bnshd->bnhcs', q, k) * decay
    inner = jnp.einsum('bnhcs,bnshe->bnche', s, v)
    k_decay = jnp.exp((C - 1 - idx)[:, None] * log_g[None, :]).astype(dt)
    kv = jnp.einsum('bnshd,bnshe->nbhde', k * k_decay[:, :, None], v)
    g_chunk = jnp.exp(C * log_g).astype(dt)[None, :, None, None]

    def step(state, kv_n):
        return g_chunk * state + kv_n, state

    _, states = lax.scan(step, jnp.zeros((B, H, dk, dv), dt), kv)
    q_decay = jnp.exp((idx + 1.0)[:, None] * log_g[None, :]).astype(dt)
    cross = jnp.einsum('bnchd,nbhde->bnche', q * q_decay[:, :, None], states)
    return (inner + cross).reshape(B, S, H, dv)

def alibi_slopes(n):
    return jnp.exp2(-8.0 * jnp.arange(1, n + 1, dtype=jnp.float32) / n)

def diff_attention(q, k, v, lam):
    S = q.shape[1]
    d = q.shape[-1]
    scale = d ** -0.5
    slopes = alibi_slopes(q.shape[2])
    outs = []
    for i in range(S // Q_BLOCK):
        q0 = i * Q_BLOCK
        kend = q0 + Q_BLOCK
        qb = q[:, q0:kend]
        kb = k[:, :kend]
        vb = v[:, :kend]
        s = jnp.einsum('bqhjd,bkhjd->bhjqk', qb, kb).astype(jnp.float32) * scale
        dist = (q0 + jnp.arange(Q_BLOCK, dtype=jnp.float32))[:, None] - jnp.arange(kend, dtype=jnp.float32)[None, :]
        s = s - slopes[None, :, None, None, None] * dist
        s = jnp.where(dist >= 0, s, -jnp.inf)
        p = jax.nn.softmax(s, axis=-1)
        a = p[:, :, 0] - lam * p[:, :, 1]
        outs.append(jnp.einsum('bhqk,bkhe->bqhe', a.astype(vb.dtype), vb))
    return jnp.concatenate(outs, axis=1)

def second_inputs(seed: int = 0) -> dict:
    key = jax.random.key(seed)
    ks = jax.random.split(key, 16)
    f = jnp.float32

    def nrm(k, shape, scale):
        return jax.random.normal(k, shape, f) * scale

    def gain(k, shape):
        return 1.0 + 0.02 * jax.random.normal(k, shape, f)

    return {
        "x": jax.random.normal(ks[0], (BATCH, SEQ, D_MODEL), f),
        "attn_norm": gain(ks[1], (DEPTH, D_MODEL)),
        "w_in": nrm(ks[2], (DEPTH, D_MODEL, IN_WIDTH), D_MODEL ** -0.5),
        "ret_norm": gain(ks[3], (DEPTH, RET_V_DIM)),
        "lambda_q1": nrm(ks[4], (DEPTH, DIFF_HEAD_DIM), 0.1),
        "lambda_k1": nrm(ks[5], (DEPTH, DIFF_HEAD_DIM), 0.1),
        "lambda_q2": nrm(ks[6], (DEPTH, DIFF_HEAD_DIM), 0.1),
        "lambda_k2": nrm(ks[7], (DEPTH, DIFF_HEAD_DIM), 0.1),
        "diff_norm": gain(ks[8], (DEPTH, DIFF_V_DIM)),
        "w_out": nrm(ks[9], (DEPTH, MIX_WIDTH, D_MODEL), MIX_WIDTH ** -0.5),
        "ffn_norm": gain(ks[10], (DEPTH, D_MODEL)),
        "w_gate": nrm(ks[11], (DEPTH, D_MODEL, FFN_HIDDEN), D_MODEL ** -0.5),
        "w_up": nrm(ks[12], (DEPTH, D_MODEL, FFN_HIDDEN), D_MODEL ** -0.5),
        "w_down": nrm(ks[13], (DEPTH, FFN_HIDDEN, D_MODEL), FFN_HIDDEN ** -0.5),
        "final_norm": gain(ks[14], (D_MODEL,)),
    }

def second_block(x, attn_norm, w_in, ret_norm, lambda_q1, lambda_k1, lambda_q2, lambda_k2,
              diff_norm, w_out, ffn_norm, w_gate, w_up, w_down, final_norm):
    B, S, _ = x.shape
    offsets = np.cumsum(IN_SPLITS)[:-1].tolist()
    h = x
    for l in range(DEPTH):
        u = rmsnorm_2(h, attn_norm[l])
        proj = u @ w_in[l]
        rq, rk, rv, rg, dq, dk, dv = jnp.split(proj, offsets, axis=-1)

        ret = retention_chunkwise(rq.reshape(B, S, RET_HEADS, RET_QK_DIM),
                                  rk.reshape(B, S, RET_HEADS, RET_QK_DIM),
                                  rv.reshape(B, S, RET_HEADS, RET_V_DIM))
        ret = rmsnorm_2(ret, ret_norm[l]).reshape(B, S, RET_V_W)
        ret = jax.nn.silu(rg) * ret

        lam_init = 0.8 - 0.6 * math.exp(-0.3 * l)
        lam = (jnp.exp(jnp.sum(lambda_q1[l].astype(jnp.float32) * lambda_k1[l].astype(jnp.float32)))
               - jnp.exp(jnp.sum(lambda_q2[l].astype(jnp.float32) * lambda_k2[l].astype(jnp.float32)))
               + lam_init)
        dif = diff_attention(dq.reshape(B, S, DIFF_HEADS, 2, DIFF_HEAD_DIM),
                             dk.reshape(B, S, DIFF_HEADS, 2, DIFF_HEAD_DIM),
                             dv.reshape(B, S, DIFF_HEADS, DIFF_V_DIM), lam)
        dif = (rmsnorm_2(dif, diff_norm[l]) * (1.0 - lam_init)).reshape(B, S, DIFF_V_W)

        mix = jnp.concatenate([ret, dif], axis=-1)
        h = h + mix @ w_out[l]

        u = rmsnorm_2(h, ffn_norm[l])
        h = h + (jax.nn.silu(u @ w_gate[l]) * (u @ w_up[l])) @ w_down[l]
    return rmsnorm_2(h, final_norm)


def setup_inputs(seed=0):
    out = dict(first_inputs(seed))
    for name, value in second_inputs(seed + 1).items():
        if name != "x":
            out[name + "_2"] = value
    return out


def reference(
    x, norm_g, w_in, w_out, conv_a_w, conv_a_b, ln_a_g, ln_a_b, conv_b_w, swa_sink, na_rpb,
    final_norm_g, attn_norm_2, w_in_2, ret_norm_2, lambda_q1_2, lambda_k1_2, lambda_q2_2,
    lambda_k2_2, diff_norm_2, w_out_2, ffn_norm_2, w_gate_2, w_up_2, w_down_2, final_norm_2,
):
    x = first_block(
        x, norm_g, w_in, w_out, conv_a_w, conv_a_b, ln_a_g, ln_a_b, conv_b_w, swa_sink, na_rpb,
        final_norm_g,
    )
    return second_block(
        x, attn_norm_2, w_in_2, ret_norm_2, lambda_q1_2, lambda_k1_2, lambda_q2_2, lambda_k2_2,
        diff_norm_2, w_out_2, ffn_norm_2, w_gate_2, w_up_2, w_down_2, final_norm_2,
    )


_drawn_inputs = setup_inputs


def setup_inputs(seed=0):
    import zlib

    import numpy as np

    out = dict(_drawn_inputs(seed))
    spreads = {}
    factors = {'conv_a_b': 2.81,
     'ln_a_b': 5.202,
     'swa_sink': 8.0,
     'na_rpb': 5.578,
     'ret_norm_2': 5.15,
     'diff_norm_2': 3.987,
     'ffn_norm_2': 2.963,
     'final_norm_2': 2.85}
    for name, (base, spread) in spreads.items():
        noise = np.random.default_rng([zlib.crc32(name.encode()), seed]).standard_normal(out[name].shape)
        drawn = base * np.exp(spread * noise) if base else spread * noise
        out[name] = __import__('jax').numpy.asarray(drawn.astype(out[name].dtype))
    for name, factor in factors.items():
        out[name] = (out[name] * factor).astype(out[name].dtype)
    return out
```

```python
from contextlib import ExitStack

import numpy as np

import concourse.bass as bass
from concourse import mybir

F32 = mybir.dt.float32
F32R = mybir.dt.float32r
I32 = mybir.dt.int32
ALU = mybir.AluOpType
ACT = mybir.ActivationFunctionType

P = 128
S = 1024
HALF = 512
D = 1024
KC = D // P
NB = S // P
DEPTH = 2
EPS = 1e-6
NEG = -1e30
HD = 64
SCALE = HD ** -0.5
FFN = 2816
HC = FFN // P
FFN_GROUPS = [8, 8, 6]
TAPS_A, TAPS_B = 31, 3
GRID_W, KH, KW = 64, 8, 16
ROWS = S // GRID_W
ND = 2 * KH - 1
SKEW = 2 * GRID_W

BLOCKS = (28 + KC, 24 + KC + 2 * HC + KC * len(FFN_GROUPS))
N_W = DEPTH * sum(BLOCKS)
SLOTS = 23

C_NORM, C_CAW, C_CAB, C_LNG, C_LNB, C_CBW, C_SINK = 0, 8, 70, 72, 74, 76, 82
W1 = 86
C_AN, C_FN, C_RN, C_DN, C_NLAM = 0, 8, 16, 17, 18
W2 = 19
O2 = DEPTH * W1
O_FIN1 = O2 + DEPTH * W2
O_FIN2 = O_FIN1 + 8
NPAR = O_FIN2 + 8

GQA_ORDER = (0, 2, 1, 3)


def tiles_of_round(kind, n):
    if kind == "gqa":
        return range(max(0, n - 1), min(NB, n + 2))
    if kind == "na":
        if 2 <= n <= NB - 3:
            return range(n - 2, n + 3)
        return range(0, 4) if n < 2 else range(NB - 4, NB)
    return range(0, n + 1)


def groups_of(tiles):
    tiles = list(tiles)
    n = -(-len(tiles) // 4)
    size = -(-len(tiles) // n)
    return [tiles[i:i + size] for i in range(0, len(tiles), size)]


def attention_counts(kind):
    groups = sum(4 * len(groups_of(tiles_of_round(kind, n))) for n in range(NB))
    maps = 2 if kind == "dif" else 1
    return {"maps": 4 * NB * maps, "units": 4 * NB, "groups": groups, "rounds": NB}


class Signal:

    def __init__(self, handle, per, before=0, between=0):
        self.handle, self.per, self.before, self.between = handle, per, before, between

    def at(self, stack, l, n):
        base = self.before + (DEPTH * self.per[0] + self.between if stack else 0)
        return l * self.per[stack] + (base + n)

    def end(self, n=0):
        return self.before + self.between + DEPTH * sum(self.per) + n

    def mid(self, n):
        return self.before + DEPTH * self.per[0] + n


class Chain:

    def __init__(self, engine, handle):
        self.engine, self.handle, self.n = engine, handle, 0

    def restart(self):
        self.engine.sem_clear(self.handle)
        self.n = 0

    def link(self, instruction):
        self.n += 1
        instruction.then_inc(self.handle, 1)
        self.engine.wait_ge(self.handle, self.n)


def build(nc, x_in, w_in, par_in, lam_in, rpb_in, c_square, c_rope, c_gqa, c_na, c_ret, c_alibi, out):
    ctx = ExitStack()
    with ctx:
        top = [-(-nc.sbuf_base // 64) * 64]

        def sb(name, shape, dt=F32, at=None):
            offset = top[0] if at is None else at
            if at is None:
                top[0] += -(-4 * int(np.prod(shape[1:])) // 32) * 32
            return nc.alloc_sbuf_tensor_at(name, shape, dt, offset=offset)

        xt = sb("xt", [P, KC, S])
        base_in = top[0]
        in_hi = sb("in_hi", [P, KC, S], F32R)
        in_lo = sb("in_lo", [P, KC, S], F32R)
        w_raw = sb("w_raw", [P, 2, KC * P])
        w_hi = sb("w_hi", [P, 2, KC * P], F32R)
        w_lo = sb("w_lo", [P, 2, KC * P], F32R)
        base_st = top[0]
        st = sb("st", [P, SLOTS, S])
        rfac = sb("rfac", [P, S])
        half = sb("half", [P, HALF])
        square = sb("square", [P, 2, P])
        ident, swap = square[:, 0, :], square[:, 1, :]
        ones = sb("ones", [P, P])
        mask_gqa = sb("mask_gqa", [P, 3 * P])
        par = sb("par", [P, NPAR])
        cur = sb("cur", [P, W1])
        small = sb("small", [P, 96])
        hs = sb("attention_space", [P, 16, S], at=base_in)
        hid_hi = sb("hid_hi", [P, 8, S], F32R, at=base_st)
        hid_lo = sb("hid_lo", [P, 8, S], F32R, at=base_st + 8 * 4 * S)

        stat, root, tmp = small[:, 0:8], small[:, 8:16], small[:, 16:24]
        negm = small[:, 24:40].rearrange("p (a b) -> p a b", a=2)
        lsum = small[:, 40:56].rearrange("p (a b) -> p a b", a=2)
        rinv = small[:, 56:72].rearrange("p (a b) -> p a b", a=2)
        esink, ssq, comb, factor = (small[:, 72 + 4 * i:76 + 4 * i] for i in range(4))

        ps = ctx.enter_context(nc.psum_tensor("ps", [P, 8, HALF], F32))

        sems = {}

        def signal(name, one=0, two=0, before=0, between=0):
            s = Signal(ctx.enter_context(nc.semaphore(name)), (one, two), before, between)
            sems[name] = s
            return s

        raw_in = [signal(f"raw_in{j}") for j in range(2)]
        w_split = signal("w_split", *BLOCKS)
        done = signal("done", *BLOCKS)
        taken = signal("taken", *BLOCKS, before=2)
        hi_ready = signal("hi_ready", 16, 24)
        lo_ready = signal("lo_ready", 16, 24)
        hid_hi_ready = signal("hid_hi_ready", 0, HC)
        hid_lo_ready = signal("hid_lo_ready", 0, HC)
        cur_ready = signal("cur_ready", 1, 1)
        squared = signal("squared", 8, 16, before=8, between=8)
        acc_ready = signal("acc_ready", 1, 2, before=1, between=1)
        stat_ready = signal("stat_ready", 2, 2, between=1)
        diag_ready = signal("diag_ready", 2, 2, between=1)
        spread_ready = signal("spread_ready", 2, 2, between=1)
        fac_ready = signal("fac_ready", 2, 2, between=1)
        tanh_ready = signal("tanh_ready", 10, 4 + HC)
        gated = signal("gated", 0, HC)
        conv_ready = signal("conv_ready", 1)
        mean_ready = signal("mean_ready", 1)
        centred = signal("centred", 2)
        lnsq_ready = signal("lnsq_ready", 2)
        normed = signal("normed", 2)
        lnact_ready = signal("lnact_ready", 2)
        rope_in = signal("rope_in", 2 * 16)
        swapped = signal("swapped", 6)
        roped = signal("roped", 6)
        vt_ready = signal("vt_ready", 6, 16)
        vt_taken = signal("vt_taken", 6, 16)
        bias_in = signal("bias_in", 4 * 16)
        bias_ready = signal("bias_ready", 1)
        ag, an, ad = (attention_counts(k) for k in ("gqa", "na", "dif"))
        both = {k: ag[k] + an[k] for k in ag}
        scored = signal("scored", both["maps"], ad["maps"])
        biased = signal("biased", both["maps"], ad["maps"])
        expd = signal("expd", both["maps"], ad["maps"])
        mixed = signal("mixed", 0, ad["units"])
        turned = signal("turned", both["groups"], ad["groups"])
        turned_out = signal("turned_out", both["groups"], ad["groups"])
        weighted = signal("weighted", both["rounds"], ad["rounds"])
        sink_ready = signal("sink_ready", ag["rounds"])
        sink_exp = signal("sink_exp", ag["rounds"])
        head_sq = signal("head_sq", 0, ad["rounds"])
        headed = signal("headed", both["rounds"], ad["rounds"])
        back = signal("back", both["rounds"], ad["rounds"])
        mixed_out = signal("mixed_out", both["rounds"], ad["rounds"])
        alibi_in = signal("alibi_in", 0, 16)
        retc_in = signal("retc_in", 0, 16)
        r_scored = signal("r_scored", 0, NB)
        r_decayed = signal("r_decayed", 0, NB)
        r_summed = signal("r_summed", 0, NB)
        r_squared = signal("r_squared", 0, NB)
        r_state = signal("r_state", 0, NB - 1)
        r_headed = signal("r_headed", 0, NB)
        r_back = signal("r_back", 0, NB)
        r_out = signal("r_out", 0, NB)
        x_in_sem = [signal(f"x_in{c}") for c in range(KC)]
        const_in = signal("const_in")
        lam_sem = signal("lam_sem")
        lam_exp = signal("lam_exp")
        par_ready = signal("par_ready")
        x_scaled = signal("x_scaled")
        out_ready = signal("out_ready")
        out_sem = signal("out_sem")
        dve_own = ctx.enter_context(nc.semaphore("dve_own"))
        dve_step = ctx.enter_context(nc.semaphore("dve_step"))
        act_own = ctx.enter_context(nc.semaphore("act_own"))
        pool_own = ctx.enter_context(nc.semaphore("pool_own"))

        ACC, DIAG, SQ = 22, 21, (18, 19)

        def rv(n, t):
            return st[:, 14 + n // 2, (n % 2) * HALF + t * P:(n % 2) * HALF + (t + 1) * P]

        def state_of(n):
            return st[:, (22, 9)[n % 2], HALF:S]

        block = ctx.enter_context(nc.Block())

        @block.sync
        def _(sp):
            def load(pair, first):
                for j in range(2):
                    if not first:
                        sp.wait_ge(w_split.handle, pair * 2 + (j - 1))
                    sp.dma_start(w_raw[:, j, :], w_in[bass.ds(pair * 2 + j, 1), :, :].rearrange("a p n -> (a p) n")
                                 ).then_inc(raw_in[j].handle, 16)
            load(0, True)
            with sp.Fori(1, N_W // 2) as pair:
                load(pair, False)

        @block.gpsimd
        def _(pool):
            def split(pair, first):
                for j in range(2):
                    pool.wait_ge(raw_in[j].handle, pair * 16 + 16)
                    if not first:
                        pool.wait_ge(done.handle, pair * 2 + (j - 1))
                    pool.tensor_tensor(w_hi[:, j, :], w_raw[:, j, :], ones[:, 0:1].broadcast_to([P, KC * P]),
                                       ALU.mult).then_inc(pool_own, 1)
                    pool.wait_ge(pool_own, pair * 2 + (j + 2))
                    pool.tensor_tensor(w_lo[:, j, :], w_raw[:, j, :], w_hi[:, j, :].bitcast(F32),
                                       ALU.subtract).then_inc(w_split.handle, 1)
            pool.memset(ones[:, :], 1.0).then_inc(pool_own, 1)
            pool.wait_ge(pool_own, 1)
            split(0, True)
            with pool.Fori(1, N_W // 2) as pair:
                split(pair, False)

        @block.tensor
        def _(pe):
            def product(stack, l, n, hi, lo, chunks=KC, before_chunk=None, midway=None):
                n, j = n if isinstance(n, tuple) else (n, n % 2)
                pe.wait_ge(w_split.handle, w_split.at(stack, l, n + 1))
                pe.wait_ge(taken.handle, taken.at(stack, l, n - 1))
                for k in range(chunks):
                    if midway and k == chunks // 2:
                        midway()
                    if before_chunk:
                        before_chunk(k)
                    for w, parts in ((w_hi, (hi, lo)), (w_lo, (hi,))):
                        for part in parts:
                            for h in range(2):
                                last = pe.matmul(ps[:, 2 * j + h, :], w[:, j, k * P:(k + 1) * P],
                                                 part[:, k, h * HALF:(h + 1) * HALF],
                                                 start=(k == 0 and w is w_hi and part is hi),
                                                 stop=(k == chunks - 1 and w is w_lo))
                last.then_inc(done.handle, 1)

            def products(stack, l, n0, n1, hi=in_hi, lo=in_lo, chunks=KC):
                if n1 - n0 == 2:
                    product(stack, l, n0, hi, lo, chunks)
                    product(stack, l, n0 + 1, hi, lo, chunks)
                elif n1 > n0:
                    with pe.Fori(n0, n1, 2) as n:
                        product(stack, l, (n, 0), hi, lo, chunks)
                        product(stack, l, (n + 1, 1), hi, lo, chunks)

            def chunk_wait(stack, l, base, ready=lo_ready):
                return lambda k: pe.wait_ge(ready.handle, ready.at(stack, l, base + k + 1))

            def row_sums(tiles):
                for b in range(NB):
                    for i, tile in enumerate(tiles):
                        last = pe.matmul(ps[:, 4, b:b + 1], tile[:, b * P:(b + 1) * P], ones[:, 0:1],
                                         start=(i == 0), stop=(i == len(tiles) - 1))
                last.then_inc(stat_ready.handle, 1)

            def spread():
                for h in range(2):
                    last = pe.matmul(ps[:, 5 + h, :], ones[:, :], st[:, DIAG, h * HALF:(h + 1) * HALF],
                                     start=True, stop=True)
                last.then_inc(spread_ready.handle, 1)

            def turn_values(stack, l, k0, tile, banks=(4, 5)):
                for g in range(2):
                    if k0 + g >= 2:
                        pe.wait_ge(vt_taken.handle, vt_taken.at(stack, l, k0 + g - 1))
                    for b in range(4):
                        last = pe.transpose(ps[:, banks[g], b * P:(b + 1) * P],
                                            tile[:, (4 * g + b) * P:(4 * g + b + 1) * P], ident)
                    last.then_inc(vt_ready.handle, 1)

            def attend(stack, l, kind, m0, g0, r0, query, key, value, width):
                maps = 2 if kind == "dif" else 1
                units = [(n, t) for n in range(NB) for t in range(4)]
                state = {"m": 0, "g": 0}
                where = {}

                def scores(u):
                    n, t = units[u]
                    tiles = tiles_of_round(kind, n)
                    cols = len(tiles) * P
                    for j in range(maps):
                        m = state["m"]
                        if m >= 2:
                            pe.wait_ge(biased.handle, biased.at(stack, l, m0 + m - 1))
                        q, base = query(t, j)
                        k = key(t, j)
                        for c in range(0, cols, HALF):
                            w = min(HALF, cols - c)
                            last = pe.matmul(ps[:, 2 * (m % 2) + c // HALF, 0:w],
                                             q[base:base + HD, n * P:(n + 1) * P],
                                             k[base:base + HD, tiles[0] * P + c:tiles[0] * P + c + w],
                                             start=True, stop=True)
                        last.then_inc(scored.handle, 1)
                        state["m"] += 1

                def turn(u):
                    n, t = units[u]
                    tiles = tiles_of_round(kind, n)
                    where[u] = []
                    for group in groups_of(tiles):
                        g = state["g"]
                        if group[0] == tiles[0]:
                            if kind == "dif":
                                pe.wait_ge(mixed.handle, mixed.at(stack, l, u + 1))
                            else:
                                pe.wait_ge(expd.handle, expd.at(stack, l, m0 + u + 1))
                        if g >= 2:
                            pe.wait_ge(turned_out.handle, turned_out.at(stack, l, g0 + g - 1))
                        e = hs[:, 7 + (maps * u) % 4, :]
                        for i, kt in enumerate(group):
                            c = (kt - tiles[0]) * P
                            last = pe.transpose(ps[:, 4 + g % 2, i * P:(i + 1) * P], e[:, c:c + P], ident)
                        last.then_inc(turned.handle, 1)
                        where[u].append((g, group))
                        state["g"] += 1

                def weigh(u):
                    n, t = units[u]
                    tiles = tiles_of_round(kind, n)
                    if t == 0 and n >= 1:
                        pe.wait_ge(headed.handle, headed.at(stack, l, r0 + n))
                    for g, group in where[u]:
                        pe.wait_ge(turned_out.handle, turned_out.at(stack, l, g0 + g + 1))
                        for i, kt in enumerate(group):
                            last = pe.matmul(ps[:, 6, t * width:(t + 1) * width],
                                             hs[:, 11 + (g % 4) // 2, (g % 2) * HALF + i * P:(g % 2) * HALF + (i + 1) * P],
                                             value(t, kt), start=(kt == tiles[0]), stop=(kt == tiles[-1]))
                    if t == 3:
                        last.then_inc(weighted.handle, 1)

                def turn_back(n):
                    pe.wait_ge(headed.handle, headed.at(stack, l, r0 + n + 1))
                    if n >= 1:
                        pe.wait_ge(mixed_out.handle, mixed_out.at(stack, l, r0 + n))
                    for c in range(4 * width // P):
                        last = pe.transpose(ps[:, 7, c * P:(c + 1) * P],
                                            hs[:, 14, (n % 2) * HALF + c * P:(n % 2) * HALF + (c + 1) * P], ident)
                    last.then_inc(back.handle, 1)

                n_units = len(units)
                for u in range(n_units + 4):
                    if u < n_units:
                        scores(u)
                    if 2 <= u < n_units + 2:
                        weigh(u - 2)
                    if 1 <= u < n_units + 1:
                        turn(u - 1)
                    if u >= 7 and (u - 7) % 4 == 0 and (u - 7) // 4 < NB:
                        turn_back((u - 7) // 4)
                return state["m"], state["g"]

            pe.wait_ge(const_in.handle, 16 * 3)

            with pe.Fori(0, DEPTH) as l:
                product(0, l, 0, in_hi, in_lo, before_chunk=chunk_wait(0, l, 0))
                pe.wait_ge(acc_ready.handle, acc_ready.at(0, l, 0))
                row_sums([st[:, ACC, :]])
                product(0, l, 1, in_hi, in_lo)
                pe.wait_ge(diag_ready.handle, diag_ready.at(0, l, 1))
                spread()
                products(0, l, 2, 14)
                product(0, l, 14, in_hi, in_lo)
                pe.wait_ge(conv_ready.handle, conv_ready.at(0, l, 1))
                for h in range(2):
                    for c in range(2):
                        last = pe.matmul(ps[:, 4 + h, :], ones[:, :], st[:, 12 + c, h * HALF:(h + 1) * HALF],
                                         start=(c == 0), stop=(c == 1))
                last.then_inc(mean_ready.handle, 1)
                product(0, l, 15, in_hi, in_lo)
                pe.wait_ge(lnsq_ready.handle, lnsq_ready.at(0, l, 2))
                row_sums([st[:, 14, :], st[:, 15, :]])
                product(0, l, 16, in_hi, in_lo)
                pe.wait_ge(diag_ready.handle, diag_ready.at(0, l, 2))
                spread()
                product(0, l, 17, in_hi, in_lo)
                product(0, l, 18, in_hi, in_lo)

                def swap_halves(i, slot):
                    for h in range(2):
                        if i >= 1:
                            pe.wait_ge(roped.handle, roped.at(0, l, 2 * i - 1 + h))
                        pe.matmul(ps[:, 6 + h, :], swap, st[:, slot, h * HALF:(h + 1) * HALF],
                                  start=True, stop=True).then_inc(swapped.handle, 1)

                product(0, l, 19, in_hi, in_lo)
                pe.wait_ge(taken.handle, taken.at(0, l, 19))
                pe.wait_ge(fac_ready.handle, fac_ready.at(0, l, 2))
                swap_halves(0, 10)
                product(0, l, 20, in_hi, in_lo)
                pe.wait_ge(taken.handle, taken.at(0, l, 20))
                swap_halves(1, 11)
                product(0, l, 21, in_hi, in_lo)
                pe.wait_ge(taken.handle, taken.at(0, l, 21))
                swap_halves(2, 17)
                product(0, l, 22, in_hi, in_lo)
                pe.wait_ge(taken.handle, taken.at(0, l, 22))
                turn_values(0, l, 0, st[:, 8, :])
                product(0, l, 23, in_hi, in_lo)
                products(0, l, 24, 28)
                pe.wait_ge(taken.handle, taken.at(0, l, 28))
                turn_values(0, l, 2, st[:, 9, :])
                turn_values(0, l, 4, st[:, 22, :])
                pe.wait_ge(vt_taken.handle, vt_taken.at(0, l, 6))
                pe.wait_ge(roped.handle, roped.at(0, l, 6))
                m, g = attend(0, l, "gqa", 0, 0, 0,
                              lambda t, j: (st[:, 10 + t // 2, :], HD * (t % 2)),
                              lambda t, j: st[:, 17, :],
                              lambda t, kt: st[:, 18, kt * P + HD * (t % 2):kt * P + HD * (t % 2 + 1)], HD)
                pe.wait_ge(biased.handle, biased.at(0, l, m))
                pe.wait_ge(turned_out.handle, turned_out.at(0, l, g))
                pe.wait_ge(headed.handle, headed.at(0, l, NB))
                pe.wait_ge(mixed_out.handle, mixed_out.at(0, l, NB))
                slots = (19, 12, 13, 14)
                attend(0, l, "na", m, g, NB,
                       lambda t, j: (st[:, slots[t // 2], :], HD * (t % 2)),
                       lambda t, j: st[:, slots[2 + t // 2], :],
                       lambda t, kt: st[:, 15 + kt // 4, (kt % 4) * 256 + t * HD:(kt % 4) * 256 + (t + 1) * HD], HD)
                product(0, l, 28, in_hi, in_lo, before_chunk=chunk_wait(0, l, 8))
                product(0, l, 29, in_hi, in_lo)
                products(0, l, 30, 36)

            pe.wait_ge(acc_ready.handle, acc_ready.mid(0))
            row_sums([st[:, ACC, :]])
            pe.wait_ge(diag_ready.handle, diag_ready.mid(1))
            spread()

            with pe.Fori(0, DEPTH) as l:
                product(1, l, 0, in_hi, in_lo, before_chunk=chunk_wait(1, l, 0))
                pe.wait_ge(acc_ready.handle, acc_ready.at(1, l, 0))
                row_sums([st[:, ACC, :]])
                product(1, l, 1, in_hi, in_lo)
                pe.wait_ge(diag_ready.handle, diag_ready.at(1, l, 1))
                spread()
                products(1, l, 2, 8)
                product(1, l, 8, in_hi, in_lo)
                product(1, l, 9, in_hi, in_lo)
                pe.wait_ge(taken.handle, taken.at(1, l, 9))
                turn_values(1, l, 0, st[:, 8, :])
                product(1, l, 10, in_hi, in_lo)
                pe.wait_ge(taken.handle, taken.at(1, l, 10))
                turn_values(1, l, 2, st[:, 9, :])
                product(1, l, 11, in_hi, in_lo)
                pe.wait_ge(taken.handle, taken.at(1, l, 11))
                turn_values(1, l, 4, st[:, 8, :])
                product(1, l, 12, in_hi, in_lo)
                pe.wait_ge(taken.handle, taken.at(1, l, 12))
                turn_values(1, l, 6, st[:, 9, :])

                def r_scores(n):
                    if n >= 1:
                        pe.wait_ge(r_decayed.handle, r_decayed.at(1, l, n))
                        pe.wait_ge(r_state.handle, r_state.at(1, l, n))
                    else:
                        pe.wait_ge(vt_taken.handle, vt_taken.at(1, l, 8))
                    for c in range(2):
                        pe.transpose(ps[:, 4, 256 + c * P:256 + (c + 1) * P], st[:, 12 + c, n * P:(n + 1) * P], ident)
                    for t in range(4):
                        b = HD * (t % 2)
                        last = pe.matmul(ps[:, 4 + t % 2, (t // 2) * P:(t // 2 + 1) * P], st[b:b + HD, 12 + t // 2, n * P:(n + 1) * P],
                                         st[b:b + HD, 10 + t // 2, n * P:(n + 1) * P], start=True, stop=True)
                    last.then_inc(r_scored.handle, 1)

                def r_sums(n):
                    pe.wait_ge(r_decayed.handle, r_decayed.at(1, l, n + 1))
                    if n >= 1:
                        pe.wait_ge(r_state.handle, r_state.at(1, l, n))
                        pe.wait_ge(r_headed.handle, r_headed.at(1, l, n))
                    for c in range(2):
                        pe.matmul(ps[:, 6, 2 * c * P:2 * (c + 1) * P], st[:, 22, 256 + c * P:256 + (c + 1) * P],
                                  state_of(n)[:, 2 * c * P:2 * (c + 1) * P],
                                  start=(c == 0), stop=False, skip_group_check=True)
                    for t in range(4):
                        last = pe.matmul(ps[:, 6, t * P:(t + 1) * P], st[:, 9, GQA_ORDER[t] * P:(GQA_ORDER[t] + 1) * P],
                                         rv(n, t), start=False, stop=(t == 3), skip_group_check=True)
                    if n < NB - 1:
                        for t in range(4):
                            b = HD * (t % 2)
                            last = pe.matmul(ps[b:b + HD, 5, 256 + (t // 2) * P:256 + (t // 2 + 1) * P],
                                             st[:, 22, t * HD:(t + 1) * HD], rv(n, t), start=True, stop=True)
                    last.then_inc(r_summed.handle, 1)

                def r_turn_back(n):
                    pe.wait_ge(r_headed.handle, r_headed.at(1, l, n + 1))
                    if n >= 1:
                        pe.wait_ge(r_out.handle, r_out.at(1, l, n))
                    for t in range(4):
                        last = pe.transpose(ps[:, 7, t * P:(t + 1) * P], half[:, t * P:(t + 1) * P], ident)
                    last.then_inc(r_back.handle, 1)

                for n in range(NB + 2):
                    if n >= 1:
                        product(1, l, 12 + n, in_hi, in_lo, midway=(lambda: r_sums(n - 1)) if n <= NB else None)
                    if n < NB:
                        r_scores(n)
                    if n >= 2:
                        r_turn_back(n - 2)
                pe.wait_ge(taken.handle, taken.at(1, l, 21))
                turn_values(1, l, 8, st[:, 8, :])
                product(1, l, 22, in_hi, in_lo)
                pe.wait_ge(taken.handle, taken.at(1, l, 22))
                turn_values(1, l, 10, st[:, 9, :])
                product(1, l, 23, in_hi, in_lo)
                pe.wait_ge(taken.handle, taken.at(1, l, 24))
                turn_values(1, l, 12, st[:, 14, :])
                turn_values(1, l, 14, st[:, 15, :])
                pe.wait_ge(vt_taken.handle, vt_taken.at(1, l, 16))
                pe.wait_ge(r_out.handle, r_out.at(1, l, NB))
                attend(1, l, "dif", 0, 0, 0,
                       lambda t, j: (st[:, 4 + t, :], HD * j),
                       lambda t, j: st[:, 18 + t, :],
                       lambda t, kt: st[:, 10 + kt // 2, (kt % 2) * HALF + t * P:(kt % 2) * HALF + (t + 1) * P], P)
                product(1, l, 24, in_hi, in_lo, before_chunk=chunk_wait(1, l, 8))
                product(1, l, 25, in_hi, in_lo)
                products(1, l, 26, 32)
                n = 32
                chunk0 = 0
                for group in FFN_GROUPS:
                    if chunk0 == 0:
                        product(1, l, n, in_hi, in_lo, before_chunk=chunk_wait(1, l, 16))
                        pe.wait_ge(acc_ready.handle, acc_ready.at(1, l, 1))
                        row_sums([st[:, ACC, :]])
                        product(1, l, n + 1, in_hi, in_lo)
                        pe.wait_ge(diag_ready.handle, diag_ready.at(1, l, 2))
                        spread()
                        products(1, l, n + 2, n + 2 * group)
                    else:
                        products(1, l, n, n + 2 * group)
                    n += 2 * group
                    product(1, l, n, hid_hi, hid_lo, chunks=group,
                            before_chunk=chunk_wait(1, l, chunk0, hid_lo_ready))
                    product(1, l, n + 1, hid_hi, hid_lo, chunks=group)
                    products(1, l, n + 2, n + KC, hid_hi, hid_lo, chunks=group)
                    n += KC
                    chunk0 += group

            pe.wait_ge(acc_ready.handle, acc_ready.end())
            row_sums([st[:, ACC, :]])
            pe.wait_ge(diag_ready.handle, diag_ready.end(1))
            spread()

        @block.scalar
        def _(act):
            def split_hi(stack, l, base, source, scale=None):
                for c in range(KC):
                    s = scale(c) if scale else 1.0
                    act.activation(in_hi[:, c, :], source(c), ACT.Copy if scale is None else ACT.Identity,
                                   scale=s).then_inc(hi_ready.handle, 1)

            def squares(c):
                act.activation(st[:, ACC if c == 0 else SQ[c % 2], :], xt[:, c, :], ACT.Square
                               ).then_inc(squared.handle, 1)

            def take_factor(wait, slot=None):
                act.wait_ge(spread_ready.handle, wait)
                to = rfac[:, :] if slot is None else st[:, slot, :]
                act.activation(to, ps[:, 5:7, :], ACT.Copy).then_inc(fac_ready.handle, 1)

            def take_values(stack, l, k0, to):
                for g in range(2):
                    act.wait_ge(vt_ready.handle, vt_ready.at(stack, l, k0 + g + 1))
                    act.activation(to(g), ps[:, 4 + g, :].rearrange("p (b c) -> p b c", b=4), ACT.Copy
                                   ).then_inc(vt_taken.handle, 1)

            def attend(stack, l, kind, m0, g0, r0):
                maps = 2 if kind == "dif" else 1
                units = [(n, t) for n in range(NB) for t in range(4)]
                state = {"g": 0}

                def exps(u):
                    n, t = units[u]
                    cols = len(tiles_of_round(kind, n)) * P
                    for j in range(maps):
                        m = maps * u + j
                        act.wait_ge(biased.handle, biased.at(stack, l, m0 + m + 1))
                        e = hs[:, 7 + m % 4, 0:cols]
                        i = maps * t + j
                        act.activation(e, e, ACT.Exp, bias=negm[:, n % 2, i:i + 1], scale=-1.0,
                                       accum_out=lsum[:, n % 2, i:i + 1]).then_inc(expd.handle, 1)
                    if kind == "gqa" and t == 3:
                        act.wait_ge(sink_ready.handle, sink_ready.at(stack, l, n + 1))
                        act.activation(esink, comb, ACT.Exp).then_inc(sink_exp.handle, 1)

                def groups(u):
                    n, t = units[u]
                    for group in groups_of(tiles_of_round(kind, n)):
                        g = state["g"]
                        act.wait_ge(turned.handle, turned.at(stack, l, g0 + g + 1))
                        w = len(group) * P
                        act.activation(hs[:, 11 + (g % 4) // 2, (g % 2) * HALF:(g % 2) * HALF + w],
                                       ps[:, 4 + g % 2, 0:w], ACT.Copy).then_inc(turned_out.handle, 1)
                        state["g"] += 1

                def head_squares(n):
                    act.wait_ge(weighted.handle, weighted.at(stack, l, r0 + n + 1))
                    for t in range(4):
                        last = act.activation(hs[:, 13, t * P:(t + 1) * P], ps[:, 6, t * P:(t + 1) * P], ACT.Square,
                                              scale=rinv[:, n % 2, 2 * t:2 * t + 1], accum_out=ssq[:, t:t + 1])
                    last.then_inc(head_sq.handle, 1)

                for u in range(len(units) + 4):
                    if u < len(units):
                        exps(u)
                    if 1 <= u < len(units) + 1:
                        groups(u - 1)
                    if kind == "dif" and u >= 5 and (u - 5) % 4 == 0 and (u - 5) // 4 < NB:
                        head_squares((u - 5) // 4)

            for c in range(KC):
                act.dma_start(xt[:, c, :], x_in[c, :, :]).then_inc(x_in_sem[c].handle, 16)
                if c == 0:
                    act.dma_start(par[:, 0:NPAR], par_in).then_inc(const_in.handle, 16)
                    act.dma_start(square[:, 0:2, :], c_square.rearrange("a p n -> p a n")).then_inc(const_in.handle, 16)
                    act.dma_start(mask_gqa[:, :], c_gqa).then_inc(const_in.handle, 16)
                    act.dma_start(st[:, 0, 0:DEPTH * 4 * HD], lam_in).then_inc(lam_sem.handle, 16)
            for c in range(KC):
                act.wait_ge(x_in_sem[c].handle, 16)
                if c >= 3:
                    act.wait_ge(dve_own, c - 2)
                squares(c)
            act.wait_ge(lam_exp.handle, 1)
            act.activation(small[:, 4:8], small[:, 0:4], ACT.Exp).then_inc(lam_exp.handle, 1)

            with act.Fori(0, DEPTH) as l:
                act.wait_ge(cur_ready.handle, cur_ready.at(0, l, 1))
                split_hi(0, l, 0, lambda c: xt[:, c, :], lambda c: cur[:, C_NORM + c:C_NORM + c + 1])
                take_factor(spread_ready.at(0, l, 1))
                for i in range(2):
                    act.wait_ge(taken.handle, taken.at(0, l, 2 * i + 1))
                    act.activation(st[:, 8 + 2 * i, :], st[:, 8 + 2 * i, :], ACT.Tanh, scale=0.5
                                   ).then_inc(tanh_ready.handle, 1)
                for k in range(8):
                    act.wait_ge(taken.handle, taken.at(0, l, 4 + k + 1))
                    act.activation(st[:, 10 + k % 2, :], st[:, 8 + k % 2, :], ACT.Tanh, scale=0.5
                                   ).then_inc(tanh_ready.handle, 1)
                for c in range(2):
                    act.wait_ge(centred.handle, centred.at(0, l, c + 1))
                    act.activation(st[:, 14 + c, :], st[:, 12 + c, :], ACT.Square).then_inc(lnsq_ready.handle, 1)
                take_factor(spread_ready.at(0, l, 2), slot=16)
                act.dma_start(st[:, 20:22, :], c_rope.rearrange("a p n -> p a n")).then_inc(rope_in.handle, 32)
                for c in range(2):
                    act.wait_ge(normed.handle, normed.at(0, l, c + 1))
                    act.activation(st[:, 12 + c, :], st[:, 12 + c, :], ACT.Identity,
                                   scale=cur[:, C_LNG + c:C_LNG + c + 1],
                                   bias=cur[:, C_LNB + c:C_LNB + c + 1]).then_inc(act_own, 1)
                    act.wait_ge(act_own, l * 2 + (c + 1))
                    act.activation(st[:, 14 + c, :], st[:, 12 + c, :], ACT.Tanh, scale=0.5
                                   ).then_inc(lnact_ready.handle, 1)
                v3 = lambda slot, g: st[:, slot, g * HALF:(g + 1) * HALF].rearrange("p (b c) -> p b c", b=4)
                take_values(0, l, 0, lambda g: v3(18, g))
                act.wait_ge(done.handle, done.at(0, l, 28))
                raw = rpb_in[bass.ds(l, 1), :, :].rearrange("a g c -> (a g) c")[:, GRID_W - 1:GRID_W - 1 + GRID_W * (SKEW - 1)
                                                                                ].rearrange("g (q s) -> q g s", s=SKEW - 1)
                table = hs[:, 0:4, :].rearrange("p a n -> p (a n)")[:, 0:4 * ND * GRID_W].rearrange(
                    "p (g c) -> p g c", c=GRID_W)
                for to, of in ((table[0:64], raw), (table[64:128, 1:4 * ND], raw[:, 0:4 * ND - 1]),
                               (table[64:128, 0:1], raw[:, 0:1])):
                    act.dma_start(to, of[:, :, 0:GRID_W]).then_inc(bias_in.handle, 16)
                act.dma_start(hs[:, 15, 0:11 * GRID_W], c_na).then_inc(bias_in.handle, 16)
                dv3 = lambda c, g: st[:, 15 + g, :].rearrange("p (b x) -> p b x", b=4)[:, :, c * P:(c + 1) * P]
                take_values(0, l, 2, lambda g: dv3(0, g))
                take_values(0, l, 4, lambda g: dv3(1, g))
                attend(0, l, "gqa", 0, 0, 0)
                attend(0, l, "na", ag["maps"], ag["groups"], NB)
                act.wait_ge(mixed_out.handle, mixed_out.at(0, l, 2 * NB))
                split_hi(0, l, 8, lambda c: st[:, c, :])
                for c in range(KC):
                    act.wait_ge(taken.handle, taken.at(0, l, 28 + c + 1))
                    squares(c)

            take_factor(spread_ready.mid(1))
            for c in range(KC):
                act.wait_ge(x_scaled.handle, c + 1)
                squares(c)

            with act.Fori(0, DEPTH) as l:
                act.wait_ge(cur_ready.handle, cur_ready.at(1, l, 1))
                split_hi(1, l, 0, lambda c: xt[:, c, :], lambda c: cur[:, C_AN + c:C_AN + c + 1])
                take_factor(spread_ready.at(1, l, 1))
                for k in range(4):
                    act.wait_ge(taken.handle, taken.at(1, l, k + 1))
                    act.activation(st[:, 10 + k % 2, :], st[:, 8 + k % 2, :], ACT.Tanh, scale=0.5
                                   ).then_inc(tanh_ready.handle, 1)
                vals = lambda slot, g, c: (st[:, slot + 2 * g:slot + 2 * g + 2, :]
                                           .rearrange("p a (b x) -> p (a b) x", b=2)[:, :, c * P:(c + 1) * P])
                for c in range(4):
                    take_values(1, l, 2 * c, lambda g: vals(14, g, c))
                    if c == 2:
                        act.dma_start(st[:, 8, :], c_ret).then_inc(retc_in.handle, 16)
                unread = mask_gqa[:, :].bitcast(mybir.dt.bfloat16)
                for n in range(NB):
                    act.wait_ge(r_summed.handle, r_summed.at(1, l, n + 1))
                    for t in range(4):
                        last = act.activation(unread[:, t * P:(t + 1) * P], ps[:, 6, t * P:(t + 1) * P], ACT.Square,
                                              accum_out=ssq[:, t:t + 1])
                    last.then_inc(r_squared.handle, 1)
                for c in range(4):
                    take_values(1, l, 8 + 2 * c, lambda g: vals(10, g, c))
                act.wait_ge(done.handle, done.at(1, l, 24))
                act.dma_start(hs[:, 0:4, :], c_alibi.rearrange("h p n -> p h n")).then_inc(alibi_in.handle, 16)
                attend(1, l, "dif", 0, 0, 0)
                act.wait_ge(mixed_out.handle, mixed_out.at(1, l, NB))
                split_hi(1, l, 8, lambda c: st[:, c, :])
                for c in range(KC):
                    act.wait_ge(taken.handle, taken.at(1, l, 24 + c + 1))
                    squares(c)
                split_hi(1, l, 16, lambda c: xt[:, c, :], lambda c: cur[:, C_FN + c:C_FN + c + 1])
                take_factor(spread_ready.at(1, l, 2))
                n, chunk0 = 32, 0
                for group in FFN_GROUPS:
                    for c in range(group):
                        act.wait_ge(taken.handle, taken.at(1, l, n + 2 * c + 1))
                        act.activation(st[:, 18 + c % 2, :], st[:, 16 + c % 2, :], ACT.Tanh, scale=0.5
                                       ).then_inc(tanh_ready.handle, 1)
                        act.wait_ge(gated.handle, gated.at(1, l, chunk0 + c + 1))
                        act.activation(hid_hi[:, c, :], st[:, 16 + c % 2, :], ACT.Copy
                                       ).then_inc(hid_hi_ready.handle, 1)
                    n += 2 * group + KC
                    chunk0 += group
                for c in range(KC):
                    act.wait_ge(taken.handle, taken.at(1, l, BLOCKS[1] - KC + c + 1))
                    squares(c)

            take_factor(spread_ready.end(1))
            for c in range(KC):
                act.wait_ge(out_ready.handle, c + 1)
                act.dma_start(out[c, :, :], xt[:, c, :]).then_inc(out_sem.handle, 16)
            act.wait_ge(out_sem.handle, 16 * KC)

        @block.vector
        def _(dve):
            own = Chain(dve, dve_own)
            link = own.link

            def evacuate(stack, l, n, to):
                j = n % 2
                dve.wait_ge(done.handle, done.at(stack, l, n + 1))
                dve.tensor_tensor(to, ps[:, 2 * j:2 * j + 2, :].rearrange("p a b -> p (a b)"), rfac[:, :], ALU.mult
                                  ).then_inc(taken.handle, 1)

            def add_to_x(stack, l, n, c):
                dve.wait_ge(done.handle, done.at(stack, l, n + 1))
                last = dve.tensor_tensor(xt[:, c, :], xt[:, c, :],
                                         ps[:, 2 * (n % 2):2 * (n % 2) + 2, :].rearrange("p a b -> p (a b)"), ALU.add)
                last.then_inc(taken.handle, 1)

            def split_lo(stack, l, base, source, scale=None):
                for c in range(KC):
                    dve.wait_ge(hi_ready.handle, hi_ready.at(stack, l, base + c + 1))
                    if scale:
                        i = dve.scalar_tensor_tensor(in_lo[:, c, :], source(c), scale(c), in_hi[:, c, :].bitcast(F32),
                                                     ALU.mult, ALU.subtract)
                    else:
                        i = dve.tensor_tensor(in_lo[:, c, :], source(c), in_hi[:, c, :].bitcast(F32), ALU.subtract)
                    i.then_inc(lo_ready.handle, 1)

            def sum_squares(wait, c):
                dve.wait_ge(squared.handle, wait)
                i = dve.tensor_tensor(st[:, ACC, :], st[:, ACC, :], st[:, SQ[c % 2], :], ALU.add)
                if c == KC - 1:
                    i.then_inc(acc_ready.handle, 1)
                else:
                    link(i)

            def rsqrt(x, y, t):
                link(dve.tensor_scalar(t.bitcast(I32), x.bitcast(I32), 1, None, ALU.logical_shift_right))
                link(dve.tensor_scalar(y.bitcast(I32), t.bitcast(I32), -1.0, float(0x5F3759DF), ALU.mult, ALU.add))
                for _ in range(3):
                    link(dve.tensor_tensor(t, y, y, ALU.mult))
                    link(dve.scalar_tensor_tensor(t, t, -0.5, x, ALU.mult, ALU.mult))
                    link(dve.scalar_tensor_tensor(y, t, 1.5, y, ALU.add, ALU.mult))

            def row_factor(wait, count):
                dve.wait_ge(stat_ready.handle, wait)
                link(dve.tensor_scalar(stat, ps[:, 4, 0:8], 1.0 / count, EPS, ALU.mult, ALU.add))
                rsqrt(stat, root, tmp)
                dve.tensor_tensor(st[:, DIAG, :].rearrange("p (b c) -> p b c", b=NB),
                                  ident.unsqueeze(1).broadcast_to([P, NB, P]),
                                  root.unsqueeze(2).broadcast_to([P, NB, P]), ALU.mult).then_inc(diag_ready.handle, 1)

            def attend(stack, l, kind, m0, g0, r0, bias, finish):
                maps = 2 if kind == "dif" else 1
                width = P if kind == "dif" else HD
                units = [(n, t) for n in range(NB) for t in range(4)]

                def scores(u):
                    n, t = units[u]
                    cols = len(tiles_of_round(kind, n)) * P
                    for j in range(maps):
                        m = maps * u + j
                        dve.wait_ge(scored.handle, scored.at(stack, l, m0 + m + 1))
                        if m >= 4:
                            gi = sum(len(groups_of(tiles_of_round(kind, units[v][0]))) for v in range((m - 4) // maps + 1))
                            dve.wait_ge(turned.handle, turned.at(stack, l, g0 + gi))
                        dve.sem_inc(dve_step)
                        i = maps * t + j
                        first = cur[:, C_SINK + t:C_SINK + t + 1] if kind == "gqa" else 3.0e38
                        b = 2 * (m % 2)
                        src = ps[:, b:b + 2, :].rearrange("p a b -> p (a b)")[:, 0:cols]
                        dve.tensor_tensor_reduce(hs[:, 7 + m % 4, 0:cols], src, bias(n, t), -SCALE, first,
                                                 ALU.add, ALU.min, negm[:, n % 2, i:i + 1]).then_inc(biased.handle, 1)
                    if kind == "gqa" and t == 3:
                        dve.wait_ge(biased.handle, biased.at(stack, l, m0 + m + 1))
                        dve.tensor_tensor(comb, negm[:, n % 2, 0:4], cur[:, C_SINK:C_SINK + 4], ALU.subtract
                                          ).then_inc(sink_ready.handle, 1)

                def mix(u):
                    n, t = units[u]
                    cols = (n + 1) * P
                    dve.wait_ge(expd.handle, expd.at(stack, l, m0 + 2 * u + 2))
                    r = rinv[:, n % 2, :]
                    link(dve.reciprocal(r[:, 2 * t:2 * t + 2], lsum[:, n % 2, 2 * t:2 * t + 2]))
                    link(dve.scalar_tensor_tensor(comb[:, t:t + 1], lsum[:, n % 2, 2 * t:2 * t + 1],
                                                  cur[:, C_NLAM:C_NLAM + 1], r[:, 2 * t + 1:2 * t + 2],
                                                  ALU.mult, ALU.mult))
                    e0, e1 = hs[:, 7 + (2 * u) % 4, 0:cols], hs[:, 7 + (2 * u + 1) % 4, 0:cols]
                    dve.scalar_tensor_tensor(e0, e1, comb[:, t:t + 1], e0, ALU.mult, ALU.add
                                             ).then_inc(mixed.handle, 1)

                def heads(n):
                    if kind == "dif":
                        dve.wait_ge(head_sq.handle, head_sq.at(stack, l, n + 1))
                        link(dve.tensor_scalar(stat[:, 0:4], ssq[:, 0:4], 1.0 / P, EPS, ALU.mult, ALU.add))
                        rsqrt(stat[:, 0:4], root[:, 0:4], tmp[:, 0:4])
                        link(dve.tensor_tensor(factor, root[:, 0:4],
                                               rinv[:, n % 2, :].rearrange("p (a b) -> p a b", b=2)[:, :, 0], ALU.mult))
                    else:
                        dve.wait_ge(expd.handle, expd.at(stack, l, m0 + 4 * n + 4))
                        total = lsum[:, n % 2, 0:4]
                        if kind == "gqa":
                            dve.wait_ge(sink_exp.handle, sink_exp.at(stack, l, n + 1))
                            link(dve.tensor_tensor(total, total, esink, ALU.add))
                        link(dve.reciprocal(factor, total))
                        dve.wait_ge(weighted.handle, weighted.at(stack, l, r0 + n + 1))
                    if n >= 2:
                        dve.wait_ge(back.handle, back.at(stack, l, r0 + n - 1))
                    dve.tensor_tensor(hs[:, 14, (n % 2) * HALF:(n % 2) * HALF + 4 * width].rearrange("p (t e) -> p t e", t=4),
                                      ps[:, 6, 0:4 * width].rearrange("p (t e) -> p t e", t=4),
                                      factor.unsqueeze(2).broadcast_to([P, 4, width]), ALU.mult
                                      ).then_inc(headed.handle, 1)

                for u in range(len(units) + 4):
                    if u < len(units):
                        scores(u)
                    if kind == "dif" and 1 <= u < len(units) + 1:
                        mix(u - 1)
                    if u >= 5 and (u - 5) % 4 == 0 and (u - 5) // 4 < NB:
                        heads((u - 5) // 4)
                    if u >= 7 and (u - 7) % 4 == 0 and (u - 7) // 4 < NB:
                        n = (u - 7) // 4
                        dve.wait_ge(back.handle, back.at(stack, l, r0 + n + 1))
                        finish(n).then_inc(mixed_out.handle, 1)

            dve.engine_nop().then_inc(taken.handle, 2)
            for c in range(1, KC):
                sum_squares(c + 1, c)
            dve.wait_ge(const_in.handle, 16 * 3)
            dve.wait_ge(lam_sem.handle, 16)
            own.restart()
            lam = st[:, 0, 0:DEPTH * 4 * HD].rearrange("p (l v d) -> p l v d", l=DEPTH, v=4)
            for l in range(DEPTH):
                for i in range(2):
                    k = 2 * l + i
                    link(dve.tensor_tensor_reduce(st[:, 1, k * HD:(k + 1) * HD], lam[:, l, 2 * i, :], lam[:, l, 2 * i + 1, :],
                                                  1.0, 0.0, ALU.mult, ALU.add, small[:, k:k + 1]))
            dve.engine_nop().then_inc(lam_exp.handle, 1)
            dve.wait_ge(lam_exp.handle, 2)
            for l in range(DEPTH):
                lam_init = 0.8 - 0.6 * float(np.exp(-0.3 * l))
                o = O2 + l * W2
                link(dve.tensor_tensor(tmp[:, 0:1], small[:, 4 + 2 * l + 1:4 + 2 * l + 2], small[:, 4 + 2 * l:4 + 2 * l + 1],
                                       ALU.subtract))
                link(dve.tensor_scalar(par[:, o + C_NLAM:o + C_NLAM + 1], tmp[:, 0:1], -lam_init, None, ALU.add))
                link(dve.tensor_scalar(par[:, o + C_RN:o + C_RN + 1], par[:, o + C_RN:o + C_RN + 1], 0.5, None, ALU.mult))
                link(dve.tensor_scalar(par[:, o + C_DN:o + C_DN + 1], par[:, o + C_DN:o + C_DN + 1], 1.0 - lam_init, None,
                                       ALU.mult))
                o = l * W1 + C_SINK
                link(dve.tensor_scalar(par[:, o:o + 4], par[:, o:o + 4], -1.0, None, ALU.mult))

            with dve.Fori(0, DEPTH) as l:
                own.restart()
                dve.tensor_copy(cur[:, :], par[:, bass.ds(l * W1, W1)]).then_inc(cur_ready.handle, 1)
                split_lo(0, l, 0, lambda c: xt[:, c, :], lambda c: cur[:, C_NORM + c:C_NORM + c + 1])
                row_factor(stat_ready.at(0, l, 1), D)
                dve.wait_ge(fac_ready.handle, fac_ready.at(0, l, 1))

                evacuate(0, l, 0, st[:, 8, :])
                evacuate(0, l, 1, st[:, 9, :])

                def gate_input(i):
                    dve.wait_ge(tanh_ready.handle, tanh_ready.at(0, l, i + 1))
                    dve.wait_ge(taken.handle, taken.at(0, l, 2 * i + 2))
                    link(dve.scalar_tensor_tensor(st[:, 14 + i, :], st[:, 8 + 2 * i, :], 1.0, st[:, 9 + 2 * i, :],
                                                  ALU.add, ALU.mult))

                gate_input(0)
                evacuate(0, l, 2, st[:, 10, :])
                evacuate(0, l, 3, st[:, 11, :])
                gate_input(1)

                def tap(acc, source, weight, d, first):
                    a, b = max(0, -d), S - max(0, d)
                    if first:
                        return dve.tensor_scalar(acc, source, weight, None, ALU.mult)
                    return dve.scalar_tensor_tensor(acc[:, a:b], source[:, a + d:b + d], weight, acc[:, a:b],
                                                    ALU.mult, ALU.add)

                mid = TAPS_A // 2
                order = [mid] + [k for k in range(TAPS_A) if k != mid]
                taps = [(k, c) for k in order for c in range(2)]

                def conv_taps(count):
                    for _ in range(count):
                        k, c = taps.pop(0)
                        w = cur[:, C_CAW + TAPS_A * c + k:C_CAW + TAPS_A * c + k + 1]
                        link(tap(st[:, 12 + c, :], st[:, 14 + c, :], w, k - mid, k == mid))

                conv_taps(6)
                def gate(k):
                    dve.wait_ge(tanh_ready.handle, tanh_ready.at(0, l, 2 + k + 1))
                    dve.scalar_tensor_tensor(st[:, k, :], st[:, 10 + k % 2, :], 1.0, st[:, 8 + k % 2, :],
                                             ALU.add, ALU.mult)
                for k in range(8):
                    evacuate(0, l, 4 + k, st[:, 8 + k % 2, :])
                    if k:
                        gate(k - 1)
                    conv_taps(6)
                evacuate(0, l, 12, st[:, 8, :])
                gate(7)
                conv_taps(len(taps) // 2)
                evacuate(0, l, 13, st[:, 9, :])

                def gated_conv(i, stage):
                    cx, y = st[:, 10, :], st[:, 11, :]
                    w = lambda k: cur[:, C_CBW + TAPS_B * i + k:C_CBW + TAPS_B * i + k + 1]
                    if stage == 0:
                        dve.wait_ge(taken.handle, taken.at(0, l, 14 + 3 * i))
                        link(dve.tensor_tensor(cx, st[:, 8, :], st[:, 9, :], ALU.mult))
                        link(tap(y, cx, w(1), 0, True))
                        link(tap(y, cx, w(0), -1, False))
                        link(tap(y, cx, w(2), 1, False))
                    else:
                        dve.wait_ge(taken.handle, taken.at(0, l, 15 + 3 * i))
                        link(dve.tensor_tensor(y, y, st[:, 8, :], ALU.mult))
                        link(dve.scalar_tensor_tensor(st[:, 2 + i, :], y, 0.5, st[:, 2 + i, :], ALU.mult, ALU.mult))

                conv_taps(len(taps))
                for c in range(2):
                    last = dve.tensor_scalar(st[:, 12 + c, :], st[:, 12 + c, :], 0.5, cur[:, C_CAB + c:C_CAB + c + 1],
                                             ALU.mult, ALU.add)
                last.then_inc(conv_ready.handle, 1)
                gated_conv(0, 0)
                evacuate(0, l, 14, st[:, 8, :])
                gated_conv(0, 1)
                evacuate(0, l, 15, st[:, 8, :])
                dve.wait_ge(mean_ready.handle, mean_ready.at(0, l, 1))
                for c in range(2):
                    dve.scalar_tensor_tensor(st[:, 12 + c, :], ps[:, 4:6, :].rearrange("p a b -> p (a b)"), -1.0 / (2 * P),
                                             st[:, 12 + c, :], ALU.mult, ALU.add).then_inc(centred.handle, 1)
                evacuate(0, l, 16, st[:, 9, :])
                row_factor(stat_ready.at(0, l, 2), 2 * P)
                gated_conv(1, 0)
                evacuate(0, l, 17, st[:, 8, :])
                gated_conv(1, 1)
                evacuate(0, l, 18, st[:, 10, :])
                dve.wait_ge(fac_ready.handle, fac_ready.at(0, l, 2))
                for c in range(2):
                    dve.tensor_tensor(st[:, 12 + c, :], st[:, 12 + c, :], st[:, 16, :], ALU.mult
                                      ).then_inc(normed.handle, 1)
                evacuate(0, l, 19, st[:, 11, :])

                def rotate(i, slot):
                    for h in range(2):
                        dve.wait_ge(swapped.handle, swapped.at(0, l, 2 * i + h + 1))
                        a = slice(h * HALF, (h + 1) * HALF)
                        link(dve.tensor_tensor(half[:, :], ps[:, 6 + h, :], st[:, 21, a], ALU.mult))
                        link(dve.tensor_tensor(st[:, slot, a], st[:, slot, a], st[:, 20, a], ALU.mult))
                        i2 = dve.tensor_tensor(st[:, slot, a], st[:, slot, a], half[:, :], ALU.add)
                        i2.then_inc(roped.handle, 1)
                        dve.wait_ge(roped.handle, roped.at(0, l, 2 * i + h + 1))

                dve.wait_ge(rope_in.handle, rope_in.at(0, l, 32))
                evacuate(0, l, 20, st[:, 17, :])
                rotate(0, 10)
                for c in range(2):
                    dve.wait_ge(lnact_ready.handle, lnact_ready.at(0, l, c + 1))
                    link(dve.scalar_tensor_tensor(st[:, 12 + c, :], st[:, 14 + c, :], 1.0, st[:, 12 + c, :],
                                                  ALU.add, ALU.mult))
                    link(dve.scalar_tensor_tensor(st[:, c, :], st[:, 12 + c, :], 0.25, st[:, c, :], ALU.mult, ALU.mult))
                evacuate(0, l, 21, st[:, 8, :])
                rotate(1, 11)
                evacuate(0, l, 22, st[:, 19, :])
                rotate(2, 17)
                for n, slot in ((23, 12), (24, 13), (25, 14), (26, 9), (27, 22)):
                    evacuate(0, l, n, st[:, slot, :])

                def back_to_chunks(first):
                    def finish(n):
                        y = st[:, first:first + 2, n * P:(n + 1) * P]
                        return dve.scalar_tensor_tensor(y, ps[:, 7, 0:2 * P].rearrange("p (c q) -> p c q", c=2), 0.5, y,
                                                        ALU.mult, ALU.mult)
                    return finish

                attend(0, l, "gqa", 0, 0, 0,
                       lambda n, t: mask_gqa[:, (tiles_of_round("gqa", n)[0] - n + 1) * P:
                                             (tiles_of_round("gqa", n)[-1] - n + 2) * P],
                       back_to_chunks(4))

                dve.wait_ge(bias_in.handle, bias_in.at(0, l, 64))
                table = hs[:, 0:4, :].rearrange("p a n -> p (a n)")[:, 0:4 * ND * GRID_W]
                inner = hs[:, 4:7, :].rearrange("p a n -> p (a n)")[:, 0:4 * 10 * GRID_W]
                link(dve.scalar_tensor_tensor(table.rearrange("p (g c) -> p g c", c=GRID_W),
                                              table.rearrange("p (g c) -> p g c", c=GRID_W), 1.0 / SCALE,
                                              hs[:, 15, 0:GRID_W].unsqueeze(1).broadcast_to([P, 4 * ND, GRID_W]),
                                              ALU.mult, ALU.add))
                table_h = table.rearrange("p (h r) -> p h r", h=4)
                inner_h = inner.rearrange("p (h r) -> p h r", h=4)
                dve.tensor_tensor(inner_h, table_h[:, :, 3 * GRID_W:13 * GRID_W],
                                  hs[:, 15, GRID_W:11 * GRID_W].unsqueeze(1).broadcast_to([P, 4, 10 * GRID_W]), ALU.add
                                  ).then_inc(bias_ready.handle, 1)
                dve.wait_ge(bias_ready.handle, bias_ready.at(0, l, 1))

                def na_bias(n, t):
                    if 2 <= n <= NB - 3:
                        return inner_h[:, t, :]
                    r = 2 * tiles_of_round("na", n)[0] - 2 * n + KH - 1
                    return table_h[:, t, r * GRID_W:(r + 8) * GRID_W]

                attend(0, l, "na", ag["maps"], ag["groups"], NB, na_bias, back_to_chunks(6))
                dve.wait_ge(mixed_out.handle, mixed_out.at(0, l, 2 * NB))
                split_lo(0, l, 8, lambda c: st[:, c, :])
                for c in range(KC):
                    add_to_x(0, l, 28 + c, c)
                    if c >= 2:
                        sum_squares(squared.at(0, l, c), c - 1)
                sum_squares(squared.at(0, l, KC), KC - 1)

            own.restart()
            row_factor(stat_ready.mid(1), D)
            dve.wait_ge(fac_ready.handle, fac_ready.mid(1))
            for c in range(KC):
                dve.scalar_tensor_tensor(xt[:, c, :], xt[:, c, :], par[:, O_FIN1 + c:O_FIN1 + c + 1], rfac[:, :],
                                         ALU.mult, ALU.mult).then_inc(x_scaled.handle, 1)
                if c >= 2:
                    sum_squares(squared.mid(c), c - 1)
            sum_squares(squared.mid(KC), KC - 1)

            with dve.Fori(0, DEPTH) as l:
                own.restart()
                dve.tensor_copy(cur[:, 0:W2], par[:, bass.ds(l * W2 + O2, W2)]).then_inc(cur_ready.handle, 1)
                split_lo(1, l, 0, lambda c: xt[:, c, :], lambda c: cur[:, C_AN + c:C_AN + c + 1])
                row_factor(stat_ready.at(1, l, 1), D)
                dve.wait_ge(fac_ready.handle, fac_ready.at(1, l, 1))
                for k in range(4):
                    evacuate(1, l, k, st[:, 8 + k % 2, :])
                    if k:
                        dve.wait_ge(tanh_ready.handle, tanh_ready.at(1, l, k))
                        link(dve.scalar_tensor_tensor(st[:, k - 1, :], st[:, 10 + (k - 1) % 2, :], 1.0,
                                                      st[:, 8 + (k - 1) % 2, :], ALU.add, ALU.mult))
                dve.wait_ge(tanh_ready.handle, tanh_ready.at(1, l, 4))
                link(dve.scalar_tensor_tensor(st[:, 3, :], st[:, 11, :], 1.0, st[:, 9, :], ALU.add, ALU.mult))
                for k in range(4):
                    evacuate(1, l, 4 + k, st[:, 10 + k, :])
                for k in range(4):
                    if k >= 2:
                        dve.wait_ge(vt_ready.handle, vt_ready.at(1, l, 2 * (k - 1)))
                    evacuate(1, l, 8 + k, st[:, 8 + k % 2, :])

                tables = st[:, 8, :]
                decay, q_decay, k_decay = tables[:, 0:512], tables[:, 512:768], tables[:, 768:1024]

                def r_decays(n):
                    dve.wait_ge(r_scored.handle, r_scored.at(1, l, n + 1))
                    if n == 0:
                        dve.wait_ge(retc_in.handle, retc_in.at(1, l, 16))
                        link(dve.memset(state_of(0), 0.0))
                        link(dve.memset(state_of(1), 0.0))
                    else:
                        dve.wait_ge(r_summed.handle, r_summed.at(1, l, n))
                    dve.tensor_tensor(st[:, 9, 0:512].rearrange("p (a b) -> p a b", a=2), ps[:, 4:6, 0:256],
                                      decay.rearrange("p (a b) -> p a b", a=2), ALU.mult)
                    dve.tensor_tensor(st[:, 22, 0:256], ps[:, 4, 256:512], k_decay, ALU.mult)
                    dve.tensor_tensor(st[:, 22, 256:512].rearrange("p (c q) -> p c q", c=2),
                                      st[:, 10:12, n * P:(n + 1) * P],
                                      q_decay.rearrange("p (c q) -> p c q", c=2), ALU.mult).then_inc(r_decayed.handle, 1)

                def r_next(n):
                    dve.wait_ge(r_summed.handle, r_summed.at(1, l, n + 1))
                    if n < NB - 1:
                        for t in range(4):
                            b = HD * (t % 2)
                            a = slice(t * P, (t + 1) * P)
                            i = dve.scalar_tensor_tensor(state_of(n + 1)[b:b + HD, a], state_of(n)[b:b + HD, a],
                                                         chunk_decay(t), ps[b:b + HD, 5, 256 + (t // 2) * P:256 + (t // 2 + 1) * P],
                                                         ALU.mult, ALU.add)
                        i.then_inc(r_state.handle, 1)
                        dve.wait_ge(r_state.handle, r_state.at(1, l, n + 1))
                    dve.wait_ge(r_squared.handle, r_squared.at(1, l, n + 1))
                    link(dve.tensor_scalar(stat[:, 0:4], ssq[:, 0:4], 1.0 / P, EPS, ALU.mult, ALU.add))
                    rsqrt(stat[:, 0:4], root[:, 0:4], tmp[:, 0:4])
                    if n >= 1:
                        dve.wait_ge(r_back.handle, r_back.at(1, l, n))
                    dve.tensor_tensor(half[:, :].rearrange("p (t e) -> p t e", t=4),
                                      ps[:, 6, :].rearrange("p (t e) -> p t e", t=4),
                                      root[:, 0:4].unsqueeze(2).broadcast_to([P, 4, P]), ALU.mult
                                      ).then_inc(r_headed.handle, 1)

                def r_finish(n):
                    dve.wait_ge(r_back.handle, r_back.at(1, l, n + 1))
                    y = st[:, 0:4, n * P:(n + 1) * P]
                    dve.scalar_tensor_tensor(y, ps[:, 7, :].rearrange("p (c q) -> p c q", c=4), cur[:, C_RN:C_RN + 1], y,
                                             ALU.mult, ALU.mult).then_inc(r_out.handle, 1)

                places = (4, 5, 6, 7, 18, 19, 20, 21, 8, 9)
                for n in range(NB + 2):
                    if 1 <= n < NB + 1:
                        r_next(n - 1)
                    evacuate(1, l, 12 + n, st[:, places[n], :])
                    if n < NB:
                        r_decays(n)
                    if n >= 2:
                        r_finish(n - 2)
                evacuate(1, l, 22, st[:, 14, :])
                evacuate(1, l, 23, st[:, 15, :])

                def dif_finish(n):
                    return dve.tensor_scalar(st[:, 4:8, n * P:(n + 1) * P], ps[:, 7, :].rearrange("p (c q) -> p c q", c=4),
                                             cur[:, C_DN:C_DN + 1], None, ALU.mult)

                dve.wait_ge(alibi_in.handle, alibi_in.at(1, l, 16))
                attend(1, l, "dif", 0, 0, 0, lambda n, t: hs[:, t, S - (n + 1) * P:S], dif_finish)
                dve.wait_ge(mixed_out.handle, mixed_out.at(1, l, NB))
                split_lo(1, l, 8, lambda c: st[:, c, :])
                for c in range(KC):
                    add_to_x(1, l, 24 + c, c)
                    if c >= 2:
                        sum_squares(squared.at(1, l, c), c - 1)
                sum_squares(squared.at(1, l, KC), KC - 1)

                split_lo(1, l, 16, lambda c: xt[:, c, :], lambda c: cur[:, C_FN + c:C_FN + c + 1])
                row_factor(stat_ready.at(1, l, 2), D)
                dve.wait_ge(fac_ready.handle, fac_ready.at(1, l, 2))
                n, chunk0 = 32, 0

                def hidden_lo(c, i):
                    dve.wait_ge(hid_hi_ready.handle, hid_hi_ready.at(1, l, i + 1))
                    dve.tensor_tensor(hid_lo[:, c, :], st[:, 16 + c % 2, :], hid_hi[:, c, :].bitcast(F32), ALU.subtract
                                      ).then_inc(hid_lo_ready.handle, 1)

                for group in FFN_GROUPS:
                    for c in range(group):
                        i = chunk0 + c
                        g, t = st[:, 16 + c % 2, :], st[:, 18 + c % 2, :]
                        evacuate(1, l, n + 2 * c, g)
                        if c:
                            hidden_lo(c - 1, i - 1)
                        dve.wait_ge(tanh_ready.handle, tanh_ready.at(1, l, 4 + i + 1))
                        link(dve.scalar_tensor_tensor(t, t, 1.0, g, ALU.add, ALU.mult))
                        up = n + 2 * c + 1
                        dve.wait_ge(done.handle, done.at(1, l, up + 1))
                        dve.scalar_tensor_tensor(g, ps[:, 2 * (up % 2):2 * (up % 2) + 2, :].rearrange("p a b -> p (a b)"),
                                                 0.5, rfac[:, :], ALU.mult, ALU.mult).then_inc(taken.handle, 1)
                        dve.wait_ge(taken.handle, taken.at(1, l, up + 1))
                        dve.tensor_tensor(g, g, t, ALU.mult).then_inc(gated.handle, 1)
                    hidden_lo(group - 1, chunk0 + group - 1)
                    n += 2 * group
                    chunk0 += group
                    for c in range(KC):
                        add_to_x(1, l, n + c, c)
                        if chunk0 == HC and c >= 2:
                            sum_squares(squared.at(1, l, KC + c), c - 1)
                    n += KC
                sum_squares(squared.at(1, l, 2 * KC), KC - 1)

            own.restart()
            row_factor(stat_ready.end(1), D)
            dve.wait_ge(fac_ready.handle, fac_ready.end(1))
            for c in range(KC):
                dve.scalar_tensor_tensor(xt[:, c, :], xt[:, c, :], par[:, O_FIN2 + c:O_FIN2 + c + 1], rfac[:, :],
                                         ALU.mult, ALU.mult).then_inc(out_ready.handle, 1)


def gammas():
    return (1.0 - np.exp2(-5.0 - np.arange(4, dtype=np.float32))).astype(np.float32)


def chunk_decay(t):
    return float(np.exp(np.float32(P) * np.log(gammas()[t])))


def constants():
    f = np.float32
    eye = np.eye(P, dtype=f)
    swap = np.zeros((P, P), f)
    for p in range(P):
        swap[(p // HD) * HD + (p % HD + HD // 2) % HD, p] = 1.0
    inv = (f(10000.0) ** (-np.arange(0, HD, 2, dtype=f) / f(HD))).astype(f)
    ang = (np.arange(S, dtype=f)[None, :] * inv[:, None]).astype(f)
    rope = np.stack([np.tile(np.cos(ang), (4, 1)), np.tile(np.concatenate([-np.sin(ang), np.sin(ang)]), (2, 1))])
    q, k = np.arange(P)[:, None], np.arange(3 * P)[None, :] - P
    gqa = np.where(np.abs(k - q) <= P, 0.0, NEG / SCALE)
    c = np.arange(GRID_W)
    c0 = np.clip(c - KW // 2, 0, GRID_W - KW)
    col = (c[None, :] >= c0[:, None]) & (c[None, :] < c0[:, None] + KW)
    col = np.tile(np.where(col, 0.0, NEG / SCALE), (2, 1))
    row = np.arange(10)[None, :] - np.repeat(np.arange(2), GRID_W)[:, None]
    row = np.where((row >= 0) & (row < KH), 0.0, NEG / SCALE)
    na = np.concatenate([col, np.repeat(row, GRID_W, axis=1)], axis=1)
    lg = np.log(gammas())
    i = np.arange(P, dtype=f)
    rel = i[None, :] - i[:, None]
    decay = [np.where(rel >= 0, np.exp(np.maximum(rel, 0) * lg[t]), 0) * SCALE for t in (0, 2, 1, 3)]
    qd = [np.repeat(np.stack([np.exp((i + 1) * lg[2 * p]), np.exp((i + 1) * lg[2 * p + 1])]), HD, axis=0) for p in range(2)]
    kd = [np.repeat(np.exp((P - 1 - i) * g)[:, None], HD, axis=1) * SCALE for g in lg]
    ret = np.concatenate(decay + qd + kd, axis=1)
    r = np.arange(S)[None, :] - (S - P) - np.arange(P)[:, None]
    alibi = np.stack([np.where(r <= 0, 2.0 ** (-2.0 * (h + 1)) * r / SCALE, NEG / SCALE) for h in range(4)])
    return {"c_square": np.stack([eye, swap]), "c_rope": rope, "c_gqa": gqa, "c_na": na, "c_ret": ret, "c_alibi": alibi}


def columns(first, count):
    return [np.arange(first + P * c, first + P * (c + 1)) for c in range(count)]


def head_columns(first):
    heads = np.concatenate([np.arange(first + HD * h, first + HD * (h + 1)) for h in GQA_ORDER])
    return [heads[:P], heads[P:]]


def weight_block(w, rows, cols):
    part = w[rows][:, cols]
    k = part.shape[0] // P
    block = np.zeros((P, KC, P), w.dtype)
    block[:, :k] = part.reshape(k, P, P).transpose(1, 0, 2)
    return block.reshape(P, KC * P)


def weight_stream(i):
    blocks = []
    u, v, az, bb, bc, bx, bz = (columns(256 * n, 2) for n in range(7))
    cq, ck, cv, cz = head_columns(1792), columns(2048, 1), columns(2176, 1), head_columns(2304)
    dq, dk, dv, dz = (columns(2560 + 256 * n, 2) for n in range(4))
    every = slice(None)
    for l in range(DEPTH):
        order = [v[0], u[0], v[1], u[1]] + az + bz + cz + dz
        order += [bc[0], bx[0], bb[0], bc[1], bx[1], bb[1]] + cq + ck + cv + dq + dk + dv
        blocks += [weight_block(i["w_in"][l], every, c) for c in order]
        rows = np.concatenate([np.arange(512)] + head_columns(512) + [np.arange(768, 1024)])
        blocks += [weight_block(i["w_out"][l], rows, c) for c in columns(0, KC)]
    for l in range(DEPTH):
        order = columns(1024, 4) + columns(0, 8) + columns(1536, 12)
        blocks += [weight_block(i["w_in_2"][l], every, c) for c in order]
        blocks += [weight_block(i["w_out_2"][l], every, c) for c in columns(0, KC)]
        chunk = 0
        for group in FFN_GROUPS:
            for c in columns(P * chunk, group):
                blocks += [weight_block(i["w_gate_2"][l], every, c), weight_block(i["w_up_2"][l], every, c)]
            rows = np.arange(P * chunk, P * (chunk + group))
            blocks += [weight_block(i["w_down_2"][l], rows, c) for c in columns(0, KC)]
            chunk += group
    return np.stack(blocks)


def parameters(i):
    def chunks(v):
        return v.reshape(-1, P).T

    cols = []
    for l in range(DEPTH):
        cols += [chunks(i["norm_g"][l])]
        cols += [i["conv_a_w"][l][:, P * c:P * (c + 1)].T for c in range(2)]
        cols += [chunks(i[n][l]) for n in ("conv_a_b", "ln_a_g", "ln_a_b")]
        cols += [i["conv_b_w"][l][:, P * c:P * (c + 1)].T for c in range(2)]
        cols += [np.broadcast_to(i["swa_sink"][l][list(GQA_ORDER)], (P, 4))]
    for l in range(DEPTH):
        cols += [chunks(i[n][l]) for n in ("attn_norm_2", "ffn_norm_2", "ret_norm_2", "diff_norm_2")]
        cols += [np.zeros((P, 1), np.float32)]
    cols += [chunks(i["final_norm_g"]), chunks(i["final_norm_2"])]
    return np.concatenate(cols, axis=1)


def kernel(**inputs):
    import concourse.bacc as bacc
    from concourse.bass_utils import run_bass_kernel_spmd

    i = {k: np.asarray(v) for k, v in inputs.items()}
    lam = np.stack([i[n] for n in ("lambda_q1_2", "lambda_k1_2", "lambda_q2_2", "lambda_k2_2")], axis=1)
    pad = np.pad(i["na_rpb"], ((0, 0), (0, 0), (0, 0), (GRID_W - KW, SKEW - GRID_W - KW + 1)))
    arrays = {
        "x_in": i["x"][0].T.reshape(KC, P, S),
        "w_in": weight_stream(i),
        "par_in": parameters(i),
        "lam_in": np.broadcast_to(lam.reshape(1, -1), (P, DEPTH * 4 * HD)),
        "rpb_in": np.broadcast_to(pad.reshape(DEPTH, 4 * ND, 1, SKEW), (DEPTH, 4 * ND, GRID_W, SKEW)
                                  ).reshape(DEPTH, 4 * ND, GRID_W * SKEW),
        **{k: v.astype(np.float32) for k, v in constants().items()},
    }
    arrays = {k: np.ascontiguousarray(v) for k, v in arrays.items()}
    nc = bacc.Bacc("TRN2", target_bir_lowering=False, num_devices=1, dynamic_dma_scratch_size=1024)
    args = {k: nc.dram_tensor(k, v.shape, F32, kind="ExternalInput").ap() for k, v in arrays.items()}
    out = nc.dram_tensor("out", (KC, P, S), F32, kind="ExternalOutput").ap()
    build(nc, out=out, **args)
    r = run_bass_kernel_spmd(nc, [arrays], core_ids=[0])
    return np.ascontiguousarray(r.results[0]["out"].reshape(D, S).T).reshape(1, S, D)
```

```python
from contextlib import ExitStack

import numpy as np

import concourse.bass as bass
from concourse import mybir

F32 = mybir.dt.float32
F32R = mybir.dt.float32r
I32 = mybir.dt.int32
ALU = mybir.AluOpType
ACT = mybir.ActivationFunctionType

P = 128
S = 1024
HALF = 512
D = 1024
KC = D // P
NB = S // P
DEPTH = 2
EPS = 1e-6
NEG = -1e30
HD = 64
SCALE = HD ** -0.5
FFN = 2816
HC = FFN // P
FFN_GROUPS = [8, 8, 6]
TAPS_A, TAPS_B = 31, 3
GRID_W, KH, KW = 64, 8, 16
ROWS = S // GRID_W
ND = 2 * KH - 1
SKEW = 2 * GRID_W

BLOCKS = (28 + 2 * KC, 24 + 2 * KC + 2 * HC + KC * len(FFN_GROUPS))
N_W = DEPTH * sum(BLOCKS)
SLOTS = 23

C_NORM, C_CAW, C_CAB, C_LNG, C_LNB, C_CBW, C_SINK = 0, 8, 70, 72, 74, 76, 82
W1 = 86
C_AN, C_FN, C_RN, C_DN, C_NLAM = 0, 8, 16, 17, 18
W2 = 19
O2 = DEPTH * W1
O_FIN1 = O2 + DEPTH * W2
O_FIN2 = O_FIN1 + 8
NPAR = O_FIN2 + 8

GQA_ORDER = (0, 2, 1, 3)


def tiles_of_round(kind, n):
    if kind == "gqa":
        return range(max(0, n - 1), min(NB, n + 2))
    if kind == "na":
        if 2 <= n <= NB - 3:
            return range(n - 2, n + 3)
        return range(0, 4) if n < 2 else range(NB - 4, NB)
    return range(0, n + 1)


def groups_of(tiles):
    tiles = list(tiles)
    n = -(-len(tiles) // 4)
    size = -(-len(tiles) // n)
    return [tiles[i:i + size] for i in range(0, len(tiles), size)]


def pieces_of(tiles):
    return groups_of(tiles)


def attention_counts(kind):
    groups = sum(4 * len(groups_of(tiles_of_round(kind, n))) for n in range(NB))
    maps = 2 if kind == "dif" else 1
    return {"maps": 4 * NB * maps, "pieces": groups * maps, "units": 4 * NB, "groups": groups, "rounds": NB}


STEPS = 4 * NB + 5


class Signal:

    def __init__(self, handle, per, before=0, between=0):
        self.handle, self.per, self.before, self.between = handle, per, before, between

    def at(self, stack, l, n):
        base = self.before + (DEPTH * self.per[0] + self.between if stack else 0)
        return l * self.per[stack] + (base + n)

    def end(self, n=0):
        return self.before + self.between + DEPTH * sum(self.per) + n

    def mid(self, n):
        return self.before + DEPTH * self.per[0] + n


class Chain:

    def __init__(self, engine, handle):
        self.engine, self.handle, self.n = engine, handle, 0

    def restart(self):
        self.engine.sem_clear(self.handle)
        self.n = 0

    def link(self, instruction):
        self.n += 1
        instruction.then_inc(self.handle, 1)
        self.engine.wait_ge(self.handle, self.n)


def build(nc, x_in, w_in, par_in, lam_in, rpb_in, c_square, c_rope, c_gqa, c_na, c_ret, c_alibi, out):
    ctx = ExitStack()
    with ctx:
        top = [-(-nc.sbuf_base // 64) * 64]

        def sb(name, shape, dt=F32, at=None):
            offset = top[0] if at is None else at
            if at is None:
                top[0] += -(-4 * int(np.prod(shape[1:])) // 32) * 32
            return nc.alloc_sbuf_tensor_at(name, shape, dt, offset=offset)

        xt = sb("xt", [P, KC, S])
        base_in = top[0]
        in_hi = sb("in_hi", [P, KC, S], F32R)
        in_lo = sb("in_lo", [P, KC, S], F32R)
        w_raw = sb("w_raw", [P, 2, KC * P])
        w_hi = sb("w_hi", [P, 2, KC * P], F32R)
        w_lo = sb("w_lo", [P, 2, KC * P], F32R)
        base_st = top[0]
        st = sb("st", [P, SLOTS, S])
        rfac = sb("rfac", [P, S])
        half = sb("half", [P, HALF])
        square = sb("square", [P, 2, P])
        ident, swap = square[:, 0, :], square[:, 1, :]
        ones = sb("ones", [P, P])
        mask_gqa = sb("mask_gqa", [P, 3 * P])
        par = sb("par", [P, NPAR])
        cur = sb("cur", [P, W1])
        small = sb("small", [P, 96])
        space_hi = sb("space_hi", [P, 4, S], at=base_in + 4 * 4 * S)
        space_lo = sb("space_lo", [P, 4, S], at=base_in + 12 * 4 * S)
        hid_hi = sb("hid_hi", [P, 8, S], F32R, at=base_st)
        hid_lo = sb("hid_lo", [P, 8, S], F32R, at=base_st + 8 * 4 * S)

        stat, root, tmp = small[:, 0:8], small[:, 8:16], small[:, 16:24]
        negm = small[:, 24:40].rearrange("p (a b) -> p a b", a=2)
        lsum = small[:, 40:56].rearrange("p (a b) -> p a b", a=2)
        rinv = small[:, 56:72].rearrange("p (a b) -> p a b", a=2)
        esink, ssq, comb, factor = (small[:, 72 + 4 * i:76 + 4 * i] for i in range(4))

        ps = ctx.enter_context(nc.psum_tensor("ps", [P, 8, HALF], F32))

        sems = {}

        def signal(name, one=0, two=0, before=0, between=0):
            s = Signal(ctx.enter_context(nc.semaphore(name)), (one, two), before, between)
            sems[name] = s
            return s

        raw_in = [signal(f"raw_in{j}") for j in range(2)]
        w_split = signal("w_split", *BLOCKS)
        done = signal("done", *BLOCKS)
        taken = signal("taken", *BLOCKS, before=2)
        hi_ready = signal("hi_ready", 16, 24)
        lo_ready = signal("lo_ready", 16, 24)
        hid_hi_ready = signal("hid_hi_ready", 0, HC)
        hid_lo_ready = signal("hid_lo_ready", 0, HC)
        cur_ready = signal("cur_ready", 1, 1)
        squared = signal("squared", 8, 16, before=8, between=8)
        acc_ready = signal("acc_ready", 1, 2, before=1, between=1)
        stat_ready = signal("stat_ready", 2, 2, between=1)
        diag_ready = signal("diag_ready", 2, 2, between=1)
        spread_ready = signal("spread_ready", 2, 2, between=1)
        fac_ready = signal("fac_ready", 2, 2, between=1)
        tanh_ready = signal("tanh_ready", 10, 4 + HC)
        gated = signal("gated", 0, HC)
        conv_ready = signal("conv_ready", 1)
        mean_ready = signal("mean_ready", 1)
        centred = signal("centred", 2)
        lnsq_ready = signal("lnsq_ready", 2)
        normed = signal("normed", 2)
        lnact_ready = signal("lnact_ready", 2)
        conv_out = signal("conv_out", 2)
        rope_in = signal("rope_in", 2 * 16)
        swapped = signal("swapped", 6)
        roped = signal("roped", 6)
        vt_ready = signal("vt_ready", 6, 16)
        vt_taken = signal("vt_taken", 6, 16)
        bias_in = signal("bias_in", 4 * 16)
        bias_ready = signal("bias_ready", 1)
        ag, an, ad = (attention_counts(k) for k in ("gqa", "na", "dif"))
        both = {k: ag[k] + an[k] for k in ag}
        scored = signal("scored", both["pieces"], ad["pieces"])
        biased = signal("biased", both["pieces"], ad["pieces"])
        expd = signal("expd", both["maps"], ad["maps"])
        mixed = signal("mixed", 0, ad["units"])
        turned = signal("turned", both["groups"], ad["groups"])
        turned_out = signal("turned_out", both["groups"], ad["groups"])
        weighted = signal("weighted", both["rounds"], ad["rounds"])
        sink_ready = signal("sink_ready", ag["rounds"])
        sink_exp = signal("sink_exp", ag["rounds"])
        head_sq = signal("head_sq", 0, ad["rounds"])
        headed = signal("headed", both["rounds"], ad["rounds"])
        back = signal("back", both["rounds"], ad["rounds"])
        mixed_out = signal("mixed_out", both["rounds"], ad["rounds"])
        alibi_in = signal("alibi_in", 0, 16)
        retc_in = signal("retc_in", 0, 16)
        r_scored = signal("r_scored", 0, NB)
        r_decayed = signal("r_decayed", 0, NB)
        r_summed = signal("r_summed", 0, NB)
        r_squared = signal("r_squared", 0, NB)
        r_state = signal("r_state", 0, NB - 1)
        r_headed = signal("r_headed", 0, NB)
        r_back = signal("r_back", 0, NB)
        r_out = signal("r_out", 0, NB)
        x_in_sem = [signal(f"x_in{c}") for c in range(KC)]
        const_in = signal("const_in")
        lam_sem = signal("lam_sem")
        lam_exp = signal("lam_exp")
        par_ready = signal("par_ready")
        x_scaled = signal("x_scaled")
        out_ready = signal("out_ready")
        out_sem = signal("out_sem")
        dve_own = ctx.enter_context(nc.semaphore("dve_own"))
        dve_step = ctx.enter_context(nc.semaphore("dve_step"))
        act_own = ctx.enter_context(nc.semaphore("act_own"))
        pool_own = ctx.enter_context(nc.semaphore("pool_own"))

        ACC, DIAG, DIAG_LN, SQ = 22, 21, 16, (18, 19)

        def flat(tensor, first, count):
            return tensor[:, first:first + count, :].rearrange("p a n -> p (a n)")

        def exp_buffer(kind, m):
            if kind == "gqa":
                m %= 4
                return st[:, 16, 3 * P * m:3 * P * (m + 1)] if m < 2 else flat(st, 21, 2)[:, 3 * P * (m - 2):3 * P * (m - 1)]
            if kind == "na":
                return space_hi[:, m % 4, :]
            return space_hi[:, m % 6, :] if m % 6 < 4 else st[:, 12 + m % 6, :]

        def exp_buffers(kind):
            return 6 if kind == "dif" else 4

        def turned_buffer(kind, g):
            if kind == "gqa":
                g %= 3
                return flat(st, 21, 2)[:, 3 * P * (g + 2):3 * P * (g + 3)]
            return st[:, 8 + (g % 4) // 2, (g % 2) * HALF:(g % 2 + 1) * HALF]

        def head_buffer(kind, n):
            if kind == "gqa":
                return half[:, (n % 2) * 2 * P:(n % 2 + 1) * 2 * P]
            return st[:, 10 if kind == "na" else 14, (n % 2) * HALF:(n % 2 + 1) * HALF]

        def rv(n, t):
            return st[:, 14 + n // 2, (n % 2) * HALF + t * P:(n % 2) * HALF + (t + 1) * P]

        def state_of(n):
            return st[:, (22, 9)[n % 2], HALF:S]

        block = ctx.enter_context(nc.Block())

        @block.sync
        def _(sp):
            def load(pair, first):
                for j in range(2):
                    if not first:
                        sp.wait_ge(w_split.handle, pair * 2 + (j - 1))
                    sp.dma_start(w_raw[:, j, :], w_in[bass.ds(pair * 2 + j, 1), :, :].rearrange("a p n -> (a p) n")
                                 ).then_inc(raw_in[j].handle, 16)
            load(0, True)
            with sp.Fori(1, N_W // 2) as pair:
                load(pair, False)

        @block.gpsimd
        def _(pool):
            def split(pair, first):
                for j in range(2):
                    pool.wait_ge(raw_in[j].handle, pair * 16 + 16)
                    if not first:
                        pool.wait_ge(done.handle, pair * 2 + (j - 1))
                    pool.tensor_tensor(w_hi[:, j, :], w_raw[:, j, :], ones[:, 0:1].broadcast_to([P, KC * P]),
                                       ALU.mult).then_inc(pool_own, 1)
                    pool.wait_ge(pool_own, pair * 2 + (j + 2))
                    pool.tensor_tensor(w_lo[:, j, :], w_raw[:, j, :], w_hi[:, j, :].bitcast(F32),
                                       ALU.subtract).then_inc(w_split.handle, 1)
            pool.memset(ones[:, :], 1.0).then_inc(pool_own, 1)
            pool.wait_ge(pool_own, 1)
            split(0, True)
            with pool.Fori(1, N_W // 2) as pair:
                split(pair, False)

        @block.tensor
        def _(pe):
            def product(stack, l, n, hi, lo, chunks=KC, k0=0, before_chunk=None, between=()):
                n, j = n if isinstance(n, tuple) else (n, n % 2)
                pe.wait_ge(w_split.handle, w_split.at(stack, l, n + 1))
                pe.wait_ge(taken.handle, taken.at(stack, l, n - 1))
                i, at = 0, [(2 * b + 1) * 3 * chunks // max(1, len(between)) // 2 for b in range(len(between))]
                for k in range(chunks):
                    if before_chunk:
                        before_chunk(k)
                    for w, parts in ((w_hi, (hi, lo)), (w_lo, (hi,))):
                        for part in parts:
                            for b, work in zip(at, between):
                                if b == i:
                                    work()
                            i += 1
                            for h in range(2):
                                last = pe.matmul(ps[:, 2 * j + h, :], w[:, j, k * P:(k + 1) * P],
                                                 part[:, k0 + k, h * HALF:(h + 1) * HALF],
                                                 start=(k == 0 and w is w_hi and part is hi),
                                                 stop=(k == chunks - 1 and w is w_lo))
                last.then_inc(done.handle, 1)

            def products(stack, l, n0, n1, hi=in_hi, lo=in_lo, chunks=KC, k0=0):
                with pe.Fori(n0, n1, 2) as n:
                    product(stack, l, (n, 0), hi, lo, chunks, k0)
                    product(stack, l, (n + 1, 1), hi, lo, chunks, k0)

            def chunk_wait(stack, l, base, ready=lo_ready):
                return lambda k: pe.wait_ge(ready.handle, ready.at(stack, l, base + k + 1))

            def row_sums(tiles):
                for b in range(NB):
                    for i, tile in enumerate(tiles):
                        last = pe.matmul(ps[:, 4, b:b + 1], tile[:, b * P:(b + 1) * P], ones[:, 0:1],
                                         start=(i == 0), stop=(i == len(tiles) - 1))
                last.then_inc(stat_ready.handle, 1)

            def spread(diag=DIAG):
                for h in range(2):
                    last = pe.matmul(ps[:, 5 + h, :], ones[:, :], st[:, diag, h * HALF:(h + 1) * HALF],
                                     start=True, stop=True)
                last.then_inc(spread_ready.handle, 1)

            def turn_values(stack, l, k0, tile, banks=(4, 5)):
                for g in range(2):
                    if k0 + g >= 2:
                        pe.wait_ge(vt_taken.handle, vt_taken.at(stack, l, k0 + g - 1))
                    for b in range(4):
                        last = pe.transpose(ps[:, banks[g], b * P:(b + 1) * P],
                                            tile[:, (4 * g + b) * P:(4 * g + b + 1) * P], ident)
                    last.then_inc(vt_ready.handle, 1)

            def attention(stack, l, kind, p0, g0, r0, query, key, value, width):
                maps = 2 if kind == "dif" else 1
                units = [(n, t) for n in range(NB) for t in range(4)]
                state = {"p": 0, "g": 0, "free": None}
                where = {}

                def scores(u):
                    n, t = units[u]
                    for j in range(maps):
                        q, base = query(t, j)
                        for piece in pieces_of(tiles_of_round(kind, n)):
                            i = state["p"]
                            if i >= 2:
                                pe.wait_ge(biased.handle, biased.at(stack, l, p0 + i - 1))
                            pe.matmul(ps[:, 4 + i % 2, 0:len(piece) * P],
                                      q[base:base + HD, n * P:(n + 1) * P],
                                      key(t, j)[base:base + HD, piece[0] * P:(piece[-1] + 1) * P],
                                      start=True, stop=True).then_inc(scored.handle, 1)
                            state["p"] += 1

                def bank_6_free():
                    if state["free"]:
                        ready, count = state["free"]
                        pe.wait_ge(ready.handle, ready.at(stack, l, count))

                def turn(u, i):
                    n, t = units[u]
                    tiles = tiles_of_round(kind, n)
                    groups = groups_of(tiles)
                    if i >= len(groups):
                        return
                    g = state["g"]
                    if i == 0:
                        if kind == "dif":
                            pe.wait_ge(mixed.handle, mixed.at(stack, l, u + 1))
                        else:
                            pe.wait_ge(expd.handle, expd.at(stack, l, (0 if kind == "gqa" else ag["maps"]) + u + 1))
                    bank_6_free()
                    e = exp_buffer(kind, maps * u)
                    for b, kt in enumerate(groups[i]):
                        c = (kt - tiles[0]) * P
                        last = pe.transpose(ps[:, 6, b * P:(b + 1) * P], e[:, c:c + P], ident)
                    last.then_inc(turned.handle, 1)
                    state["free"] = (turned_out, g0 + g + 1)
                    where.setdefault(u, []).append((g, groups[i]))
                    state["g"] += 1

                def weigh(u):
                    n, t = units[u]
                    tiles = tiles_of_round(kind, n)
                    if t == 0 and n >= 1:
                        pe.wait_ge(headed.handle, headed.at(stack, l, r0 + n))
                    for g, group in where[u]:
                        pe.wait_ge(turned_out.handle, turned_out.at(stack, l, g0 + g + 1))
                        for b, kt in enumerate(group):
                            last = pe.matmul(ps[:, 7, t * width:(t + 1) * width],
                                             turned_buffer(kind, g)[:, b * P:(b + 1) * P],
                                             value(t, kt), start=(kt == tiles[0]), stop=(kt == tiles[-1]))
                    if t == 3:
                        last.then_inc(weighted.handle, 1)

                def turn_back(n):
                    pe.wait_ge(headed.handle, headed.at(stack, l, r0 + n + 1))
                    bank_6_free()
                    for c in range(4 * width // P):
                        last = pe.transpose(ps[:, 6, c * P:(c + 1) * P],
                                            head_buffer(kind, n)[:, c * P:(c + 1) * P], ident)
                    last.then_inc(back.handle, 1)
                    state["free"] = (mixed_out, r0 + n + 1)

                def step(u):
                    if 2 <= u < len(units) + 2:
                        turn(u - 2, 0)
                    if u < len(units):
                        scores(u)
                    if 3 <= u < len(units) + 3:
                        weigh(u - 3)
                    if 2 <= u < len(units) + 2:
                        turn(u - 2, 1)
                    if u >= 8 and u % 4 == 0:
                        turn_back((u - 8) // 4)

                return [lambda u=u: step(u) for u in range(STEPS)]

            pe.wait_ge(const_in.handle, 16 * 3)

            with pe.Fori(0, DEPTH) as l:
                block_of = lambda n, **k: product(0, l, n, in_hi, in_lo, **k)

                def evacuated(n):
                    pe.wait_ge(taken.handle, taken.at(0, l, n))

                def swap_halves(i, slot):
                    for h in range(2):
                        if i >= 1:
                            pe.wait_ge(roped.handle, roped.at(0, l, 2 * i - 1 + h))
                        pe.matmul(ps[:, 6 + h, :], swap, st[:, slot, h * HALF:(h + 1) * HALF],
                                  start=True, stop=True).then_inc(swapped.handle, 1)

                block_of(0, before_chunk=chunk_wait(0, l, 0))
                pe.wait_ge(acc_ready.handle, acc_ready.at(0, l, 0))
                row_sums([st[:, ACC, :]])
                block_of(1)
                pe.wait_ge(diag_ready.handle, diag_ready.at(0, l, 1))
                spread()
                block_of(2)
                block_of(3)
                pe.wait_ge(fac_ready.handle, fac_ready.at(0, l, 1))
                evacuated(1)
                swap_halves(0, 19)
                block_of(4)
                evacuated(2)
                swap_halves(1, 20)
                block_of(5)
                evacuated(3)
                swap_halves(2, 17)
                block_of(6)
                evacuated(4)
                turn_values(0, l, 0, st[:, 8, :])
                block_of(7)
                pe.wait_ge(roped.handle, roped.at(0, l, 6))
                pe.wait_ge(vt_taken.handle, vt_taken.at(0, l, 2))
                steps = attention(0, l, "gqa", 0, 0, 0,
                                  lambda t, j: (st[:, 19 + t // 2, :], HD * (t % 2)),
                                  lambda t, j: st[:, 17, :],
                                  lambda t, kt: st[:, 18, kt * P + HD * (t % 2):kt * P + HD * (t % 2 + 1)], HD)
                block_of(8)
                for n in range(9, 18):
                    block_of(n, between=steps[4 * (n - 9):4 * (n - 8)])
                steps[36]()
                for n in range(18, 22):
                    block_of(n)
                pe.wait_ge(conv_ready.handle, conv_ready.at(0, l, 1))
                for h in range(2):
                    for c in range(2):
                        last = pe.matmul(ps[:, 4 + h, :], ones[:, :], st[:, 12 + c, h * HALF:(h + 1) * HALF],
                                         start=(c == 0), stop=(c == 1))
                last.then_inc(mean_ready.handle, 1)
                block_of(22)
                block_of(23)
                pe.wait_ge(lnsq_ready.handle, lnsq_ready.at(0, l, 2))
                row_sums([st[:, 14, :], st[:, 15, :]])
                block_of(24)
                block_of(25)
                pe.wait_ge(diag_ready.handle, diag_ready.at(0, l, 2))
                pe.wait_ge(mixed_out.handle, mixed_out.at(0, l, NB))
                spread(DIAG_LN)
                block_of(26)
                block_of(27)
                pe.wait_ge(fac_ready.handle, fac_ready.at(0, l, 2))
                evacuated(27)
                turn_values(0, l, 2, st[:, 8, :])
                evacuated(28)
                turn_values(0, l, 4, st[:, 9, :])
                wait = chunk_wait(0, l, 8)
                block_of(28, chunks=4, before_chunk=wait)
                block_of(29, chunks=4)
                pe.wait_ge(vt_taken.handle, vt_taken.at(0, l, 6))
                slots = (19, 20, 17, 18)
                steps = attention(0, l, "na", ag["pieces"], ag["groups"], NB,
                                  lambda t, j: (st[:, slots[t // 2], :], HD * (t % 2)),
                                  lambda t, j: st[:, slots[2 + t // 2], :],
                                  lambda t, kt: st[:, 21 + kt // 4, (kt % 4) * 256 + t * HD:(kt % 4) * 256 + (t + 1) * HD],
                                  HD)
                for n in range(30, 36):
                    block_of(n, chunks=4, between=steps[6 * (n - 30):6 * (n - 29)])
                steps[36]()
                block_of(36, chunks=4, k0=4, before_chunk=chunk_wait(0, l, 12))
                block_of(37, chunks=4, k0=4)
                products(0, l, 38, 44, chunks=4, k0=4)

            pe.wait_ge(acc_ready.handle, acc_ready.mid(0))
            row_sums([st[:, ACC, :]])
            pe.wait_ge(diag_ready.handle, diag_ready.mid(1))
            spread()

            with pe.Fori(0, DEPTH) as l:
                product(1, l, 0, in_hi, in_lo, before_chunk=chunk_wait(1, l, 0))
                pe.wait_ge(acc_ready.handle, acc_ready.at(1, l, 0))
                row_sums([st[:, ACC, :]])
                product(1, l, 1, in_hi, in_lo)
                pe.wait_ge(diag_ready.handle, diag_ready.at(1, l, 1))
                spread()
                products(1, l, 2, 10)
                pe.wait_ge(taken.handle, taken.at(1, l, 9))
                turn_values(1, l, 0, st[:, 8, :])
                product(1, l, 10, in_hi, in_lo)
                pe.wait_ge(taken.handle, taken.at(1, l, 10))
                turn_values(1, l, 2, st[:, 9, :])
                product(1, l, 11, in_hi, in_lo)
                pe.wait_ge(taken.handle, taken.at(1, l, 11))
                turn_values(1, l, 4, st[:, 8, :])
                product(1, l, 12, in_hi, in_lo)
                pe.wait_ge(taken.handle, taken.at(1, l, 12))
                turn_values(1, l, 6, st[:, 9, :])

                def r_scores(n):
                    if n >= 1:
                        pe.wait_ge(r_decayed.handle, r_decayed.at(1, l, n))
                        pe.wait_ge(r_state.handle, r_state.at(1, l, n))
                    else:
                        pe.wait_ge(vt_taken.handle, vt_taken.at(1, l, 8))
                    for c in range(2):
                        pe.transpose(ps[:, 4, 256 + c * P:256 + (c + 1) * P], st[:, 12 + c, n * P:(n + 1) * P], ident)
                    for t in range(4):
                        b = HD * (t % 2)
                        last = pe.matmul(ps[:, 4 + t % 2, (t // 2) * P:(t // 2 + 1) * P], st[b:b + HD, 12 + t // 2, n * P:(n + 1) * P],
                                         st[b:b + HD, 10 + t // 2, n * P:(n + 1) * P], start=True, stop=True)
                    last.then_inc(r_scored.handle, 1)

                def r_sums(n):
                    pe.wait_ge(r_decayed.handle, r_decayed.at(1, l, n + 1))
                    if n >= 1:
                        pe.wait_ge(r_state.handle, r_state.at(1, l, n))
                        pe.wait_ge(r_headed.handle, r_headed.at(1, l, n))
                    for c in range(2):
                        pe.matmul(ps[:, 6, 2 * c * P:2 * (c + 1) * P], st[:, 22, 256 + c * P:256 + (c + 1) * P],
                                  state_of(n)[:, 2 * c * P:2 * (c + 1) * P],
                                  start=(c == 0), stop=False, skip_group_check=True)
                    for t in range(4):
                        last = pe.matmul(ps[:, 6, t * P:(t + 1) * P], st[:, 9, GQA_ORDER[t] * P:(GQA_ORDER[t] + 1) * P],
                                         rv(n, t), start=False, stop=(t == 3), skip_group_check=True)
                    if n < NB - 1:
                        for t in range(4):
                            b = HD * (t % 2)
                            last = pe.matmul(ps[b:b + HD, 5, 256 + (t // 2) * P:256 + (t // 2 + 1) * P],
                                             st[:, 22, t * HD:(t + 1) * HD], rv(n, t), start=True, stop=True)
                    last.then_inc(r_summed.handle, 1)

                def r_turn_back(n):
                    pe.wait_ge(r_headed.handle, r_headed.at(1, l, n + 1))
                    if n >= 1:
                        pe.wait_ge(r_out.handle, r_out.at(1, l, n))
                    for t in range(4):
                        last = pe.transpose(ps[:, 7, t * P:(t + 1) * P], half[:, t * P:(t + 1) * P], ident)
                    last.then_inc(r_back.handle, 1)

                for n in range(NB + 2):
                    if n >= 1:
                        product(1, l, 12 + n, in_hi, in_lo, between=[lambda: r_sums(n - 1)] if n <= NB else [])
                    if n < NB:
                        r_scores(n)
                    if n >= 2:
                        r_turn_back(n - 2)
                pe.wait_ge(taken.handle, taken.at(1, l, 21))
                turn_values(1, l, 8, st[:, 8, :])
                product(1, l, 22, in_hi, in_lo)
                pe.wait_ge(taken.handle, taken.at(1, l, 22))
                turn_values(1, l, 10, st[:, 9, :])
                product(1, l, 23, in_hi, in_lo)
                pe.wait_ge(taken.handle, taken.at(1, l, 23))
                turn_values(1, l, 12, st[:, 14, :])
                pe.wait_ge(taken.handle, taken.at(1, l, 24))
                turn_values(1, l, 14, st[:, 15, :])
                product(1, l, 24, in_hi, in_lo, chunks=4, before_chunk=chunk_wait(1, l, 8))
                product(1, l, 25, in_hi, in_lo, chunks=4)
                pe.wait_ge(vt_taken.handle, vt_taken.at(1, l, 16))
                pe.wait_ge(r_out.handle, r_out.at(1, l, NB))
                steps = attention(1, l, "dif", 0, 0, 0,
                                  lambda t, j: (st[:, 4 + t, :], HD * j),
                                  lambda t, j: st[:, 18 + t, :],
                                  lambda t, kt: st[:, 10 + kt // 2, (kt % 2) * HALF + t * P:(kt % 2) * HALF + (t + 1) * P], P)
                for n in range(26, 32):
                    product(1, l, n, in_hi, in_lo, chunks=4, between=steps[6 * (n - 26):6 * (n - 25)])
                steps[36]()
                product(1, l, 32, in_hi, in_lo, chunks=4, k0=4, before_chunk=chunk_wait(1, l, 12))
                product(1, l, 33, in_hi, in_lo, chunks=4, k0=4)
                products(1, l, 34, 40, chunks=4, k0=4)
                n = 40
                chunk0 = 0
                for group in FFN_GROUPS:
                    if chunk0 == 0:
                        product(1, l, n, in_hi, in_lo, before_chunk=chunk_wait(1, l, 16))
                        pe.wait_ge(acc_ready.handle, acc_ready.at(1, l, 1))
                        row_sums([st[:, ACC, :]])
                        product(1, l, n + 1, in_hi, in_lo)
                        pe.wait_ge(diag_ready.handle, diag_ready.at(1, l, 2))
                        spread()
                        products(1, l, n + 2, n + 2 * group)
                    else:
                        products(1, l, n, n + 2 * group)
                    n += 2 * group
                    product(1, l, n, hid_hi, hid_lo, chunks=group,
                            before_chunk=chunk_wait(1, l, chunk0, hid_lo_ready))
                    product(1, l, n + 1, hid_hi, hid_lo, chunks=group)
                    products(1, l, n + 2, n + KC, hid_hi, hid_lo, chunks=group)
                    n += KC
                    chunk0 += group

            pe.wait_ge(acc_ready.handle, acc_ready.end())
            row_sums([st[:, ACC, :]])
            pe.wait_ge(diag_ready.handle, diag_ready.end(1))
            spread()

        @block.scalar
        def _(act):
            def split_hi(stack, source, scale=None, chunks=range(KC)):
                for c in chunks:
                    s = scale(c) if scale else 1.0
                    act.activation(in_hi[:, c, :], source(c), ACT.Copy if scale is None else ACT.Identity,
                                   scale=s).then_inc(hi_ready.handle, 1)

            def squares(c):
                act.activation(st[:, ACC if c == 0 else SQ[c % 2], :], xt[:, c, :], ACT.Square
                               ).then_inc(squared.handle, 1)

            def take_factor(wait, slot=None):
                act.wait_ge(spread_ready.handle, wait)
                to = rfac[:, :] if slot is None else st[:, slot, :]
                act.activation(to, ps[:, 5:7, :], ACT.Copy).then_inc(fac_ready.handle, 1)

            def take_values(stack, l, k0, to):
                for g in range(2):
                    act.wait_ge(vt_ready.handle, vt_ready.at(stack, l, k0 + g + 1))
                    act.activation(to(g), ps[:, 4 + g, :].rearrange("p (b c) -> p b c", b=4), ACT.Copy
                                   ).then_inc(vt_taken.handle, 1)

            def attention(stack, l, kind, p0, g0, r0):
                maps = 2 if kind == "dif" else 1
                units = [(n, t) for n in range(NB) for t in range(4)]
                state = {"g": 0, "p": 0}

                def exps(u):
                    n, t = units[u]
                    tiles = tiles_of_round(kind, n)
                    for j in range(maps):
                        m = maps * u + j
                        state["p"] += len(pieces_of(tiles))
                        act.wait_ge(biased.handle, biased.at(stack, l, p0 + state["p"]))
                        e = exp_buffer(kind, m)[:, 0:len(tiles) * P]
                        i = maps * t + j
                        act.activation(e, e, ACT.Exp, bias=negm[:, n % 2, i:i + 1], scale=-1.0,
                                       accum_out=lsum[:, n % 2, i:i + 1]).then_inc(expd.handle, 1)
                    if kind == "gqa" and t == 3:
                        act.wait_ge(sink_ready.handle, sink_ready.at(stack, l, n + 1))
                        act.activation(esink, comb, ACT.Exp).then_inc(sink_exp.handle, 1)

                def groups(u):
                    n, t = units[u]
                    for group in groups_of(tiles_of_round(kind, n)):
                        g = state["g"]
                        act.wait_ge(turned.handle, turned.at(stack, l, g0 + g + 1))
                        w = len(group) * P
                        act.activation(turned_buffer(kind, g)[:, 0:w], ps[:, 6, 0:w], ACT.Copy
                                       ).then_inc(turned_out.handle, 1)
                        state["g"] += 1

                def head_squares(n):
                    act.wait_ge(weighted.handle, weighted.at(stack, l, r0 + n + 1))
                    for t in range(4):
                        last = act.activation(st[:, 15, t * P:(t + 1) * P], ps[:, 7, t * P:(t + 1) * P], ACT.Square,
                                              scale=rinv[:, n % 2, 2 * t:2 * t + 1], accum_out=ssq[:, t:t + 1])
                    last.then_inc(head_sq.handle, 1)

                def step(u):
                    if 2 <= u < len(units) + 2:
                        groups(u - 2)
                    if u < len(units):
                        exps(u)
                    if kind == "dif" and u >= 6 and (u - 6) % 4 == 0 and (u - 6) // 4 < NB:
                        head_squares((u - 6) // 4)

                return [lambda u=u: step(u) for u in range(STEPS)]

            for c in range(KC):
                act.dma_start(xt[:, c, :], x_in[c, :, :]).then_inc(x_in_sem[c].handle, 16)
                if c == 0:
                    act.dma_start(par[:, 0:NPAR], par_in).then_inc(const_in.handle, 16)
                    act.dma_start(square[:, 0:2, :], c_square.rearrange("a p n -> p a n")).then_inc(const_in.handle, 16)
                    act.dma_start(mask_gqa[:, :], c_gqa).then_inc(const_in.handle, 16)
                    act.dma_start(st[:, 0, 0:DEPTH * 4 * HD], lam_in).then_inc(lam_sem.handle, 16)
            for c in range(KC):
                act.wait_ge(x_in_sem[c].handle, 16)
                if c >= 3:
                    act.wait_ge(dve_own, c - 2)
                squares(c)
            act.wait_ge(lam_exp.handle, 1)
            act.activation(small[:, 4:8], small[:, 0:4], ACT.Exp).then_inc(lam_exp.handle, 1)

            with act.Fori(0, DEPTH) as l:
                act.wait_ge(cur_ready.handle, cur_ready.at(0, l, 1))
                split_hi(0, lambda c: xt[:, c, :], lambda c: cur[:, C_NORM + c:C_NORM + c + 1])
                take_factor(spread_ready.at(0, l, 1))
                act.dma_start(st[:, 21:23, :], c_rope.rearrange("a p n -> p a n")).then_inc(rope_in.handle, 32)
                for i in range(2):
                    act.wait_ge(taken.handle, taken.at(0, l, 4 + 2 * i + 1))
                    act.activation(st[:, (9, 11)[i], :], st[:, (9, 11)[i], :], ACT.Tanh, scale=0.5
                                   ).then_inc(tanh_ready.handle, 1)
                    if i == 0:
                        v3 = lambda slot, g: st[:, slot, g * HALF:(g + 1) * HALF].rearrange("p (b c) -> p b c", b=4)
                        take_values(0, l, 0, lambda g: v3(18, g))
                steps = attention(0, l, "gqa", 0, 0, 0)
                for n in range(8, 18):
                    if n > 8:
                        for work in steps[4 * (n - 9):4 * (n - 8)]:
                            work()
                    if n < 16:
                        act.wait_ge(taken.handle, taken.at(0, l, n + 1))
                        act.activation(st[:, 10 + n % 2, :], st[:, 8 + n % 2, :], ACT.Tanh, scale=0.5
                                       ).then_inc(tanh_ready.handle, 1)
                steps[36]()
                for c in range(2):
                    act.wait_ge(centred.handle, centred.at(0, l, c + 1))
                    act.activation(st[:, 14 + c, :], st[:, 12 + c, :], ACT.Square).then_inc(lnsq_ready.handle, 1)
                take_factor(spread_ready.at(0, l, 2), slot=10)
                for c in range(2):
                    act.wait_ge(normed.handle, normed.at(0, l, c + 1))
                    act.activation(st[:, 12 + c, :], st[:, 12 + c, :], ACT.Identity,
                                   scale=cur[:, C_LNG + c:C_LNG + c + 1],
                                   bias=cur[:, C_LNB + c:C_LNB + c + 1]).then_inc(act_own, 1)
                    act.wait_ge(act_own, l * 2 + (c + 1))
                    act.activation(st[:, 14 + c, :], st[:, 12 + c, :], ACT.Tanh, scale=0.5
                                   ).then_inc(lnact_ready.handle, 1)
                act.wait_ge(done.handle, done.at(0, l, 28))
                raw = rpb_in[bass.ds(l, 1), :, :].rearrange("a g c -> (a g) c")[:, GRID_W - 1:GRID_W - 1 + GRID_W * (SKEW - 1)
                                                                                ].rearrange("g (q s) -> q g s", s=SKEW - 1)
                table = flat(space_lo, 0, 4)[:, 0:4 * ND * GRID_W].rearrange("p (g c) -> p g c", c=GRID_W)
                for to, of in ((table[0:64], raw), (table[64:128, 1:4 * ND], raw[:, 0:4 * ND - 1]),
                               (table[64:128, 0:1], raw[:, 0:1])):
                    act.dma_start(to, of[:, :, 0:GRID_W]).then_inc(bias_in.handle, 16)
                act.wait_ge(conv_out.handle, conv_out.at(0, l, 2))
                act.dma_start(st[:, 15, 0:11 * GRID_W], c_na).then_inc(bias_in.handle, 16)
                split_hi(0, lambda c: st[:, c, :], chunks=range(4))
                dv3 = lambda c, g: st[:, 21 + g, :].rearrange("p (b x) -> p b x", b=4)[:, :, c * P:(c + 1) * P]
                take_values(0, l, 2, lambda g: dv3(0, g))
                take_values(0, l, 4, lambda g: dv3(1, g))
                for work in attention(0, l, "na", ag["pieces"], ag["groups"], NB):
                    work()
                act.wait_ge(mixed_out.handle, mixed_out.at(0, l, 2 * NB))
                split_hi(0, lambda c: st[:, c, :], chunks=range(4, 8))
                for c in range(KC):
                    act.wait_ge(taken.handle, taken.at(0, l, 36 + c + 1))
                    squares(c)

            take_factor(spread_ready.mid(1))
            for c in range(KC):
                act.wait_ge(x_scaled.handle, c + 1)
                squares(c)

            with act.Fori(0, DEPTH) as l:
                act.wait_ge(cur_ready.handle, cur_ready.at(1, l, 1))
                split_hi(1, lambda c: xt[:, c, :], lambda c: cur[:, C_AN + c:C_AN + c + 1])
                take_factor(spread_ready.at(1, l, 1))
                for k in range(4):
                    act.wait_ge(taken.handle, taken.at(1, l, k + 1))
                    act.activation(st[:, 10 + k % 2, :], st[:, 8 + k % 2, :], ACT.Tanh, scale=0.5
                                   ).then_inc(tanh_ready.handle, 1)
                vals = lambda slot, g, c: (st[:, slot + 2 * g:slot + 2 * g + 2, :]
                                           .rearrange("p a (b x) -> p (a b) x", b=2)[:, :, c * P:(c + 1) * P])
                for c in range(4):
                    take_values(1, l, 2 * c, lambda g: vals(14, g, c))
                    if c == 2:
                        act.dma_start(st[:, 8, :], c_ret).then_inc(retc_in.handle, 16)
                unread = mask_gqa[:, :].bitcast(mybir.dt.bfloat16)
                for n in range(NB):
                    act.wait_ge(r_summed.handle, r_summed.at(1, l, n + 1))
                    for t in range(4):
                        last = act.activation(unread[:, t * P:(t + 1) * P], ps[:, 6, t * P:(t + 1) * P], ACT.Square,
                                              accum_out=ssq[:, t:t + 1])
                    last.then_inc(r_squared.handle, 1)
                for c in (0, 1):
                    take_values(1, l, 8 + 2 * c, lambda g: vals(10, g, c))
                act.wait_ge(done.handle, done.at(1, l, 24))
                act.dma_start(space_lo[:, :, :], c_alibi.rearrange("h p n -> p h n")).then_inc(alibi_in.handle, 16)
                act.wait_ge(r_out.handle, r_out.at(1, l, NB))
                split_hi(1, lambda c: st[:, c, :], chunks=range(4))
                for c in (2, 3):
                    take_values(1, l, 8 + 2 * c, lambda g: vals(10, g, c))
                for work in attention(1, l, "dif", 0, 0, 0):
                    work()
                act.wait_ge(mixed_out.handle, mixed_out.at(1, l, NB))
                split_hi(1, lambda c: st[:, c, :], chunks=range(4, 8))
                for c in range(KC):
                    act.wait_ge(taken.handle, taken.at(1, l, 32 + c + 1))
                    squares(c)
                split_hi(1, lambda c: xt[:, c, :], lambda c: cur[:, C_FN + c:C_FN + c + 1])
                take_factor(spread_ready.at(1, l, 2))
                n, chunk0 = 40, 0
                for group in FFN_GROUPS:
                    for c in range(group):
                        act.wait_ge(taken.handle, taken.at(1, l, n + 2 * c + 1))
                        act.activation(st[:, 18 + c % 2, :], st[:, 16 + c % 2, :], ACT.Tanh, scale=0.5
                                       ).then_inc(tanh_ready.handle, 1)
                        act.wait_ge(gated.handle, gated.at(1, l, chunk0 + c + 1))
                        act.activation(hid_hi[:, c, :], st[:, 16 + c % 2, :], ACT.Copy
                                       ).then_inc(hid_hi_ready.handle, 1)
                    n += 2 * group + KC
                    chunk0 += group
                for c in range(KC):
                    act.wait_ge(taken.handle, taken.at(1, l, BLOCKS[1] - KC + c + 1))
                    squares(c)

            take_factor(spread_ready.end(1))
            for c in range(KC):
                act.wait_ge(out_ready.handle, c + 1)
                act.dma_start(out[c, :, :], xt[:, c, :]).then_inc(out_sem.handle, 16)
            act.wait_ge(out_sem.handle, 16 * KC)

        @block.vector
        def _(dve):
            own = Chain(dve, dve_own)
            link = own.link

            def evacuate(stack, l, n, to):
                j = n % 2
                dve.wait_ge(done.handle, done.at(stack, l, n + 1))
                dve.tensor_tensor(to, ps[:, 2 * j:2 * j + 2, :].rearrange("p a b -> p (a b)"), rfac[:, :], ALU.mult
                                  ).then_inc(taken.handle, 1)

            def add_to_x(stack, l, n, c):
                dve.wait_ge(done.handle, done.at(stack, l, n + 1))
                last = dve.tensor_tensor(xt[:, c, :], xt[:, c, :],
                                         flat(ps, 2 * (n % 2), 2), ALU.add)
                last.then_inc(taken.handle, 1)

            def split_lo(stack, l, base, source, scale=None, chunks=range(KC)):
                for c in chunks:
                    dve.wait_ge(hi_ready.handle, hi_ready.at(stack, l, base + c + 1))
                    if scale:
                        i = dve.scalar_tensor_tensor(in_lo[:, c, :], source(c), scale(c), in_hi[:, c, :].bitcast(F32),
                                                     ALU.mult, ALU.subtract)
                    else:
                        i = dve.tensor_tensor(in_lo[:, c, :], source(c), in_hi[:, c, :].bitcast(F32), ALU.subtract)
                    i.then_inc(lo_ready.handle, 1)

            def sum_squares(wait, c):
                dve.wait_ge(squared.handle, wait)
                i = dve.tensor_tensor(st[:, ACC, :], st[:, ACC, :], st[:, SQ[c % 2], :], ALU.add)
                if c == KC - 1:
                    i.then_inc(acc_ready.handle, 1)
                else:
                    link(i)

            def rsqrt(x, y, t):
                link(dve.tensor_scalar(t.bitcast(I32), x.bitcast(I32), 1, None, ALU.logical_shift_right))
                link(dve.tensor_scalar(y.bitcast(I32), t.bitcast(I32), -1.0, float(0x5F3759DF), ALU.mult, ALU.add))
                for _ in range(3):
                    link(dve.tensor_tensor(t, y, y, ALU.mult))
                    link(dve.scalar_tensor_tensor(t, t, -0.5, x, ALU.mult, ALU.mult))
                    link(dve.scalar_tensor_tensor(y, t, 1.5, y, ALU.add, ALU.mult))

            def row_factor(wait, count, diag=DIAG):
                dve.wait_ge(stat_ready.handle, wait)
                link(dve.tensor_scalar(stat, ps[:, 4, 0:8], 1.0 / count, EPS, ALU.mult, ALU.add))
                rsqrt(stat, root, tmp)
                dve.tensor_tensor(st[:, diag, :].rearrange("p (b c) -> p b c", b=NB),
                                  ident.unsqueeze(1).broadcast_to([P, NB, P]),
                                  root.unsqueeze(2).broadcast_to([P, NB, P]), ALU.mult).then_inc(diag_ready.handle, 1)

            def attention(stack, l, kind, p0, g0, r0, bias, finish):
                maps = 2 if kind == "dif" else 1
                m0 = ag["maps"] if kind == "na" else 0
                width = P if kind == "dif" else HD
                units = [(n, t) for n in range(NB) for t in range(4)]
                state = {"p": 0}

                def scores(u):
                    n, t = units[u]
                    tiles = tiles_of_round(kind, n)
                    for j in range(maps):
                        m = maps * u + j
                        i = maps * t + j
                        first = cur[:, C_SINK + t:C_SINK + t + 1] if kind == "gqa" else 3.0e38
                        for piece in pieces_of(tiles):
                            dve.wait_ge(scored.handle, scored.at(stack, l, p0 + state["p"] + 1))
                            if piece[0] > tiles[0]:
                                dve.wait_ge(biased.handle, biased.at(stack, l, p0 + state["p"]))
                            elif m >= exp_buffers(kind):
                                turned_units = (m - exp_buffers(kind)) // maps + 1
                                gi = sum(len(groups_of(tiles_of_round(kind, units[v][0]))) for v in range(turned_units))
                                dve.wait_ge(turned.handle, turned.at(stack, l, g0 + gi))
                            dve.sem_inc(dve_step)
                            a, w = (piece[0] - tiles[0]) * P, len(piece) * P
                            dve.tensor_tensor_reduce(exp_buffer(kind, m)[:, a:a + w], ps[:, 4 + state["p"] % 2, 0:w],
                                                     bias(n, t)[:, a:a + w], -SCALE, first,
                                                     ALU.add, ALU.min, negm[:, n % 2, i:i + 1]).then_inc(biased.handle, 1)
                            first = negm[:, n % 2, i:i + 1]
                            state["p"] += 1
                    if kind == "gqa" and t == 3:
                        dve.wait_ge(biased.handle, biased.at(stack, l, p0 + state["p"]))
                        dve.tensor_tensor(comb, negm[:, n % 2, 0:4], cur[:, C_SINK:C_SINK + 4], ALU.subtract
                                          ).then_inc(sink_ready.handle, 1)

                def mix(u):
                    n, t = units[u]
                    cols = (n + 1) * P
                    dve.wait_ge(expd.handle, expd.at(stack, l, m0 + 2 * u + 2))
                    r = rinv[:, n % 2, :]
                    link(dve.reciprocal(r[:, 2 * t:2 * t + 2], lsum[:, n % 2, 2 * t:2 * t + 2]))
                    link(dve.scalar_tensor_tensor(comb[:, t:t + 1], lsum[:, n % 2, 2 * t:2 * t + 1],
                                                  cur[:, C_NLAM:C_NLAM + 1], r[:, 2 * t + 1:2 * t + 2],
                                                  ALU.mult, ALU.mult))
                    e0, e1 = (exp_buffer(kind, 2 * u + j)[:, 0:cols] for j in range(2))
                    dve.scalar_tensor_tensor(e0, e1, comb[:, t:t + 1], e0, ALU.mult, ALU.add
                                             ).then_inc(mixed.handle, 1)

                def heads(n):
                    if kind == "dif":
                        dve.wait_ge(head_sq.handle, head_sq.at(stack, l, n + 1))
                        link(dve.tensor_scalar(stat[:, 0:4], ssq[:, 0:4], 1.0 / P, EPS, ALU.mult, ALU.add))
                        rsqrt(stat[:, 0:4], root[:, 0:4], tmp[:, 0:4])
                        link(dve.tensor_tensor(factor, root[:, 0:4],
                                               rinv[:, n % 2, :].rearrange("p (a b) -> p a b", b=2)[:, :, 0], ALU.mult))
                    else:
                        dve.wait_ge(expd.handle, expd.at(stack, l, m0 + 4 * n + 4))
                        total = lsum[:, n % 2, 0:4]
                        if kind == "gqa":
                            dve.wait_ge(sink_exp.handle, sink_exp.at(stack, l, n + 1))
                            link(dve.tensor_tensor(total, total, esink, ALU.add))
                        link(dve.reciprocal(factor, total))
                        dve.wait_ge(weighted.handle, weighted.at(stack, l, r0 + n + 1))
                    if n >= 2:
                        dve.wait_ge(back.handle, back.at(stack, l, r0 + n - 1))
                    dve.tensor_tensor(head_buffer(kind, n)[:, 0:4 * width].rearrange("p (t e) -> p t e", t=4),
                                      ps[:, 7, 0:4 * width].rearrange("p (t e) -> p t e", t=4),
                                      factor.unsqueeze(2).broadcast_to([P, 4, width]), ALU.mult
                                      ).then_inc(headed.handle, 1)

                def step(u):
                    if u < len(units):
                        scores(u)
                    if kind == "dif" and 1 <= u < len(units) + 1:
                        mix(u - 1)
                    if u >= 6 and (u - 6) % 4 == 0 and (u - 6) // 4 < NB:
                        heads((u - 6) // 4)
                    if u >= 8 and u % 4 == 0:
                        n = (u - 8) // 4
                        dve.wait_ge(back.handle, back.at(stack, l, r0 + n + 1))
                        finish(n).then_inc(mixed_out.handle, 1)

                return [lambda u=u: step(u) for u in range(STEPS)]

            dve.engine_nop().then_inc(taken.handle, 2)
            for c in range(1, KC):
                sum_squares(c + 1, c)
            dve.wait_ge(const_in.handle, 16 * 3)
            dve.wait_ge(lam_sem.handle, 16)
            own.restart()
            lam = st[:, 0, 0:DEPTH * 4 * HD].rearrange("p (l v d) -> p l v d", l=DEPTH, v=4)
            for l in range(DEPTH):
                for i in range(2):
                    k = 2 * l + i
                    link(dve.tensor_tensor_reduce(st[:, 1, k * HD:(k + 1) * HD], lam[:, l, 2 * i, :], lam[:, l, 2 * i + 1, :],
                                                  1.0, 0.0, ALU.mult, ALU.add, small[:, k:k + 1]))
            dve.engine_nop().then_inc(lam_exp.handle, 1)
            dve.wait_ge(lam_exp.handle, 2)
            for l in range(DEPTH):
                lam_init = 0.8 - 0.6 * float(np.exp(-0.3 * l))
                o = O2 + l * W2
                link(dve.tensor_tensor(tmp[:, 0:1], small[:, 4 + 2 * l + 1:4 + 2 * l + 2], small[:, 4 + 2 * l:4 + 2 * l + 1],
                                       ALU.subtract))
                link(dve.tensor_scalar(par[:, o + C_NLAM:o + C_NLAM + 1], tmp[:, 0:1], -lam_init, None, ALU.add))
                link(dve.tensor_scalar(par[:, o + C_RN:o + C_RN + 1], par[:, o + C_RN:o + C_RN + 1], 0.5, None, ALU.mult))
                link(dve.tensor_scalar(par[:, o + C_DN:o + C_DN + 1], par[:, o + C_DN:o + C_DN + 1], 1.0 - lam_init, None,
                                       ALU.mult))
                o = l * W1 + C_SINK
                link(dve.tensor_scalar(par[:, o:o + 4], par[:, o:o + 4], -1.0, None, ALU.mult))

            with dve.Fori(0, DEPTH) as l:
                own.restart()
                dve.tensor_copy(cur[:, :], par[:, bass.ds(l * W1, W1)]).then_inc(cur_ready.handle, 1)
                split_lo(0, l, 0, lambda c: xt[:, c, :], lambda c: cur[:, C_NORM + c:C_NORM + c + 1])
                row_factor(stat_ready.at(0, l, 1), D)
                dve.wait_ge(fac_ready.handle, fac_ready.at(0, l, 1))

                def rotate(i, slot):
                    for h in range(2):
                        dve.wait_ge(swapped.handle, swapped.at(0, l, 2 * i + h + 1))
                        a = slice(h * HALF, (h + 1) * HALF)
                        link(dve.tensor_tensor(half[:, :], ps[:, 6 + h, :], st[:, 22, a], ALU.mult))
                        link(dve.tensor_tensor(st[:, slot, a], st[:, slot, a], st[:, 21, a], ALU.mult))
                        dve.tensor_tensor(st[:, slot, a], st[:, slot, a], half[:, :], ALU.add).then_inc(roped.handle, 1)
                        dve.wait_ge(roped.handle, roped.at(0, l, 2 * i + h + 1))

                def gate_input(i):
                    dve.wait_ge(tanh_ready.handle, tanh_ready.at(0, l, i + 1))
                    dve.wait_ge(taken.handle, taken.at(0, l, 4 + 2 * i + 2))
                    gate_slot, input_slot = ((9, 10), (11, 8))[i]
                    link(dve.scalar_tensor_tensor(st[:, 14 + i, :], st[:, gate_slot, :], 1.0, st[:, input_slot, :],
                                                  ALU.add, ALU.mult))

                def tap(acc, source, weight, d, first):
                    a, b = max(0, -d), S - max(0, d)
                    if first:
                        return dve.tensor_scalar(acc, source, weight, None, ALU.mult)
                    return dve.scalar_tensor_tensor(acc[:, a:b], source[:, a + d:b + d], weight, acc[:, a:b],
                                                    ALU.mult, ALU.add)

                mid = TAPS_A // 2
                order = [mid] + [k for k in range(TAPS_A) if k != mid]
                taps = [(k, c) for k in order for c in range(2)]

                def conv_taps(count):
                    for _ in range(min(count, len(taps))):
                        k, c = taps.pop(0)
                        w = cur[:, C_CAW + TAPS_A * c + k:C_CAW + TAPS_A * c + k + 1]
                        link(tap(st[:, 12 + c, :], st[:, 14 + c, :], w, k - mid, k == mid))

                def gate(k):
                    dve.wait_ge(tanh_ready.handle, tanh_ready.at(0, l, 2 + k + 1))
                    link(dve.scalar_tensor_tensor(st[:, (4, 5, 0, 1, 2, 3, 6, 7)[k], :], st[:, 10 + k % 2, :], 1.0,
                                                  st[:, 8 + k % 2, :],
                                                  ALU.add, ALU.mult))

                def back_to_chunks(first):
                    def finish(n):
                        y = st[:, first:first + 2, n * P:(n + 1) * P]
                        return dve.scalar_tensor_tensor(y, ps[:, 6, 0:2 * P].rearrange("p (c q) -> p c q", c=2), 0.5, y,
                                                        ALU.mult, ALU.mult)
                    return finish

                def gated_conv(i, stage):
                    cx, y = st[:, 10, :], st[:, 11, :]
                    w = lambda k: cur[:, C_CBW + TAPS_B * i + k:C_CBW + TAPS_B * i + k + 1]
                    if stage == 0:
                        dve.wait_ge(taken.handle, taken.at(0, l, 18 + 3 * i))
                        link(dve.tensor_tensor(cx, st[:, 8, :], st[:, 9, :], ALU.mult))
                        link(tap(y, cx, w(1), 0, True))
                        link(tap(y, cx, w(0), -1, False))
                        link(tap(y, cx, w(2), 1, False))
                    else:
                        dve.wait_ge(taken.handle, taken.at(0, l, 19 + 3 * i))
                        link(dve.tensor_tensor(y, y, st[:, 8, :], ALU.mult))
                        link(dve.scalar_tensor_tensor(st[:, 2 + i, :], y, 0.5, st[:, 2 + i, :], ALU.mult, ALU.mult))

                evacuate(0, l, 0, st[:, 19, :])
                evacuate(0, l, 1, st[:, 20, :])
                evacuate(0, l, 2, st[:, 17, :])
                evacuate(0, l, 3, st[:, 8, :])
                dve.wait_ge(rope_in.handle, rope_in.at(0, l, 32))
                rotate(0, 19)
                evacuate(0, l, 4, st[:, 9, :])
                rotate(1, 20)
                evacuate(0, l, 5, st[:, 10, :])
                rotate(2, 17)
                evacuate(0, l, 6, st[:, 11, :])
                gate_input(0)
                dve.wait_ge(vt_ready.handle, vt_ready.at(0, l, 2))
                evacuate(0, l, 7, st[:, 8, :])
                gate_input(1)
                steps = attention(0, l, "gqa", 0, 0, 0,
                                  lambda n, t: mask_gqa[:, (tiles_of_round("gqa", n)[0] - n + 1) * P:
                                                        (tiles_of_round("gqa", n)[-1] - n + 2) * P],
                                  back_to_chunks(4))
                conv_taps(4)
                evacuate(0, l, 8, st[:, 8, :])
                for n in range(9, 18):
                    for i, work in enumerate(steps[4 * (n - 9):4 * (n - 8)]):
                        work()
                        conv_taps(1)
                        if i == 1 and n <= 16:
                            gate(n - 9)
                    evacuate(0, l, n, st[:, 8 + n % 2, :])
                steps[36]()
                gated_conv(0, 0)
                conv_taps(3)
                evacuate(0, l, 18, st[:, 8, :])
                gated_conv(0, 1)
                conv_taps(6)
                evacuate(0, l, 19, st[:, 8, :])
                conv_taps(7)
                evacuate(0, l, 20, st[:, 9, :])
                conv_taps(len(taps))
                for c in range(2):
                    last = dve.tensor_scalar(st[:, 12 + c, :], st[:, 12 + c, :], 0.5, cur[:, C_CAB + c:C_CAB + c + 1],
                                             ALU.mult, ALU.add)
                last.then_inc(conv_ready.handle, 1)
                gated_conv(1, 0)
                evacuate(0, l, 21, st[:, 8, :])
                gated_conv(1, 1)
                evacuate(0, l, 22, st[:, 19, :])
                dve.wait_ge(mean_ready.handle, mean_ready.at(0, l, 1))
                for c in range(2):
                    dve.scalar_tensor_tensor(st[:, 12 + c, :], flat(ps, 4, 2), -1.0 / (2 * P),
                                             st[:, 12 + c, :], ALU.mult, ALU.add).then_inc(centred.handle, 1)
                evacuate(0, l, 23, st[:, 20, :])
                row_factor(stat_ready.at(0, l, 2), 2 * P, DIAG_LN)
                evacuate(0, l, 24, st[:, 17, :])
                evacuate(0, l, 25, st[:, 18, :])
                evacuate(0, l, 26, st[:, 8, :])
                dve.wait_ge(fac_ready.handle, fac_ready.at(0, l, 2))
                for c in range(2):
                    dve.tensor_tensor(st[:, 12 + c, :], st[:, 12 + c, :], st[:, 10, :], ALU.mult
                                      ).then_inc(normed.handle, 1)
                evacuate(0, l, 27, st[:, 9, :])
                for c in range(2):
                    dve.wait_ge(lnact_ready.handle, lnact_ready.at(0, l, c + 1))
                    link(dve.scalar_tensor_tensor(st[:, 12 + c, :], st[:, 14 + c, :], 1.0, st[:, 12 + c, :],
                                                  ALU.add, ALU.mult))
                    dve.scalar_tensor_tensor(st[:, c, :], st[:, 12 + c, :], 0.25, st[:, c, :], ALU.mult, ALU.mult
                                             ).then_inc(conv_out.handle, 1)
                dve.wait_ge(conv_out.handle, conv_out.at(0, l, 2))
                split_lo(0, l, 8, lambda c: st[:, c, :], chunks=range(4))

                dve.wait_ge(bias_in.handle, bias_in.at(0, l, 64))
                table = flat(space_lo, 0, 4)[:, 0:4 * ND * GRID_W]
                inner = flat(st, 12, 3)[:, 0:4 * 10 * GRID_W]
                by_row = table.rearrange("p (g c) -> p g c", c=GRID_W)
                link(dve.scalar_tensor_tensor(by_row, by_row, 1.0 / SCALE,
                                              st[:, 15, 0:GRID_W].unsqueeze(1).broadcast_to([P, 4 * ND, GRID_W]),
                                              ALU.mult, ALU.add))
                table_h = table.rearrange("p (h r) -> p h r", h=4)
                inner_h = inner.rearrange("p (h r) -> p h r", h=4)
                dve.tensor_tensor(inner_h, table_h[:, :, 3 * GRID_W:13 * GRID_W],
                                  st[:, 15, GRID_W:11 * GRID_W].unsqueeze(1).broadcast_to([P, 4, 10 * GRID_W]), ALU.add
                                  ).then_inc(bias_ready.handle, 1)
                dve.wait_ge(bias_ready.handle, bias_ready.at(0, l, 1))

                def na_bias(n, t):
                    if 2 <= n <= NB - 3:
                        return inner_h[:, t, :]
                    r = 2 * tiles_of_round("na", n)[0] - 2 * n + KH - 1
                    return table_h[:, t, r * GRID_W:(r + 8) * GRID_W]

                add_to_x(0, l, 28, 0)
                add_to_x(0, l, 29, 1)
                steps = attention(0, l, "na", ag["pieces"], ag["groups"], NB, na_bias, back_to_chunks(6))
                for c in range(2, KC):
                    for work in steps[6 * (c - 2):6 * (c - 1)]:
                        work()
                    add_to_x(0, l, 28 + c, c)
                steps[36]()
                dve.wait_ge(mixed_out.handle, mixed_out.at(0, l, 2 * NB))
                split_lo(0, l, 8, lambda c: st[:, c, :], chunks=range(4, 8))
                for c in range(KC):
                    add_to_x(0, l, 36 + c, c)
                    if c >= 2:
                        sum_squares(squared.at(0, l, c), c - 1)
                sum_squares(squared.at(0, l, KC), KC - 1)

            own.restart()
            row_factor(stat_ready.mid(1), D)
            dve.wait_ge(fac_ready.handle, fac_ready.mid(1))
            for c in range(KC):
                dve.scalar_tensor_tensor(xt[:, c, :], xt[:, c, :], par[:, O_FIN1 + c:O_FIN1 + c + 1], rfac[:, :],
                                         ALU.mult, ALU.mult).then_inc(x_scaled.handle, 1)
                if c >= 2:
                    sum_squares(squared.mid(c), c - 1)
            sum_squares(squared.mid(KC), KC - 1)

            with dve.Fori(0, DEPTH) as l:
                own.restart()
                dve.tensor_copy(cur[:, 0:W2], par[:, bass.ds(l * W2 + O2, W2)]).then_inc(cur_ready.handle, 1)
                split_lo(1, l, 0, lambda c: xt[:, c, :], lambda c: cur[:, C_AN + c:C_AN + c + 1])
                row_factor(stat_ready.at(1, l, 1), D)
                dve.wait_ge(fac_ready.handle, fac_ready.at(1, l, 1))
                for k in range(4):
                    evacuate(1, l, k, st[:, 8 + k % 2, :])
                    if k:
                        dve.wait_ge(tanh_ready.handle, tanh_ready.at(1, l, k))
                        link(dve.scalar_tensor_tensor(st[:, k - 1, :], st[:, 10 + (k - 1) % 2, :], 1.0,
                                                      st[:, 8 + (k - 1) % 2, :], ALU.add, ALU.mult))
                dve.wait_ge(tanh_ready.handle, tanh_ready.at(1, l, 4))
                link(dve.scalar_tensor_tensor(st[:, 3, :], st[:, 11, :], 1.0, st[:, 9, :], ALU.add, ALU.mult))
                for k in range(4):
                    evacuate(1, l, 4 + k, st[:, 10 + k, :])
                for k in range(4):
                    if k >= 2:
                        dve.wait_ge(vt_ready.handle, vt_ready.at(1, l, 2 * (k - 1)))
                    evacuate(1, l, 8 + k, st[:, 8 + k % 2, :])

                tables = st[:, 8, :]
                decay, q_decay, k_decay = tables[:, 0:512], tables[:, 512:768], tables[:, 768:1024]

                def r_decays(n):
                    dve.wait_ge(r_scored.handle, r_scored.at(1, l, n + 1))
                    if n == 0:
                        dve.wait_ge(retc_in.handle, retc_in.at(1, l, 16))
                        link(dve.memset(state_of(0), 0.0))
                        link(dve.memset(state_of(1), 0.0))
                    else:
                        dve.wait_ge(r_summed.handle, r_summed.at(1, l, n))
                    dve.tensor_tensor(st[:, 9, 0:512].rearrange("p (a b) -> p a b", a=2), ps[:, 4:6, 0:256],
                                      decay.rearrange("p (a b) -> p a b", a=2), ALU.mult)
                    dve.tensor_tensor(st[:, 22, 0:256], ps[:, 4, 256:512], k_decay, ALU.mult)
                    dve.tensor_tensor(st[:, 22, 256:512].rearrange("p (c q) -> p c q", c=2),
                                      st[:, 10:12, n * P:(n + 1) * P],
                                      q_decay.rearrange("p (c q) -> p c q", c=2), ALU.mult).then_inc(r_decayed.handle, 1)

                def r_next(n):
                    dve.wait_ge(r_summed.handle, r_summed.at(1, l, n + 1))
                    if n < NB - 1:
                        for t in range(4):
                            b = HD * (t % 2)
                            a = slice(t * P, (t + 1) * P)
                            i = dve.scalar_tensor_tensor(state_of(n + 1)[b:b + HD, a], state_of(n)[b:b + HD, a],
                                                         chunk_decay(t), ps[b:b + HD, 5, 256 + (t // 2) * P:256 + (t // 2 + 1) * P],
                                                         ALU.mult, ALU.add)
                        i.then_inc(r_state.handle, 1)
                        dve.wait_ge(r_state.handle, r_state.at(1, l, n + 1))
                    dve.wait_ge(r_squared.handle, r_squared.at(1, l, n + 1))
                    link(dve.tensor_scalar(stat[:, 0:4], ssq[:, 0:4], 1.0 / P, EPS, ALU.mult, ALU.add))
                    rsqrt(stat[:, 0:4], root[:, 0:4], tmp[:, 0:4])
                    if n >= 1:
                        dve.wait_ge(r_back.handle, r_back.at(1, l, n))
                    dve.tensor_tensor(half[:, :].rearrange("p (t e) -> p t e", t=4),
                                      ps[:, 6, :].rearrange("p (t e) -> p t e", t=4),
                                      root[:, 0:4].unsqueeze(2).broadcast_to([P, 4, P]), ALU.mult
                                      ).then_inc(r_headed.handle, 1)

                def r_finish(n):
                    dve.wait_ge(r_back.handle, r_back.at(1, l, n + 1))
                    y = st[:, 0:4, n * P:(n + 1) * P]
                    dve.scalar_tensor_tensor(y, ps[:, 7, :].rearrange("p (c q) -> p c q", c=4), cur[:, C_RN:C_RN + 1], y,
                                             ALU.mult, ALU.mult).then_inc(r_out.handle, 1)

                places = (4, 5, 6, 7, 18, 19, 20, 21, 8, 9)
                for n in range(NB + 2):
                    if 1 <= n < NB + 1:
                        r_next(n - 1)
                    evacuate(1, l, 12 + n, st[:, places[n], :])
                    if n < NB:
                        r_decays(n)
                    if n >= 2:
                        r_finish(n - 2)
                evacuate(1, l, 22, st[:, 14, :])
                evacuate(1, l, 23, st[:, 15, :])

                def dif_finish(n):
                    return dve.tensor_scalar(st[:, 4:8, n * P:(n + 1) * P], ps[:, 6, :].rearrange("p (c q) -> p c q", c=4),
                                             cur[:, C_DN:C_DN + 1], None, ALU.mult)

                dve.wait_ge(r_out.handle, r_out.at(1, l, NB))
                split_lo(1, l, 8, lambda c: st[:, c, :], chunks=range(4))
                dve.wait_ge(alibi_in.handle, alibi_in.at(1, l, 16))
                add_to_x(1, l, 24, 0)
                add_to_x(1, l, 25, 1)
                steps = attention(1, l, "dif", 0, 0, 0, lambda n, t: space_lo[:, t, S - (n + 1) * P:S], dif_finish)
                for c in range(2, KC):
                    for work in steps[6 * (c - 2):6 * (c - 1)]:
                        work()
                    add_to_x(1, l, 24 + c, c)
                steps[36]()
                dve.wait_ge(mixed_out.handle, mixed_out.at(1, l, NB))
                split_lo(1, l, 8, lambda c: st[:, c, :], chunks=range(4, 8))
                for c in range(KC):
                    add_to_x(1, l, 32 + c, c)
                    if c >= 2:
                        sum_squares(squared.at(1, l, c), c - 1)
                sum_squares(squared.at(1, l, KC), KC - 1)

                split_lo(1, l, 16, lambda c: xt[:, c, :], lambda c: cur[:, C_FN + c:C_FN + c + 1])
                row_factor(stat_ready.at(1, l, 2), D)
                dve.wait_ge(fac_ready.handle, fac_ready.at(1, l, 2))
                n, chunk0 = 40, 0

                def hidden_lo(c, i):
                    dve.wait_ge(hid_hi_ready.handle, hid_hi_ready.at(1, l, i + 1))
                    dve.tensor_tensor(hid_lo[:, c, :], st[:, 16 + c % 2, :], hid_hi[:, c, :].bitcast(F32), ALU.subtract
                                      ).then_inc(hid_lo_ready.handle, 1)

                for group in FFN_GROUPS:
                    for c in range(group):
                        i = chunk0 + c
                        g, t = st[:, 16 + c % 2, :], st[:, 18 + c % 2, :]
                        evacuate(1, l, n + 2 * c, g)
                        if c:
                            hidden_lo(c - 1, i - 1)
                        dve.wait_ge(tanh_ready.handle, tanh_ready.at(1, l, 4 + i + 1))
                        link(dve.scalar_tensor_tensor(t, t, 1.0, g, ALU.add, ALU.mult))
                        up = n + 2 * c + 1
                        dve.wait_ge(done.handle, done.at(1, l, up + 1))
                        dve.scalar_tensor_tensor(g, ps[:, 2 * (up % 2):2 * (up % 2) + 2, :].rearrange("p a b -> p (a b)"),
                                                 0.5, rfac[:, :], ALU.mult, ALU.mult).then_inc(taken.handle, 1)
                        dve.wait_ge(taken.handle, taken.at(1, l, up + 1))
                        dve.tensor_tensor(g, g, t, ALU.mult).then_inc(gated.handle, 1)
                    hidden_lo(group - 1, chunk0 + group - 1)
                    n += 2 * group
                    chunk0 += group
                    for c in range(KC):
                        add_to_x(1, l, n + c, c)
                        if chunk0 == HC and c >= 2:
                            sum_squares(squared.at(1, l, KC + c), c - 1)
                    n += KC
                sum_squares(squared.at(1, l, 2 * KC), KC - 1)

            own.restart()
            row_factor(stat_ready.end(1), D)
            dve.wait_ge(fac_ready.handle, fac_ready.end(1))
            for c in range(KC):
                dve.scalar_tensor_tensor(xt[:, c, :], xt[:, c, :], par[:, O_FIN2 + c:O_FIN2 + c + 1], rfac[:, :],
                                         ALU.mult, ALU.mult).then_inc(out_ready.handle, 1)


def gammas():
    return (1.0 - np.exp2(-5.0 - np.arange(4, dtype=np.float32))).astype(np.float32)


def chunk_decay(t):
    return float(np.exp(np.float32(P) * np.log(gammas()[t])))


def constants():
    f = np.float32
    eye = np.eye(P, dtype=f)
    swap = np.zeros((P, P), f)
    for p in range(P):
        swap[(p // HD) * HD + (p % HD + HD // 2) % HD, p] = 1.0
    inv = (f(10000.0) ** (-np.arange(0, HD, 2, dtype=f) / f(HD))).astype(f)
    ang = (np.arange(S, dtype=f)[None, :] * inv[:, None]).astype(f)
    rope = np.stack([np.tile(np.cos(ang), (4, 1)), np.tile(np.concatenate([-np.sin(ang), np.sin(ang)]), (2, 1))])
    q, k = np.arange(P)[:, None], np.arange(3 * P)[None, :] - P
    gqa = np.where(np.abs(k - q) <= P, 0.0, NEG / SCALE)
    c = np.arange(GRID_W)
    c0 = np.clip(c - KW // 2, 0, GRID_W - KW)
    col = (c[None, :] >= c0[:, None]) & (c[None, :] < c0[:, None] + KW)
    col = np.tile(np.where(col, 0.0, NEG / SCALE), (2, 1))
    row = np.arange(10)[None, :] - np.repeat(np.arange(2), GRID_W)[:, None]
    row = np.where((row >= 0) & (row < KH), 0.0, NEG / SCALE)
    na = np.concatenate([col, np.repeat(row, GRID_W, axis=1)], axis=1)
    lg = np.log(gammas())
    i = np.arange(P, dtype=f)
    rel = i[None, :] - i[:, None]
    decay = [np.where(rel >= 0, np.exp(np.maximum(rel, 0) * lg[t]), 0) * SCALE for t in (0, 2, 1, 3)]
    qd = [np.repeat(np.stack([np.exp((i + 1) * lg[2 * p]), np.exp((i + 1) * lg[2 * p + 1])]), HD, axis=0) for p in range(2)]
    kd = [np.repeat(np.exp((P - 1 - i) * g)[:, None], HD, axis=1) * SCALE for g in lg]
    ret = np.concatenate(decay + qd + kd, axis=1)
    r = np.arange(S)[None, :] - (S - P) - np.arange(P)[:, None]
    alibi = np.stack([np.where(r <= 0, 2.0 ** (-2.0 * (h + 1)) * r / SCALE, NEG / SCALE) for h in range(4)])
    return {"c_square": np.stack([eye, swap]), "c_rope": rope, "c_gqa": gqa, "c_na": na, "c_ret": ret, "c_alibi": alibi}


def columns(first, count):
    return [np.arange(first + P * c, first + P * (c + 1)) for c in range(count)]


def head_columns(first):
    heads = np.concatenate([np.arange(first + HD * h, first + HD * (h + 1)) for h in GQA_ORDER])
    return [heads[:P], heads[P:]]


def weight_block(w, rows, cols):
    part = w[rows][:, cols]
    k = part.shape[0] // P
    block = np.zeros((P, KC, P), w.dtype)
    block[:, :k] = part.reshape(k, P, P).transpose(1, 0, 2)
    return block.reshape(P, KC * P)


def weight_stream(i):
    blocks = []
    u, v, az, bb, bc, bx, bz = (columns(256 * n, 2) for n in range(7))
    cq, ck, cv, cz = head_columns(1792), columns(2048, 1), columns(2176, 1), head_columns(2304)
    dq, dk, dv, dz = (columns(2560 + 256 * n, 2) for n in range(4))
    every = slice(None)
    for l in range(DEPTH):
        order = cq + ck + cv + [v[0], u[0], v[1], u[1]] + cz + az + bz + dz
        order += [bc[0], bx[0], bb[0], bc[1], bx[1], bb[1]] + dq + dk + dv
        blocks += [weight_block(i["w_in"][l], every, c) for c in order]
        rows = np.concatenate([np.arange(512)] + head_columns(512) + [np.arange(768, 1024)])
        blocks += [weight_block(i["w_out"][l], r, c) for r in (rows[:512], rows[512:]) for c in columns(0, KC)]
    for l in range(DEPTH):
        order = columns(1024, 4) + columns(0, 8) + columns(1536, 12)
        blocks += [weight_block(i["w_in_2"][l], every, c) for c in order]
        blocks += [weight_block(i["w_out_2"][l], r, c) for r in (slice(0, 512), slice(512, 1024)) for c in columns(0, KC)]
        chunk = 0
        for group in FFN_GROUPS:
            for c in columns(P * chunk, group):
                blocks += [weight_block(i["w_gate_2"][l], every, c), weight_block(i["w_up_2"][l], every, c)]
            rows = np.arange(P * chunk, P * (chunk + group))
            blocks += [weight_block(i["w_down_2"][l], rows, c) for c in columns(0, KC)]
            chunk += group
    return np.stack(blocks)


def parameters(i):
    def chunks(v):
        return v.reshape(-1, P).T

    cols = []
    for l in range(DEPTH):
        cols += [chunks(i["norm_g"][l])]
        cols += [i["conv_a_w"][l][:, P * c:P * (c + 1)].T for c in range(2)]
        cols += [chunks(i[n][l]) for n in ("conv_a_b", "ln_a_g", "ln_a_b")]
        cols += [i["conv_b_w"][l][:, P * c:P * (c + 1)].T for c in range(2)]
        cols += [np.broadcast_to(i["swa_sink"][l][list(GQA_ORDER)], (P, 4))]
    for l in range(DEPTH):
        cols += [chunks(i[n][l]) for n in ("attn_norm_2", "ffn_norm_2", "ret_norm_2", "diff_norm_2")]
        cols += [np.zeros((P, 1), np.float32)]
    cols += [chunks(i["final_norm_g"]), chunks(i["final_norm_2"])]
    return np.concatenate(cols, axis=1)


def kernel(**inputs):
    import concourse.bacc as bacc
    from concourse.bass_utils import run_bass_kernel_spmd

    i = {k: np.asarray(v) for k, v in inputs.items()}
    lam = np.stack([i[n] for n in ("lambda_q1_2", "lambda_k1_2", "lambda_q2_2", "lambda_k2_2")], axis=1)
    pad = np.pad(i["na_rpb"], ((0, 0), (0, 0), (0, 0), (GRID_W - KW, SKEW - GRID_W - KW + 1)))
    arrays = {
        "x_in": i["x"][0].T.reshape(KC, P, S),
        "w_in": weight_stream(i),
        "par_in": parameters(i),
        "lam_in": np.broadcast_to(lam.reshape(1, -1), (P, DEPTH * 4 * HD)),
        "rpb_in": np.broadcast_to(pad.reshape(DEPTH, 4 * ND, 1, SKEW), (DEPTH, 4 * ND, GRID_W, SKEW)
                                  ).reshape(DEPTH, 4 * ND, GRID_W * SKEW),
        **{k: v.astype(np.float32) for k, v in constants().items()},
    }
    arrays = {k: np.ascontiguousarray(v) for k, v in arrays.items()}
    nc = bacc.Bacc("TRN2", target_bir_lowering=False, num_devices=1, dynamic_dma_scratch_size=1024)
    args = {k: nc.dram_tensor(k, v.shape, F32, kind="ExternalInput").ap() for k, v in arrays.items()}
    out = nc.dram_tensor("out", (KC, P, S), F32, kind="ExternalOutput").ap()
    build(nc, out=out, **args)
    r = run_bass_kernel_spmd(nc, [arrays], core_ids=[0])
    return np.ascontiguousarray(r.results[0]["out"].reshape(D, S).T).reshape(1, S, D)
```

```python
from contextlib import ExitStack

import numpy as np

import concourse.bass as bass
from concourse import mybir

F32 = mybir.dt.float32
F32R = mybir.dt.float32r
I32 = mybir.dt.int32
ALU = mybir.AluOpType
ACT = mybir.ActivationFunctionType

P = 128
S = 1024
HALF = 512
D = 1024
KC = D // P
NB = S // P
DEPTH = 2
EPS = 1e-6
NEG = -1e30
HD = 64
SCALE = HD ** -0.5
FFN = 2816
HC = FFN // P
FFN_GROUPS = [8, 8, 6]
TAPS_A, TAPS_B = 31, 3
GRID_W, KH, KW = 64, 8, 16
ROWS = S // GRID_W
ND = 2 * KH - 1
SKEW = 2 * GRID_W

BLOCKS = (28 + 2 * KC, 24 + 2 * KC + 2 * HC + KC * len(FFN_GROUPS))
N_W = DEPTH * sum(BLOCKS)
SLOTS = 23

C_NEXT = 0
C_CAW, C_CAB, C_LNG, C_LNB, C_CBW, C_SINK, C_POST = 8, 70, 72, 74, 76, 82, 86
W1 = 94
C_FN, C_RN, C_DN, C_NLAM = 8, 16, 17, 18
W2 = 19
O2 = DEPTH * W1
O_FIRST = O2 + DEPTH * W2
O_FIRST2 = O_FIRST + 8
O_FIN1 = O_FIRST2 + 8
O_FIN2 = O_FIN1 + 8
NPAR = O_FIN2 + 8

GQA_ORDER = (0, 2, 1, 3)


def tiles_of_round(kind, n):
    if kind == "gqa":
        return range(max(0, n - 1), min(NB, n + 2))
    if kind == "na":
        if 2 <= n <= NB - 3:
            return range(n - 2, n + 3)
        return range(0, 4) if n < 2 else range(NB - 4, NB)
    return range(0, n + 1)


def groups_of(tiles):
    tiles = list(tiles)
    n = -(-len(tiles) // 4)
    size = -(-len(tiles) // n)
    return [tiles[i:i + size] for i in range(0, len(tiles), size)]


def pieces_of(tiles):
    return groups_of(tiles)


def attention_counts(kind):
    groups = sum(4 * len(groups_of(tiles_of_round(kind, n))) for n in range(NB))
    maps = 2 if kind == "dif" else 1
    return {"maps": 4 * NB * maps, "pieces": groups * maps, "units": 4 * NB, "groups": groups, "rounds": NB}


STEPS = 4 * NB + 8


def heads_step(kind, n):
    return 4 * n + (9 if kind == "dif" else 7)


CUTS = {"gqa": tuple(STEPS * i // 10 for i in range(11)), "na": (0, 8, 16, 24, 32, STEPS), "dif": (0, 5, 11, 17, 33, STEPS)}


def share(kind, steps, i):
    return steps[CUTS[kind][i]:CUTS[kind][i + 1]]


class Signal:

    def __init__(self, handle, per, before=0, between=0):
        self.handle, self.per, self.before, self.between = handle, per, before, between

    def at(self, stack, l, n):
        base = self.before + (DEPTH * self.per[0] + self.between if stack else 0)
        return l * self.per[stack] + (base + n)

    def end(self, n=0):
        return self.before + self.between + DEPTH * sum(self.per) + n

    def mid(self, n):
        return self.before + DEPTH * self.per[0] + n


class Chain:

    def __init__(self, engine, handle):
        self.engine, self.handle, self.n = engine, handle, 0

    def restart(self):
        self.engine.sem_clear(self.handle)
        self.n = 0

    def link(self, instruction):
        self.n += 1
        instruction.then_inc(self.handle, 1)
        self.engine.wait_ge(self.handle, self.n)


def build(nc, x_in, w_in, par_in, lam_in, rpb_in, c_ident, c_rope, c_gqa, c_na, c_ret, c_alibi, out):
    ctx = ExitStack()
    with ctx:
        top = [-(-nc.sbuf_base // 64) * 64]

        def sb(name, shape, dt=F32, at=None):
            offset = top[0] if at is None else at
            if at is None:
                top[0] += -(-4 * int(np.prod(shape[1:])) // 32) * 32
            return nc.alloc_sbuf_tensor_at(name, shape, dt, offset=offset)

        xt = sb("xt", [P, KC, S])
        base_in = top[0]
        in_hi = sb("in_hi", [P, KC, S], F32R)
        in_lo = sb("in_lo", [P, KC, S], F32R)
        w_raw = sb("w_raw", [P, 2, KC * P])
        w_hi = sb("w_hi", [P, 2, KC * P], F32R)
        w_lo = sb("w_lo", [P, 2, KC * P], F32R)
        base_st = top[0]
        st = sb("st", [P, SLOTS, S])
        rfac = sb("rfac", [P, S])
        half = sb("half", [P, HALF])
        ident = sb("ident", [P, P])[:, :]
        ones = sb("ones", [P, P])
        mask_gqa = sb("mask_gqa", [P, 3 * P])
        par = sb("par", [P, NPAR])
        cur = sb("cur", [P, W1])
        small = sb("small", [P, 104])
        space_hi = sb("space_hi", [P, 4, S], at=base_in + 4 * 4 * S)
        space_lo = sb("space_lo", [P, 4, S], at=base_in + 12 * 4 * S)
        hid_hi = sb("hid_hi", [P, 8, S], F32R, at=base_st)
        hid_lo = sb("hid_lo", [P, 8, S], F32R, at=base_st + 8 * 4 * S)

        stat, root, tmp = small[:, 0:8], small[:, 8:16], small[:, 16:24]
        negm = small[:, 24:40].rearrange("p (a b) -> p a b", a=2)
        lsum = small[:, 40:56].rearrange("p (a b) -> p a b", a=2)
        rinv = small[:, 56:72].rearrange("p (a b) -> p a b", a=2)
        esink, ssq, comb, factor = (small[:, 72 + 4 * i:76 + 4 * i] for i in range(4))
        prior = small[:, 88:96]

        ps = ctx.enter_context(nc.psum_tensor("ps", [P, 8, HALF], F32))

        sems = {}

        def signal(name, one=0, two=0, before=0, between=0):
            s = Signal(ctx.enter_context(nc.semaphore(name)), (one, two), before, between)
            sems[name] = s
            return s

        raw_in = [signal(f"raw_in{j}") for j in range(2)]
        w_split = signal("w_split", *BLOCKS)
        done = signal("done", *BLOCKS)
        taken = signal("taken", *BLOCKS, before=2)
        hi_ready = signal("hi_ready", 16, 24, before=8)
        lo_ready = signal("lo_ready", 16, 24, before=8)
        hid_hi_ready = signal("hid_hi_ready", 0, HC)
        hid_lo_ready = signal("hid_lo_ready", 0, HC)
        cur_ready = signal("cur_ready", 1, 1)
        squared = signal("squared", 8, 16, before=8)
        acc_ready = signal("acc_ready", 1, 2, before=1)
        squared_x = signal("squared_x", 8)
        acc_x_ready = signal("acc_x_ready", 1)
        stat_ready = signal("stat_ready", 2, 2, between=1)
        diag_ready = signal("diag_ready", 2, 2, between=1)
        spread_ready = signal("spread_ready", 2, 2, between=1)
        fac_ready = signal("fac_ready", 2, 2, between=1)
        tanh_ready = signal("tanh_ready", 10, 4 + HC)
        gated = signal("gated", 0, HC)
        conv_ready = signal("conv_ready", 1)
        mean_ready = signal("mean_ready", 1)
        centred = signal("centred", 2)
        lnsq_ready = signal("lnsq_ready", 2)
        lnsq_sum = signal("lnsq_sum", 1)
        normed = signal("normed", 2)
        lnact_ready = signal("lnact_ready", 2)
        conv_out = signal("conv_out", 2)
        rope_in = signal("rope_in", 2 * 16)
        swapped = [signal(f"swapped{i}", 4 * 16) for i in range(3)]
        roped = signal("roped", 3)
        vt_ready = signal("vt_ready", 6, 16)
        vt_taken = signal("vt_taken", 6, 16)
        bias_in = signal("bias_in", 4 * 16)
        bias_ready = signal("bias_ready", 1)
        ag, an, ad = (attention_counts(k) for k in ("gqa", "na", "dif"))
        both = {k: ag[k] + an[k] for k in ag}
        scored = signal("scored", both["pieces"], ad["pieces"])
        biased = signal("biased", both["pieces"], ad["pieces"])
        expd = signal("expd", both["maps"], ad["maps"])
        mixed = signal("mixed", 0, ad["units"])
        turned = signal("turned", both["groups"], ad["groups"])
        turned_out = signal("turned_out", both["groups"], ad["groups"])
        weighted = signal("weighted", both["rounds"], ad["rounds"])
        sink_ready = signal("sink_ready", ag["rounds"])
        sink_exp = signal("sink_exp", ag["rounds"])
        raw_heads = signal("raw_heads", 0, ad["rounds"])
        head_sq = signal("head_sq", 0, ad["rounds"])
        headed = signal("headed", both["rounds"], ad["rounds"])
        back = signal("back", both["rounds"], ad["rounds"])
        mixed_out = signal("mixed_out", both["rounds"], ad["rounds"])
        alibi_in = signal("alibi_in", 0, 16)
        retc_in = signal("retc_in", 0, 16)
        r_scored = signal("r_scored", 0, NB)
        r_decayed = signal("r_decayed", 0, NB)
        r_summed = signal("r_summed", 0, NB)
        r_squared = signal("r_squared", 0, NB)
        r_state = signal("r_state", 0, NB - 1)
        r_headed = signal("r_headed", 0, NB)
        r_back = signal("r_back", 0, NB)
        r_out = signal("r_out", 0, NB)
        x_in_sem = [signal(f"x_in{c}") for c in range(KC)]
        const_in = signal("const_in")
        lam_sem = signal("lam_sem")
        lam_exp = signal("lam_exp")
        par_in_sem = signal("par_in_sem")
        out_ready = signal("out_ready")
        out_sem = signal("out_sem")
        dve_own = ctx.enter_context(nc.semaphore("dve_own"))
        dve_step = ctx.enter_context(nc.semaphore("dve_step"))
        act_own = ctx.enter_context(nc.semaphore("act_own"))
        pool_own = ctx.enter_context(nc.semaphore("pool_own"))

        ACC, DIAG, DIAG_LN, SQ = 22, 21, 16, (18, 19)
        ACC_X, SQ_X, DIAG_X, FAC_X = 11, (12, 13), 14, 15

        def flat(tensor, first, count):
            return tensor[:, first:first + count, :].rearrange("p a n -> p (a n)")

        def exp_buffer(kind, m):
            if kind == "gqa":
                m %= 4
                return st[:, 16, 3 * P * m:3 * P * (m + 1)] if m < 2 else flat(st, 21, 2)[:, 3 * P * (m - 2):3 * P * (m - 1)]
            if kind == "na":
                return space_hi[:, m % 4, :]
            return space_hi[:, m % 8, :] if m % 8 < 4 else st[:, m % 4, :]

        def exp_buffers(kind):
            return 8 if kind == "dif" else 4

        def turned_buffer(kind, g):
            if kind == "gqa":
                g %= 3
                return flat(st, 21, 2)[:, 3 * P * (g + 2):3 * P * (g + 3)]
            return st[:, 8 + (g % 4) // 2, (g % 2) * HALF:(g % 2 + 1) * HALF]

        def raw_buffer(n):
            return st[:, 16, (n % 2) * HALF:(n % 2 + 1) * HALF]

        def head_buffer(kind, n):
            if kind == "gqa":
                return half[:, (n % 2) * 2 * P:(n % 2 + 1) * 2 * P]
            return st[:, 10 if kind == "na" else 14, (n % 2) * HALF:(n % 2 + 1) * HALF]

        def rv(n, t):
            return st[:, 14 + n // 2, (n % 2) * HALF + t * P:(n % 2) * HALF + (t + 1) * P]

        def state_of(n):
            return st[:, (22, 9)[n % 2], HALF:S]

        block = ctx.enter_context(nc.Block())

        @block.sync
        def _(sp):
            def load(pair, first):
                for j in range(2):
                    if not first:
                        sp.wait_ge(w_split.handle, pair * 2 + (j - 1))
                    sp.dma_start(w_raw[:, j, :], w_in[bass.ds(pair * 2 + j, 1), :, :].rearrange("a p n -> (a p) n")
                                 ).then_inc(raw_in[j].handle, 16)
            load(0, True)
            with sp.Fori(1, N_W // 2) as pair:
                load(pair, False)

        @block.gpsimd
        def _(pool):
            def split(pair, first):
                for j in range(2):
                    pool.wait_ge(raw_in[j].handle, pair * 16 + 16)
                    if not first:
                        pool.wait_ge(done.handle, pair * 2 + (j - 1))
                    pool.tensor_tensor(w_hi[:, j, :], w_raw[:, j, :], ones[:, 0:1].broadcast_to([P, KC * P]),
                                       ALU.mult).then_inc(pool_own, 1)
                    pool.wait_ge(pool_own, pair * 2 + (j + 2))
                    pool.tensor_tensor(w_lo[:, j, :], w_raw[:, j, :], w_hi[:, j, :].bitcast(F32),
                                       ALU.subtract).then_inc(w_split.handle, 1)
            pool.memset(ones[:, :], 1.0).then_inc(pool_own, 1)
            pool.wait_ge(pool_own, 1)
            split(0, True)
            with pool.Fori(1, N_W // 2) as pair:
                split(pair, False)

        @block.tensor
        def _(pe):
            def product(stack, l, n, hi, lo, chunks=KC, k0=0, before_chunk=None, between=()):
                n, j = n if isinstance(n, tuple) else (n, n % 2)
                pe.wait_ge(w_split.handle, w_split.at(stack, l, n + 1))
                pe.wait_ge(taken.handle, taken.at(stack, l, n - 1))
                i, at = 0, [(2 * b + 1) * 3 * chunks // max(1, len(between)) // 2 for b in range(len(between))]
                for k in range(chunks):
                    if before_chunk:
                        before_chunk(k)
                    for w, parts in ((w_hi, (hi, lo)), (w_lo, (hi,))):
                        for part in parts:
                            for b, work in zip(at, between):
                                if b == i and work:
                                    work()
                            i += 1
                            for h in range(2):
                                last = pe.matmul(ps[:, 2 * j + h, :], w[:, j, k * P:(k + 1) * P],
                                                 part[:, k0 + k, h * HALF:(h + 1) * HALF],
                                                 start=(k == 0 and w is w_hi and part is hi),
                                                 stop=(k == chunks - 1 and w is w_lo))
                last.then_inc(done.handle, 1)

            def products(stack, l, n0, n1, hi=in_hi, lo=in_lo, chunks=KC, k0=0):
                with pe.Fori(n0, n1, 2) as n:
                    product(stack, l, (n, 0), hi, lo, chunks, k0)
                    product(stack, l, (n + 1, 1), hi, lo, chunks, k0)

            def chunk_wait(stack, l, base, ready=lo_ready):
                return lambda k: pe.wait_ge(ready.handle, ready.at(stack, l, base + k + 1))

            def row_sums(tile):
                for b in range(NB):
                    last = pe.matmul(ps[:, 4, b:b + 1], tile[:, b * P:(b + 1) * P], ones[:, 0:1], start=True, stop=True)
                last.then_inc(stat_ready.handle, 1)

            def spread(wait, diag=DIAG):
                pe.wait_ge(diag_ready.handle, wait)
                for h in range(2):
                    last = pe.matmul(ps[:, 5 + h, :], ones[:, :], st[:, diag, h * HALF:(h + 1) * HALF],
                                     start=True, stop=True)
                last.then_inc(spread_ready.handle, 1)

            def turn_values(stack, l, k0, tile, banks=(4, 5)):
                for g in range(2):
                    if k0 + g >= 2:
                        pe.wait_ge(vt_taken.handle, vt_taken.at(stack, l, k0 + g - 1))
                    for b in range(4):
                        last = pe.transpose(ps[:, banks[g], b * P:(b + 1) * P],
                                            tile[:, (4 * g + b) * P:(4 * g + b + 1) * P], ident)
                    last.then_inc(vt_ready.handle, 1)

            def attention(stack, l, kind, p0, g0, r0, query, key, value, width):
                maps = 2 if kind == "dif" else 1
                units = [(n, t) for n in range(NB) for t in range(4)]
                state = {"p": 0, "g": 0, "free": None}
                where = {}

                def scores(u, i):
                    n, t = units[u]
                    for piece in pieces_of(tiles_of_round(kind, n))[i:i + 1]:
                        for j in range(maps):
                            q, base = query(t, j)
                            p = state["p"]
                            if p >= 2:
                                pe.wait_ge(biased.handle, biased.at(stack, l, p0 + p - 1))
                            pe.matmul(ps[:, 4 + p % 2, 0:len(piece) * P],
                                      q[base:base + HD, n * P:(n + 1) * P],
                                      key(t, j)[base:base + HD, piece[0] * P:(piece[-1] + 1) * P],
                                      start=True, stop=True).then_inc(scored.handle, 1)
                            state["p"] += 1

                def bank_6_free():
                    if state["free"]:
                        ready, count = state["free"]
                        pe.wait_ge(ready.handle, ready.at(stack, l, count))

                def turn(u, i):
                    n, t = units[u]
                    tiles = tiles_of_round(kind, n)
                    groups = groups_of(tiles)
                    if i >= len(groups):
                        return
                    g = state["g"]
                    if i == 0:
                        if kind == "dif":
                            pe.wait_ge(mixed.handle, mixed.at(stack, l, u + 1))
                        else:
                            pe.wait_ge(expd.handle, expd.at(stack, l, (0 if kind == "gqa" else ag["maps"]) + u + 1))
                    bank_6_free()
                    e = exp_buffer(kind, maps * u)
                    for b, kt in enumerate(groups[i]):
                        c = (kt - tiles[0]) * P
                        last = pe.transpose(ps[:, 6, b * P:(b + 1) * P], e[:, c:c + P], ident)
                    last.then_inc(turned.handle, 1)
                    state["free"] = (turned_out, g0 + g + 1)
                    where.setdefault(u, []).append((g, groups[i]))
                    state["g"] += 1

                def weigh(u):
                    n, t = units[u]
                    tiles = tiles_of_round(kind, n)
                    if t == 0 and n >= 1:
                        free = raw_heads if kind == "dif" else headed
                        pe.wait_ge(free.handle, free.at(stack, l, r0 + n))
                    for g, group in where[u]:
                        pe.wait_ge(turned_out.handle, turned_out.at(stack, l, g0 + g + 1))
                        for b, kt in enumerate(group):
                            last = pe.matmul(ps[:, 7, t * width:(t + 1) * width],
                                             turned_buffer(kind, g)[:, b * P:(b + 1) * P],
                                             value(t, kt), start=(kt == tiles[0]), stop=(kt == tiles[-1]))
                    if t == 3:
                        last.then_inc(weighted.handle, 1)

                def turn_back(n):
                    pe.wait_ge(headed.handle, headed.at(stack, l, r0 + n + 1))
                    bank_6_free()
                    for c in range(4 * width // P):
                        last = pe.transpose(ps[:, 6, c * P:(c + 1) * P],
                                            head_buffer(kind, n)[:, c * P:(c + 1) * P], ident)
                    last.then_inc(back.handle, 1)
                    state["free"] = (mixed_out, r0 + n + 1)

                def step(u):
                    if 3 <= u < len(units) + 3:
                        turn(u - 3, 0)
                    if u < len(units):
                        scores(u, 0)
                    if 4 <= u < len(units) + 4:
                        weigh(u - 4)
                    if u < len(units):
                        scores(u, 1)
                    if 3 <= u < len(units) + 3:
                        turn(u - 3, 1)
                    for n in range(NB):
                        if u == heads_step(kind, n) + 2:
                            turn_back(n)

                return [lambda u=u: step(u) for u in range(STEPS)]


            with pe.Fori(0, DEPTH) as l:
                block_of = lambda n, **k: product(0, l, n, in_hi, in_lo, **k)

                def evacuated(n):
                    pe.wait_ge(taken.handle, taken.at(0, l, n))

                block_of(0, before_chunk=chunk_wait(0, l, -8))
                pe.wait_ge(acc_ready.handle, acc_ready.at(0, l, 0))
                row_sums(st[:, ACC, :])
                block_of(1, between=[None, lambda: spread(diag_ready.at(0, l, 1))])
                block_of(2)
                block_of(3)
                for n in (4, 5, 6):
                    block_of(n)
                evacuated(4)
                turn_values(0, l, 0, st[:, 8, :])
                block_of(7)
                pe.wait_ge(roped.handle, roped.at(0, l, 3))
                pe.wait_ge(vt_taken.handle, vt_taken.at(0, l, 2))
                steps = attention(0, l, "gqa", 0, 0, 0,
                                  lambda t, j: (st[:, 19 + t // 2, :], HD * (t % 2)),
                                  lambda t, j: st[:, 17, :],
                                  lambda t, kt: st[:, 18, kt * P + HD * (t % 2):kt * P + HD * (t % 2 + 1)], HD)
                block_of(8)
                for n in range(9, 19):
                    block_of(n, between=share("gqa", steps, n - 9))
                for n in range(19, 23):
                    block_of(n)
                pe.wait_ge(conv_ready.handle, conv_ready.at(0, l, 1))
                for h in range(2):
                    for c in range(2):
                        last = pe.matmul(ps[:, 4 + h, :], ones[:, :], st[:, 12 + c, h * HALF:(h + 1) * HALF],
                                         start=(c == 0), stop=(c == 1))
                last.then_inc(mean_ready.handle, 1)
                block_of(23)
                block_of(24)
                pe.wait_ge(lnsq_sum.handle, lnsq_sum.at(0, l, 1))
                row_sums(st[:, 14, :])
                pe.wait_ge(mixed_out.handle, mixed_out.at(0, l, NB))
                block_of(25, between=[None, lambda: spread(diag_ready.at(0, l, 2), DIAG_LN)])
                block_of(26)
                pe.wait_ge(fac_ready.handle, fac_ready.at(0, l, 2))
                block_of(27, between=[None, lambda: evacuated(27), lambda: turn_values(0, l, 2, st[:, 8, :])])
                evacuated(28)
                turn_values(0, l, 4, st[:, 9, :])
                wait = chunk_wait(0, l, 0)
                block_of(28, chunks=4, before_chunk=wait)
                block_of(29, chunks=4)
                pe.wait_ge(vt_taken.handle, vt_taken.at(0, l, 6))
                slots = (19, 20, 17, 18)
                steps = attention(0, l, "na", ag["pieces"], ag["groups"], NB,
                                  lambda t, j: (st[:, slots[t // 2], :], HD * (t % 2)),
                                  lambda t, j: st[:, slots[2 + t // 2], :],
                                  lambda t, kt: st[:, 21 + kt // 4, (kt % 4) * 256 + t * HD:(kt % 4) * 256 + (t + 1) * HD],
                                  HD)
                for n in range(30, 35):
                    block_of(n, chunks=4, between=share("na", steps, n - 30))
                block_of(35, chunks=4)
                block_of(36, chunks=4, k0=4, before_chunk=chunk_wait(0, l, 4))
                block_of(37, chunks=4, k0=4)
                products(0, l, 38, 44, chunks=4, k0=4)

            pe.wait_ge(acc_x_ready.handle, DEPTH)
            row_sums(st[:, ACC_X, :])
            spread(diag_ready.mid(1), DIAG_X)

            with pe.Fori(0, DEPTH) as l:
                product(1, l, 0, in_hi, in_lo, before_chunk=chunk_wait(1, l, -8))
                pe.wait_ge(acc_ready.handle, acc_ready.at(1, l, 0))
                pe.wait_ge(fac_ready.handle, fac_ready.at(1, l, 0))
                row_sums(st[:, ACC, :])
                product(1, l, 1, in_hi, in_lo, between=[None, lambda: spread(diag_ready.at(1, l, 1))])
                products(1, l, 2, 10)
                pe.wait_ge(taken.handle, taken.at(1, l, 9))
                turn_values(1, l, 0, st[:, 8, :])
                product(1, l, 10, in_hi, in_lo)
                pe.wait_ge(taken.handle, taken.at(1, l, 10))
                turn_values(1, l, 2, st[:, 9, :])
                product(1, l, 11, in_hi, in_lo)
                pe.wait_ge(taken.handle, taken.at(1, l, 11))
                turn_values(1, l, 4, st[:, 8, :])
                product(1, l, 12, in_hi, in_lo)
                pe.wait_ge(taken.handle, taken.at(1, l, 12))
                turn_values(1, l, 6, st[:, 9, :])

                def r_scores(n):
                    if n >= 1:
                        pe.wait_ge(r_decayed.handle, r_decayed.at(1, l, n))
                        pe.wait_ge(r_state.handle, r_state.at(1, l, n))
                    else:
                        pe.wait_ge(vt_taken.handle, vt_taken.at(1, l, 8))
                    for c in range(2):
                        pe.transpose(ps[:, 4, 256 + c * P:256 + (c + 1) * P], st[:, 12 + c, n * P:(n + 1) * P], ident)
                    for t in range(4):
                        b = HD * (t % 2)
                        last = pe.matmul(ps[:, 4 + t % 2, (t // 2) * P:(t // 2 + 1) * P], st[b:b + HD, 12 + t // 2, n * P:(n + 1) * P],
                                         st[b:b + HD, 10 + t // 2, n * P:(n + 1) * P], start=True, stop=True)
                    last.then_inc(r_scored.handle, 1)

                def r_sums(n):
                    pe.wait_ge(r_decayed.handle, r_decayed.at(1, l, n + 1))
                    if n >= 1:
                        pe.wait_ge(r_state.handle, r_state.at(1, l, n))
                        pe.wait_ge(r_headed.handle, r_headed.at(1, l, n))
                    for c in range(2):
                        pe.matmul(ps[:, 6, 2 * c * P:2 * (c + 1) * P], st[:, 22, 256 + c * P:256 + (c + 1) * P],
                                  state_of(n)[:, 2 * c * P:2 * (c + 1) * P],
                                  start=(c == 0), stop=False, skip_group_check=True)
                    for t in range(4):
                        last = pe.matmul(ps[:, 6, t * P:(t + 1) * P], st[:, 9, GQA_ORDER[t] * P:(GQA_ORDER[t] + 1) * P],
                                         rv(n, t), start=False, stop=(t == 3), skip_group_check=True)
                    if n < NB - 1:
                        for t in range(4):
                            b = HD * (t % 2)
                            last = pe.matmul(ps[b:b + HD, 5, 256 + (t // 2) * P:256 + (t // 2 + 1) * P],
                                             st[:, 22, t * HD:(t + 1) * HD], rv(n, t), start=True, stop=True)
                    last.then_inc(r_summed.handle, 1)

                def r_turn_back(n):
                    pe.wait_ge(r_headed.handle, r_headed.at(1, l, n + 1))
                    if n >= 1:
                        pe.wait_ge(r_out.handle, r_out.at(1, l, n))
                    for t in range(4):
                        last = pe.transpose(ps[:, 7, t * P:(t + 1) * P], half[:, t * P:(t + 1) * P], ident)
                    last.then_inc(r_back.handle, 1)

                for n in range(NB + 2):
                    if n >= 1:
                        product(1, l, 12 + n, in_hi, in_lo, between=[lambda: r_sums(n - 1)] if n <= NB else [])
                    if n < NB:
                        r_scores(n)
                    if n >= 2:
                        r_turn_back(n - 2)
                pe.wait_ge(taken.handle, taken.at(1, l, 21))
                turn_values(1, l, 8, st[:, 8, :])
                product(1, l, 22, in_hi, in_lo)
                pe.wait_ge(taken.handle, taken.at(1, l, 22))
                turn_values(1, l, 10, st[:, 9, :])
                product(1, l, 23, in_hi, in_lo,
                        between=[None, lambda: pe.wait_ge(taken.handle, taken.at(1, l, 23)),
                                 lambda: turn_values(1, l, 12, st[:, 14, :])])
                pe.wait_ge(taken.handle, taken.at(1, l, 24))
                turn_values(1, l, 14, st[:, 15, :])
                product(1, l, 24, in_hi, in_lo, chunks=4, before_chunk=chunk_wait(1, l, 0))
                product(1, l, 25, in_hi, in_lo, chunks=4)
                pe.wait_ge(vt_taken.handle, vt_taken.at(1, l, 16))
                pe.wait_ge(r_out.handle, r_out.at(1, l, NB))
                steps = attention(1, l, "dif", 0, 0, 0,
                                  lambda t, j: (st[:, 4 + t, :], HD * j),
                                  lambda t, j: st[:, 18 + t, :],
                                  lambda t, kt: st[:, 10 + kt // 2, (kt % 2) * HALF + t * P:(kt % 2) * HALF + (t + 1) * P], P)
                for n in range(26, 31):
                    product(1, l, n, in_hi, in_lo, chunks=4, between=share("dif", steps, n - 26))
                product(1, l, 31, in_hi, in_lo, chunks=4)
                product(1, l, 32, in_hi, in_lo, chunks=4, k0=4, before_chunk=chunk_wait(1, l, 4))
                product(1, l, 33, in_hi, in_lo, chunks=4, k0=4)
                products(1, l, 34, 40, chunks=4, k0=4)
                n = 40
                chunk0 = 0
                for group in FFN_GROUPS:
                    if chunk0 == 0:
                        product(1, l, n, in_hi, in_lo, before_chunk=chunk_wait(1, l, 8))
                        pe.wait_ge(acc_ready.handle, acc_ready.at(1, l, 1))
                        row_sums(st[:, ACC, :])
                        product(1, l, n + 1, in_hi, in_lo, between=[None, lambda: spread(diag_ready.at(1, l, 2))])
                        products(1, l, n + 2, n + 2 * group)
                    else:
                        products(1, l, n, n + 2 * group)
                    n += 2 * group
                    product(1, l, n, hid_hi, hid_lo, chunks=group,
                            before_chunk=chunk_wait(1, l, chunk0, hid_lo_ready))
                    product(1, l, n + 1, hid_hi, hid_lo, chunks=group)
                    products(1, l, n + 2, n + KC, hid_hi, hid_lo, chunks=group)
                    n += KC
                    chunk0 += group

            pe.wait_ge(acc_ready.handle, acc_ready.end())
            row_sums(st[:, ACC, :])
            spread(diag_ready.end(1))

        @block.scalar
        def _(act):
            def split_hi(stack, source, scale=None, chunks=range(KC)):
                for c in chunks:
                    s = scale(c) if scale else 1.0
                    act.activation(in_hi[:, c, :], source(c), ACT.Copy if scale is None else ACT.Identity,
                                   scale=s).then_inc(hi_ready.handle, 1)

            def squares(c, scale=1.0):
                act.activation(st[:, ACC if c == 0 else SQ[c % 2], :], xt[:, c, :], ACT.Square, scale=scale
                               ).then_inc(squared.handle, 1)

            def take_factor(wait, slot=None):
                act.wait_ge(spread_ready.handle, wait)
                to = rfac[:, :] if slot is None else st[:, slot, :]
                act.activation(to, ps[:, 5:7, :], ACT.Copy).then_inc(fac_ready.handle, 1)

            def take_values(stack, l, k0, to):
                for g in range(2):
                    act.wait_ge(vt_ready.handle, vt_ready.at(stack, l, k0 + g + 1))
                    act.activation(to(g), ps[:, 4 + g, :].rearrange("p (b c) -> p b c", b=4), ACT.Copy
                                   ).then_inc(vt_taken.handle, 1)

            def attention(stack, l, kind, p0, g0, r0):
                maps = 2 if kind == "dif" else 1
                units = [(n, t) for n in range(NB) for t in range(4)]
                state = {"g": 0, "p": 0}

                def exps(u):
                    n, t = units[u]
                    tiles = tiles_of_round(kind, n)
                    state["p"] += maps * len(pieces_of(tiles))
                    for j in range(maps):
                        m = maps * u + j
                        act.wait_ge(biased.handle, biased.at(stack, l, p0 + state["p"] - (maps - 1 - j)))
                        e = exp_buffer(kind, m)[:, 0:len(tiles) * P]
                        i = maps * t + j
                        act.activation(e, e, ACT.Exp, bias=negm[:, n % 2, i:i + 1], scale=-1.0,
                                       accum_out=lsum[:, n % 2, i:i + 1]).then_inc(expd.handle, 1)
                    if kind == "gqa" and t == 3:
                        act.wait_ge(sink_ready.handle, sink_ready.at(stack, l, n + 1))
                        act.activation(esink, comb, ACT.Exp).then_inc(sink_exp.handle, 1)

                def groups(u, i):
                    n, t = units[u]
                    for group in groups_of(tiles_of_round(kind, n))[i:i + 1]:
                        g = state["g"]
                        act.wait_ge(turned.handle, turned.at(stack, l, g0 + g + 1))
                        w = len(group) * P
                        act.activation(turned_buffer(kind, g)[:, 0:w], ps[:, 6, 0:w], ACT.Copy
                                       ).then_inc(turned_out.handle, 1)
                        state["g"] += 1

                def head_squares(n):
                    act.wait_ge(weighted.handle, weighted.at(stack, l, r0 + n + 1))
                    if n >= 2:
                        act.wait_ge(headed.handle, headed.at(stack, l, r0 + n - 1))
                    raw = raw_buffer(n)
                    act.activation(raw, ps[:, 7, :], ACT.Copy).then_inc(raw_heads.handle, 1)
                    act.wait_ge(raw_heads.handle, raw_heads.at(stack, l, n + 1))
                    for t in range(4):
                        last = act.activation(st[:, 15, t * P:(t + 1) * P], raw[:, t * P:(t + 1) * P], ACT.Square,
                                              scale=rinv[:, n % 2, 2 * t:2 * t + 1], accum_out=ssq[:, t:t + 1])
                    last.then_inc(head_sq.handle, 1)

                def step(u):
                    if 3 <= u < len(units) + 3:
                        groups(u - 3, 0)
                    if 1 <= u < len(units) + 1:
                        exps(u - 1)
                    if 3 <= u < len(units) + 3:
                        groups(u - 3, 1)
                    for n in range(NB):
                        if kind == "dif" and u == heads_step(kind, n) + 2:
                            act.wait_ge(back.handle, back.at(stack, l, n + 1))
                            act.activation(st[:, 4:8, n * P:(n + 1) * P], ps[:, 6, :].rearrange("p (c q) -> p c q", c=4),
                                           ACT.Identity, scale=cur[:, C_DN:C_DN + 1]).then_inc(mixed_out.handle, 1)
                    if kind == "dif" and u % 4 == 3 and 0 <= u // 4 - 1 < NB:
                        head_squares(u // 4 - 1)

                return [lambda u=u: step(u) for u in range(STEPS)]

            act.dma_start(par[:, 0:NPAR], par_in).then_inc(par_in_sem.handle, 16)
            for c in range(KC):
                act.dma_start(xt[:, c, :], x_in[c, :, :]).then_inc(x_in_sem[c].handle, 16)
            act.dma_start(ident, c_ident).then_inc(const_in.handle, 16)
            act.dma_start(mask_gqa[:, :], c_gqa).then_inc(const_in.handle, 16)
            act.dma_start(st[:, 0, 0:DEPTH * 4 * HD], lam_in).then_inc(lam_sem.handle, 16)
            act.wait_ge(par_in_sem.handle, 16)
            for c in range(KC):
                act.wait_ge(x_in_sem[c].handle, 16)
                split_hi(0, lambda c: xt[:, c, :], lambda c: par[:, O_FIRST + c:O_FIRST + c + 1], chunks=[c])
                if c >= 3:
                    act.wait_ge(dve_own, c - 2)
                squares(c)
            act.wait_ge(lam_exp.handle, 1)
            act.activation(small[:, 4:8], small[:, 0:4], ACT.Exp).then_inc(lam_exp.handle, 1)

            with act.Fori(0, DEPTH) as l:
                act.wait_ge(cur_ready.handle, cur_ready.at(0, l, 1))
                take_factor(spread_ready.at(0, l, 1))
                act.dma_start(st[:, 21:23, :], c_rope.rearrange("a p n -> p a n")).then_inc(rope_in.handle, 32)
                for i, slot in enumerate((19, 20, 17)):
                    act.wait_ge(taken.handle, taken.at(0, l, i + 1))
                    for a in range(4):
                        to = 32 * (a ^ 1)
                        act.dma_start(st[to:to + 32, i, :], st[32 * a:32 * a + 32, slot, :]).then_inc(swapped[i].handle, 16)
                for i in range(2):
                    act.wait_ge(taken.handle, taken.at(0, l, 4 + 2 * i + 1))
                    act.activation(st[:, (9, 11)[i], :], st[:, (9, 11)[i], :], ACT.Tanh, scale=0.5
                                   ).then_inc(tanh_ready.handle, 1)
                    if i == 0:
                        v3 = lambda slot, g: st[:, slot, g * HALF:(g + 1) * HALF].rearrange("p (b c) -> p b c", b=4)
                        take_values(0, l, 0, lambda g: v3(18, g))
                steps = attention(0, l, "gqa", 0, 0, 0)
                for n in range(8, 19):
                    if n > 8:
                        for work in share("gqa", steps, n - 9):
                            work()
                    if n < 16:
                        act.wait_ge(taken.handle, taken.at(0, l, n + 1))
                        act.activation(st[:, 10 + n % 2, :], st[:, 8 + n % 2, :], ACT.Tanh, scale=0.5
                                       ).then_inc(tanh_ready.handle, 1)
                for c in range(2):
                    act.wait_ge(centred.handle, centred.at(0, l, c + 1))
                    act.activation(st[:, 14 + c, :], st[:, 12 + c, :], ACT.Square).then_inc(lnsq_ready.handle, 1)
                take_factor(spread_ready.at(0, l, 2), slot=10)
                for c in range(2):
                    act.wait_ge(normed.handle, normed.at(0, l, c + 1))
                    act.activation(st[:, 12 + c, :], st[:, 12 + c, :], ACT.Identity,
                                   scale=cur[:, C_LNG + c:C_LNG + c + 1],
                                   bias=cur[:, C_LNB + c:C_LNB + c + 1]).then_inc(act_own, 1)
                    act.wait_ge(act_own, l * 2 + (c + 1))
                    act.activation(st[:, 14 + c, :], st[:, 12 + c, :], ACT.Tanh, scale=0.5
                                   ).then_inc(lnact_ready.handle, 1)
                dv3 = lambda c, g: st[:, 21 + g, :].rearrange("p (b x) -> p b x", b=4)[:, :, c * P:(c + 1) * P]
                take_values(0, l, 2, lambda g: dv3(0, g))
                act.wait_ge(done.handle, done.at(0, l, 28))
                raw = rpb_in[bass.ds(l, 1), :, :].rearrange("a g c -> (a g) c")[:, GRID_W - 1:GRID_W - 1 + GRID_W * (SKEW - 1)
                                                                                ].rearrange("g (q s) -> q g s", s=SKEW - 1)
                table = flat(space_lo, 0, 4)[:, 0:4 * ND * GRID_W].rearrange("p (g c) -> p g c", c=GRID_W)
                for to, of in ((table[0:64], raw), (table[64:128, 1:4 * ND], raw[:, 0:4 * ND - 1]),
                               (table[64:128, 0:1], raw[:, 0:1])):
                    act.dma_start(to, of[:, :, 0:GRID_W]).then_inc(bias_in.handle, 16)
                act.wait_ge(conv_out.handle, conv_out.at(0, l, 2))
                act.dma_start(st[:, 15, 0:11 * GRID_W], c_na).then_inc(bias_in.handle, 16)
                split_hi(0, lambda c: st[:, c, :], chunks=range(4))
                take_values(0, l, 4, lambda g: dv3(1, g))
                for work in attention(0, l, "na", ag["pieces"], ag["groups"], NB):
                    work()
                act.wait_ge(mixed_out.handle, mixed_out.at(0, l, 2 * NB))
                split_hi(0, lambda c: st[:, c, :], chunks=range(4, 8))
                gains = lambda c: cur[:, C_NEXT + c:C_NEXT + c + 1]
                for c in range(KC):
                    act.wait_ge(taken.handle, taken.at(0, l, 36 + c + 1))
                    squares(c, cur[:, C_POST + c:C_POST + c + 1])
                    act.activation(st[:, ACC_X if c == 0 else SQ_X[c % 2], :], xt[:, c, :], ACT.Square
                                   ).then_inc(squared_x.handle, 1)
                    if c < 4:
                        split_hi(0, lambda c: xt[:, c, :], gains, chunks=[c])
                split_hi(0, lambda c: xt[:, c, :], gains, chunks=range(4, KC))

            take_factor(spread_ready.mid(1), slot=FAC_X)

            with act.Fori(0, DEPTH) as l:
                act.wait_ge(cur_ready.handle, cur_ready.at(1, l, 1))
                take_factor(spread_ready.at(1, l, 1))
                for k in range(4):
                    act.wait_ge(taken.handle, taken.at(1, l, k + 1))
                    act.activation(st[:, 10 + k % 2, :], st[:, 8 + k % 2, :], ACT.Tanh, scale=0.5
                                   ).then_inc(tanh_ready.handle, 1)
                vals = lambda slot, g, c: (st[:, slot + 2 * g:slot + 2 * g + 2, :]
                                           .rearrange("p a (b x) -> p (a b) x", b=2)[:, :, c * P:(c + 1) * P])
                for c in range(4):
                    take_values(1, l, 2 * c, lambda g: vals(14, g, c))
                    if c == 2:
                        act.dma_start(st[:, 8, :], c_ret).then_inc(retc_in.handle, 16)
                unread = mask_gqa[:, :].bitcast(mybir.dt.bfloat16)
                for n in range(NB):
                    act.wait_ge(r_summed.handle, r_summed.at(1, l, n + 1))
                    for t in range(4):
                        last = act.activation(unread[:, t * P:(t + 1) * P], ps[:, 6, t * P:(t + 1) * P], ACT.Square,
                                              accum_out=ssq[:, t:t + 1])
                    last.then_inc(r_squared.handle, 1)
                for c in (0, 1, 2):
                    take_values(1, l, 8 + 2 * c, lambda g: vals(10, g, c))
                act.wait_ge(done.handle, done.at(1, l, 24))
                act.dma_start(space_lo[:, :, :], c_alibi.rearrange("h p n -> p h n")).then_inc(alibi_in.handle, 16)
                act.wait_ge(r_out.handle, r_out.at(1, l, NB))
                split_hi(1, lambda c: st[:, c, :], chunks=range(4))
                take_values(1, l, 14, lambda g: vals(10, g, 3))
                for work in attention(1, l, "dif", 0, 0, 0):
                    work()
                act.wait_ge(mixed_out.handle, mixed_out.at(1, l, NB))
                split_hi(1, lambda c: st[:, c, :], chunks=range(4, 8))
                gains = lambda c: cur[:, C_FN + c:C_FN + c + 1]
                for c in range(KC):
                    act.wait_ge(taken.handle, taken.at(1, l, 32 + c + 1))
                    squares(c)
                    if c < 4:
                        split_hi(1, lambda c: xt[:, c, :], gains, chunks=[c])
                split_hi(1, lambda c: xt[:, c, :], gains, chunks=range(4, KC))
                take_factor(spread_ready.at(1, l, 2))
                n, chunk0 = 40, 0
                for group in FFN_GROUPS:
                    for c in range(group):
                        act.wait_ge(taken.handle, taken.at(1, l, n + 2 * c + 1))
                        act.activation(st[:, 18 + c % 2, :], st[:, 16 + c % 2, :], ACT.Tanh, scale=0.5
                                       ).then_inc(tanh_ready.handle, 1)
                        act.wait_ge(gated.handle, gated.at(1, l, chunk0 + c + 1))
                        act.activation(hid_hi[:, c, :], st[:, 16 + c % 2, :], ACT.Copy
                                       ).then_inc(hid_hi_ready.handle, 1)
                    n += 2 * group + KC
                    chunk0 += group
                for c in range(KC):
                    act.wait_ge(taken.handle, taken.at(1, l, BLOCKS[1] - KC + c + 1))
                    squares(c)
                    split_hi(1, lambda c: xt[:, c, :], lambda c: cur[:, C_NEXT + c:C_NEXT + c + 1], chunks=[c])

            take_factor(spread_ready.end(1))
            for c in range(KC):
                act.wait_ge(out_ready.handle, c + 1)
                act.dma_start(out[c, :, :], xt[:, c, :]).then_inc(out_sem.handle, 16)
            act.wait_ge(out_sem.handle, 16 * KC)

        @block.vector
        def _(dve):
            own = Chain(dve, dve_own)
            link = own.link

            def evacuate(stack, l, n, to):
                j = n % 2
                dve.wait_ge(done.handle, done.at(stack, l, n + 1))
                dve.tensor_tensor(to, ps[:, 2 * j:2 * j + 2, :].rearrange("p a b -> p (a b)"), rfac[:, :], ALU.mult
                                  ).then_inc(taken.handle, 1)

            def add_to_x(stack, l, n, c):
                dve.wait_ge(done.handle, done.at(stack, l, n + 1))
                last = dve.tensor_tensor(xt[:, c, :], xt[:, c, :],
                                         flat(ps, 2 * (n % 2), 2), ALU.add)
                last.then_inc(taken.handle, 1)

            def split_lo(stack, l, base, source, scale=None, chunks=range(KC)):
                for c in chunks:
                    dve.wait_ge(hi_ready.handle, hi_ready.at(stack, l, base + c + 1))
                    if scale:
                        i = dve.scalar_tensor_tensor(in_lo[:, c, :], source(c), scale(c), in_hi[:, c, :].bitcast(F32),
                                                     ALU.mult, ALU.subtract)
                    else:
                        i = dve.tensor_tensor(in_lo[:, c, :], source(c), in_hi[:, c, :].bitcast(F32), ALU.subtract)
                    i.then_inc(lo_ready.handle, 1)

            def sum_squares(wait, c):
                dve.wait_ge(squared.handle, wait)
                i = dve.tensor_tensor(st[:, ACC, :], st[:, ACC, :], st[:, SQ[c % 2], :], ALU.add)
                if c == KC - 1:
                    i.then_inc(acc_ready.handle, 1)
                else:
                    link(i)

            def sum_squares_x(wait, c):
                dve.wait_ge(squared_x.handle, wait)
                i = dve.tensor_tensor(st[:, ACC_X, :], st[:, ACC_X, :], st[:, SQ_X[c % 2], :], ALU.add)
                if c == KC - 1:
                    i.then_inc(acc_x_ready.handle, 1)
                else:
                    link(i)

            def rsqrt(x, y, t, steps=(0, 1, 2, 3)):
                if 0 in steps:
                    link(dve.tensor_scalar(t.bitcast(I32), x.bitcast(I32), 1, None, ALU.logical_shift_right))
                    link(dve.tensor_scalar(y.bitcast(I32), t.bitcast(I32), -1.0, float(0x5F3759DF), ALU.mult, ALU.add))
                for _ in range(len(steps) - (0 in steps)):
                    link(dve.tensor_tensor(t, y, y, ALU.mult))
                    link(dve.scalar_tensor_tensor(t, t, -0.5, x, ALU.mult, ALU.mult))
                    link(dve.scalar_tensor_tensor(y, t, 1.5, y, ALU.add, ALU.mult))

            def row_factor(wait, count, diag=DIAG, after=None):
                dve.wait_ge(stat_ready.handle, wait)
                if after is None:
                    link(dve.tensor_scalar(stat, ps[:, 4, 0:8], 1.0 / count, EPS, ALU.mult, ALU.add))
                    rsqrt(stat, root, tmp)
                else:
                    link(dve.tensor_tensor(tmp, after, after, ALU.mult))
                    link(dve.scalar_tensor_tensor(stat, ps[:, 4, 0:8], 1.0 / count, tmp, ALU.mult, ALU.mult))
                    link(dve.tensor_scalar(stat, stat, EPS, None, ALU.add))
                    rsqrt(stat, root, tmp)
                    link(dve.tensor_tensor(root, root, after, ALU.mult))
                dve.tensor_tensor(st[:, diag, :].rearrange("p (b c) -> p b c", b=NB),
                                  ident.unsqueeze(1).broadcast_to([P, NB, P]),
                                  root.unsqueeze(2).broadcast_to([P, NB, P]), ALU.mult).then_inc(diag_ready.handle, 1)

            def attention(stack, l, kind, p0, g0, r0, bias, finish):
                maps = 2 if kind == "dif" else 1
                m0 = ag["maps"] if kind == "na" else 0
                width = P if kind == "dif" else HD
                units = [(n, t) for n in range(NB) for t in range(4)]
                state = {"p": 0}

                def scores(u, i):
                    n, t = units[u]
                    tiles = tiles_of_round(kind, n)
                    for piece in pieces_of(tiles)[i:i + 1]:
                        for j in range(maps):
                            m = maps * u + j
                            i = maps * t + j
                            first = cur[:, C_SINK + t:C_SINK + t + 1] if kind == "gqa" else 3.0e38
                            dve.wait_ge(scored.handle, scored.at(stack, l, p0 + state["p"] + 1))
                            if piece[0] > tiles[0]:
                                first = negm[:, n % 2, i:i + 1]
                                dve.wait_ge(biased.handle, biased.at(stack, l, p0 + state["p"] + 1 - maps))
                            elif m >= exp_buffers(kind):
                                turned_units = (m - exp_buffers(kind)) // maps + 1
                                gi = sum(len(groups_of(tiles_of_round(kind, units[v][0]))) for v in range(turned_units))
                                dve.wait_ge(turned.handle, turned.at(stack, l, g0 + gi))
                            dve.sem_inc(dve_step)
                            a, w = (piece[0] - tiles[0]) * P, len(piece) * P
                            dve.tensor_tensor_reduce(exp_buffer(kind, m)[:, a:a + w], ps[:, 4 + state["p"] % 2, 0:w],
                                                     bias(n, t)[:, a:a + w], -SCALE, first,
                                                     ALU.add, ALU.min, negm[:, n % 2, i:i + 1]).then_inc(biased.handle, 1)
                            state["p"] += 1

                def sink(n):
                    dve.wait_ge(biased.handle, biased.at(stack, l, p0 + state["p"]))
                    dve.tensor_tensor(comb, negm[:, n % 2, 0:4], cur[:, C_SINK:C_SINK + 4], ALU.subtract
                                      ).then_inc(sink_ready.handle, 1)

                def mix(u):
                    n, t = units[u]
                    cols = (n + 1) * P
                    dve.wait_ge(expd.handle, expd.at(stack, l, m0 + 2 * u + 2))
                    r = rinv[:, n % 2, :]
                    link(dve.reciprocal(r[:, 2 * t:2 * t + 2], lsum[:, n % 2, 2 * t:2 * t + 2]))
                    link(dve.scalar_tensor_tensor(comb[:, t:t + 1], lsum[:, n % 2, 2 * t:2 * t + 1],
                                                  cur[:, C_NLAM:C_NLAM + 1], r[:, 2 * t + 1:2 * t + 2],
                                                  ALU.mult, ALU.mult))
                    e0, e1 = (exp_buffer(kind, 2 * u + j)[:, 0:cols] for j in range(2))
                    dve.scalar_tensor_tensor(e0, e1, comb[:, t:t + 1], e0, ALU.mult, ALU.add
                                             ).then_inc(mixed.handle, 1)

                def head_root(n):
                    dve.wait_ge(head_sq.handle, head_sq.at(stack, l, n + 1))
                    link(dve.tensor_scalar(stat[:, 0:4], ssq[:, 0:4], 1.0 / P, EPS, ALU.mult, ALU.add))
                    rsqrt(stat[:, 0:4], root[:, 0:4], tmp[:, 0:4], (0, 1))

                def heads(n):
                    if kind == "dif":
                        rsqrt(stat[:, 0:4], root[:, 0:4], tmp[:, 0:4], (3,))
                        link(dve.tensor_tensor(factor, root[:, 0:4],
                                               rinv[:, n % 2, :].rearrange("p (a b) -> p a b", b=2)[:, :, 0], ALU.mult))
                    else:
                        dve.wait_ge(expd.handle, expd.at(stack, l, m0 + 4 * n + 4))
                        total = lsum[:, n % 2, 0:4]
                        if kind == "gqa":
                            dve.wait_ge(sink_exp.handle, sink_exp.at(stack, l, n + 1))
                            link(dve.tensor_tensor(total, total, esink, ALU.add))
                        link(dve.reciprocal(factor, total))
                        dve.wait_ge(weighted.handle, weighted.at(stack, l, r0 + n + 1))
                    outputs = raw_buffer(n) if kind == "dif" else ps[:, 7, 0:4 * width]
                    if n >= 2:
                        dve.wait_ge(back.handle, back.at(stack, l, r0 + n - 1))
                    dve.tensor_tensor(head_buffer(kind, n)[:, 0:4 * width].rearrange("p (t e) -> p t e", t=4),
                                      outputs.rearrange("p (t e) -> p t e", t=4),
                                      factor.unsqueeze(2).broadcast_to([P, 4, width]), ALU.mult
                                      ).then_inc(headed.handle, 1)

                def step(u):
                    if kind == "dif" and 2 <= u < len(units) + 2:
                        mix(u - 2)
                    if u < len(units):
                        scores(u, 0)
                    if kind == "dif" and u % 4 == 1 and u >= 9:
                        rsqrt(stat[:, 0:4], root[:, 0:4], tmp[:, 0:4], (2,))
                    if u < len(units):
                        scores(u, 1)
                    for n in range(NB):
                        if kind == "dif" and u == heads_step(kind, n) - 1:
                            head_root(n)
                        if u == heads_step(kind, n):
                            heads(n)
                        if finish and u == heads_step(kind, n) + 2:
                            dve.wait_ge(back.handle, back.at(stack, l, r0 + n + 1))
                            finish(n).then_inc(mixed_out.handle, 1)
                    if kind == "gqa" and u % 4 == 3 and u < len(units):
                        sink(u // 4)

                return [lambda u=u: step(u) for u in range(STEPS)]

            dve.engine_nop().then_inc(taken.handle, 2)
            for c in range(KC):
                split_lo(0, 0, -8, lambda c: xt[:, c, :], lambda c: par[:, O_FIRST + c:O_FIRST + c + 1], chunks=[c])
                if c:
                    sum_squares(c + 1, c)
            dve.wait_ge(const_in.handle, 16 * 2)
            dve.wait_ge(lam_sem.handle, 16)
            own.restart()
            lam = st[:, 0, 0:DEPTH * 4 * HD].rearrange("p (l v d) -> p l v d", l=DEPTH, v=4)
            for l in range(DEPTH):
                for i in range(2):
                    k = 2 * l + i
                    link(dve.tensor_tensor_reduce(st[:, 1, k * HD:(k + 1) * HD], lam[:, l, 2 * i, :], lam[:, l, 2 * i + 1, :],
                                                  1.0, 0.0, ALU.mult, ALU.add, small[:, k:k + 1]))
            dve.engine_nop().then_inc(lam_exp.handle, 1)
            dve.wait_ge(lam_exp.handle, 2)
            for l in range(DEPTH):
                lam_init = 0.8 - 0.6 * float(np.exp(-0.3 * l))
                o = O2 + l * W2
                link(dve.tensor_tensor(tmp[:, 0:1], small[:, 4 + 2 * l + 1:4 + 2 * l + 2], small[:, 4 + 2 * l:4 + 2 * l + 1],
                                       ALU.subtract))
                link(dve.tensor_scalar(par[:, o + C_NLAM:o + C_NLAM + 1], tmp[:, 0:1], -lam_init, None, ALU.add))
                link(dve.tensor_scalar(par[:, o + C_RN:o + C_RN + 1], par[:, o + C_RN:o + C_RN + 1], 0.5, None, ALU.mult))
                link(dve.tensor_scalar(par[:, o + C_DN:o + C_DN + 1], par[:, o + C_DN:o + C_DN + 1], 1.0 - lam_init, None,
                                       ALU.mult))
                o = l * W1 + C_SINK
                link(dve.tensor_scalar(par[:, o:o + 4], par[:, o:o + 4], -1.0, None, ALU.mult))
            o = (DEPTH - 1) * W1 + C_NEXT
            link(dve.tensor_tensor(par[:, o:o + 8], par[:, o:o + 8], par[:, O_FIRST2:O_FIRST2 + 8], ALU.mult))

            with dve.Fori(0, DEPTH) as l:
                own.restart()
                dve.wait_ge(lo_ready.handle, lo_ready.at(0, l, 0))
                dve.tensor_copy(cur[:, :], par[:, bass.ds(l * W1, W1)]).then_inc(cur_ready.handle, 1)
                row_factor(stat_ready.at(0, l, 1), D)
                dve.wait_ge(fac_ready.handle, fac_ready.at(0, l, 1))

                def rotate(i, slot):
                    dve.wait_ge(swapped[i].handle, swapped[i].at(0, l, 4 * 16))
                    other, chunk = st[:, i, :], st[:, slot, :]
                    link(dve.tensor_tensor(other, other, st[:, 22, :], ALU.mult))
                    link(dve.tensor_tensor(chunk, chunk, st[:, 21, :], ALU.mult))
                    dve.tensor_tensor(chunk, chunk, other, ALU.add).then_inc(roped.handle, 1)
                    dve.wait_ge(roped.handle, roped.at(0, l, i + 1))

                def gate_input(i):
                    dve.wait_ge(tanh_ready.handle, tanh_ready.at(0, l, i + 1))
                    dve.wait_ge(taken.handle, taken.at(0, l, 4 + 2 * i + 2))
                    gate_slot, input_slot = ((9, 10), (11, 8))[i]
                    link(dve.scalar_tensor_tensor(st[:, 14 + i, :], st[:, gate_slot, :], 1.0, st[:, input_slot, :],
                                                  ALU.add, ALU.mult))

                def tap(acc, source, weight, d, first):
                    a, b = max(0, -d), S - max(0, d)
                    if first:
                        return dve.tensor_scalar(acc, source, weight, None, ALU.mult)
                    return dve.scalar_tensor_tensor(acc[:, a:b], source[:, a + d:b + d], weight, acc[:, a:b],
                                                    ALU.mult, ALU.add)

                mid = TAPS_A // 2
                order = [mid] + [k for k in range(TAPS_A) if k != mid]
                taps = [(k, c) for k in order for c in range(2)]

                def conv_taps(count):
                    for _ in range(min(count, len(taps))):
                        k, c = taps.pop(0)
                        w = cur[:, C_CAW + TAPS_A * c + k:C_CAW + TAPS_A * c + k + 1]
                        link(tap(st[:, 12 + c, :], st[:, 14 + c, :], w, k - mid, k == mid))

                def gate(k):
                    dve.wait_ge(tanh_ready.handle, tanh_ready.at(0, l, 2 + k + 1))
                    link(dve.scalar_tensor_tensor(st[:, (4, 5, 0, 1, 2, 3, 6, 7)[k], :], st[:, 10 + k % 2, :], 1.0,
                                                  st[:, 8 + k % 2, :],
                                                  ALU.add, ALU.mult))

                def back_to_chunks(first):
                    def finish(n):
                        y = st[:, first:first + 2, n * P:(n + 1) * P]
                        return dve.scalar_tensor_tensor(y, ps[:, 6, 0:2 * P].rearrange("p (c q) -> p c q", c=2), 0.5, y,
                                                        ALU.mult, ALU.mult)
                    return finish

                def gated_conv(i, stage):
                    cx, y = st[:, 10, :], st[:, 11, :]
                    w = lambda k: cur[:, C_CBW + TAPS_B * i + k:C_CBW + TAPS_B * i + k + 1]
                    if stage == 0:
                        dve.wait_ge(taken.handle, taken.at(0, l, 18 + 3 * i))
                        link(dve.tensor_tensor(cx, st[:, 8, :], st[:, 9, :], ALU.mult))
                        link(tap(y, cx, w(1), 0, True))
                        link(tap(y, cx, w(0), -1, False))
                        link(tap(y, cx, w(2), 1, False))
                    else:
                        dve.wait_ge(taken.handle, taken.at(0, l, 19 + 3 * i))
                        link(dve.tensor_tensor(y, y, st[:, 8, :], ALU.mult))
                        link(dve.scalar_tensor_tensor(st[:, 2 + i, :], y, 0.5, st[:, 2 + i, :], ALU.mult, ALU.mult))

                evacuate(0, l, 0, st[:, 19, :])
                evacuate(0, l, 1, st[:, 20, :])
                evacuate(0, l, 2, st[:, 17, :])
                evacuate(0, l, 3, st[:, 8, :])
                dve.wait_ge(rope_in.handle, rope_in.at(0, l, 32))
                rotate(0, 19)
                evacuate(0, l, 4, st[:, 9, :])
                rotate(1, 20)
                evacuate(0, l, 5, st[:, 10, :])
                rotate(2, 17)
                evacuate(0, l, 6, st[:, 11, :])
                gate_input(0)
                dve.wait_ge(vt_ready.handle, vt_ready.at(0, l, 2))
                evacuate(0, l, 7, st[:, 8, :])
                gate_input(1)
                steps = attention(0, l, "gqa", 0, 0, 0,
                                  lambda n, t: mask_gqa[:, (tiles_of_round("gqa", n)[0] - n + 1) * P:
                                                        (tiles_of_round("gqa", n)[-1] - n + 2) * P],
                                  back_to_chunks(4))
                conv_taps(4)
                evacuate(0, l, 8, st[:, 8, :])
                for n in range(9, 19):
                    for i, work in enumerate(share("gqa", steps, n - 9)):
                        work()
                        conv_taps(1)
                        if i == 1 and n <= 16:
                            gate(n - 9)
                    if n == 18:
                        gated_conv(0, 0)
                    evacuate(0, l, n, st[:, 8 + n % 2, :])
                conv_taps(2)
                gated_conv(0, 1)
                conv_taps(6)
                evacuate(0, l, 19, st[:, 8, :])
                conv_taps(7)
                evacuate(0, l, 20, st[:, 9, :])
                conv_taps(len(taps))
                for c in range(2):
                    last = dve.tensor_scalar(st[:, 12 + c, :], st[:, 12 + c, :], 0.5, cur[:, C_CAB + c:C_CAB + c + 1],
                                             ALU.mult, ALU.add)
                last.then_inc(conv_ready.handle, 1)
                gated_conv(1, 0)
                evacuate(0, l, 21, st[:, 8, :])
                gated_conv(1, 1)
                evacuate(0, l, 22, st[:, 19, :])
                evacuate(0, l, 23, st[:, 20, :])
                dve.wait_ge(mean_ready.handle, mean_ready.at(0, l, 1))
                for c in range(2):
                    dve.scalar_tensor_tensor(st[:, 12 + c, :], flat(ps, 4, 2), -1.0 / (2 * P),
                                             st[:, 12 + c, :], ALU.mult, ALU.add).then_inc(centred.handle, 1)
                dve.wait_ge(lnsq_ready.handle, lnsq_ready.at(0, l, 2))
                dve.tensor_tensor(st[:, 14, :], st[:, 14, :], st[:, 15, :], ALU.add).then_inc(lnsq_sum.handle, 1)
                evacuate(0, l, 24, st[:, 17, :])
                row_factor(stat_ready.at(0, l, 2), 2 * P, DIAG_LN)
                evacuate(0, l, 25, st[:, 18, :])
                dve.wait_ge(fac_ready.handle, fac_ready.at(0, l, 2))
                for c in range(2):
                    dve.tensor_tensor(st[:, 12 + c, :], st[:, 12 + c, :], st[:, 10, :], ALU.mult
                                      ).then_inc(normed.handle, 1)
                evacuate(0, l, 26, st[:, 8, :])
                for c in range(2):
                    dve.wait_ge(lnact_ready.handle, lnact_ready.at(0, l, c + 1))
                    link(dve.scalar_tensor_tensor(st[:, 12 + c, :], st[:, 14 + c, :], 1.0, st[:, 12 + c, :],
                                                  ALU.add, ALU.mult))
                    dve.scalar_tensor_tensor(st[:, c, :], st[:, 12 + c, :], 0.25, st[:, c, :], ALU.mult, ALU.mult
                                             ).then_inc(conv_out.handle, 1)
                evacuate(0, l, 27, st[:, 9, :])
                dve.wait_ge(conv_out.handle, conv_out.at(0, l, 2))
                split_lo(0, l, 0, lambda c: st[:, c, :], chunks=range(4))

                dve.wait_ge(bias_in.handle, bias_in.at(0, l, 64))
                table = flat(space_lo, 0, 4)[:, 0:4 * ND * GRID_W]
                inner = flat(st, 12, 3)[:, 0:4 * 10 * GRID_W]
                by_row = table.rearrange("p (g c) -> p g c", c=GRID_W)
                link(dve.scalar_tensor_tensor(by_row, by_row, 1.0 / SCALE,
                                              st[:, 15, 0:GRID_W].unsqueeze(1).broadcast_to([P, 4 * ND, GRID_W]),
                                              ALU.mult, ALU.add))
                table_h = table.rearrange("p (h r) -> p h r", h=4)
                inner_h = inner.rearrange("p (h r) -> p h r", h=4)
                def na_bias(n, t):
                    if 2 <= n <= NB - 3:
                        return inner_h[:, t, :]
                    r = 2 * tiles_of_round("na", n)[0] - 2 * n + KH - 1
                    return table_h[:, t, r * GRID_W:(r + 8) * GRID_W]

                add_to_x(0, l, 28, 0)
                add_to_x(0, l, 29, 1)
                steps = attention(0, l, "na", ag["pieces"], ag["groups"], NB, na_bias, back_to_chunks(6))
                for c in range(2, KC - 1):
                    for work in share("na", steps, c - 2):
                        work()
                    add_to_x(0, l, 28 + c, c)
                    if c == 2:
                        dve.tensor_tensor(inner_h, table_h[:, :, 3 * GRID_W:13 * GRID_W],
                                          st[:, 15, GRID_W:11 * GRID_W].unsqueeze(1).broadcast_to([P, 4, 10 * GRID_W]),
                                          ALU.add).then_inc(bias_ready.handle, 1)
                        dve.wait_ge(bias_ready.handle, bias_ready.at(0, l, 1))
                dve.wait_ge(mixed_out.handle, mixed_out.at(0, l, 2 * NB))
                split_lo(0, l, 0, lambda c: st[:, c, :], chunks=range(4, 8))
                add_to_x(0, l, 35, 7)
                gains = lambda c: cur[:, C_NEXT + c:C_NEXT + c + 1]
                for c in range(KC):
                    add_to_x(0, l, 36 + c, c)
                    if c >= 2:
                        sum_squares(squared.at(0, l, c), c - 1)
                        sum_squares_x(squared_x.at(0, l, c), c - 1)
                    if 1 <= c <= 4:
                        split_lo(0, l, 8, lambda c: xt[:, c, :], gains, chunks=[c - 1])
                sum_squares(squared.at(0, l, KC), KC - 1)
                sum_squares_x(squared_x.at(0, l, KC), KC - 1)
                split_lo(0, l, 8, lambda c: xt[:, c, :], gains, chunks=range(4, KC))

            own.restart()
            row_factor(stat_ready.mid(1), D, DIAG_X)
            link(dve.tensor_copy(prior, root))
            dve.wait_ge(fac_ready.handle, fac_ready.mid(1))
            dve.wait_ge(lo_ready.handle, lo_ready.mid(0))
            for c in range(KC):
                link(dve.scalar_tensor_tensor(xt[:, c, :], xt[:, c, :], par[:, O_FIN1 + c:O_FIN1 + c + 1], st[:, FAC_X, :],
                                              ALU.mult, ALU.mult))

            with dve.Fori(0, DEPTH) as l:
                own.restart()
                dve.wait_ge(lo_ready.handle, lo_ready.at(1, l, 0))
                dve.tensor_copy(cur[:, 0:W2], par[:, bass.ds(l * W2 + O2, W2)]).then_inc(cur_ready.handle, 1)
                row_factor(stat_ready.at(1, l, 1), D, after=prior)
                link(dve.memset(prior, 1.0))
                dve.wait_ge(fac_ready.handle, fac_ready.at(1, l, 1))
                for k in range(4):
                    evacuate(1, l, k, st[:, 8 + k % 2, :])
                    if k:
                        dve.wait_ge(tanh_ready.handle, tanh_ready.at(1, l, k))
                        link(dve.scalar_tensor_tensor(st[:, k - 1, :], st[:, 10 + (k - 1) % 2, :], 1.0,
                                                      st[:, 8 + (k - 1) % 2, :], ALU.add, ALU.mult))
                dve.wait_ge(tanh_ready.handle, tanh_ready.at(1, l, 4))
                link(dve.scalar_tensor_tensor(st[:, 3, :], st[:, 11, :], 1.0, st[:, 9, :], ALU.add, ALU.mult))
                for k in range(4):
                    evacuate(1, l, 4 + k, st[:, 10 + k, :])
                for k in range(4):
                    if k >= 2:
                        dve.wait_ge(vt_ready.handle, vt_ready.at(1, l, 2 * (k - 1)))
                    evacuate(1, l, 8 + k, st[:, 8 + k % 2, :])

                tables = st[:, 8, :]
                decay, q_decay, k_decay = tables[:, 0:512], tables[:, 512:768], tables[:, 768:1024]

                def r_decays(n):
                    dve.wait_ge(r_scored.handle, r_scored.at(1, l, n + 1))
                    if n == 0:
                        dve.wait_ge(retc_in.handle, retc_in.at(1, l, 16))
                        link(dve.memset(state_of(0), 0.0))
                        link(dve.memset(state_of(1), 0.0))
                    else:
                        dve.wait_ge(r_summed.handle, r_summed.at(1, l, n))
                    dve.tensor_tensor(st[:, 9, 0:512].rearrange("p (a b) -> p a b", a=2), ps[:, 4:6, 0:256],
                                      decay.rearrange("p (a b) -> p a b", a=2), ALU.mult)
                    dve.tensor_tensor(st[:, 22, 0:256], ps[:, 4, 256:512], k_decay, ALU.mult)
                    dve.tensor_tensor(st[:, 22, 256:512].rearrange("p (c q) -> p c q", c=2),
                                      st[:, 10:12, n * P:(n + 1) * P],
                                      q_decay.rearrange("p (c q) -> p c q", c=2), ALU.mult).then_inc(r_decayed.handle, 1)

                def r_next(n):
                    dve.wait_ge(r_summed.handle, r_summed.at(1, l, n + 1))
                    if n < NB - 1:
                        for t in range(4):
                            b = HD * (t % 2)
                            a = slice(t * P, (t + 1) * P)
                            i = dve.scalar_tensor_tensor(state_of(n + 1)[b:b + HD, a], state_of(n)[b:b + HD, a],
                                                         chunk_decay(t), ps[b:b + HD, 5, 256 + (t // 2) * P:256 + (t // 2 + 1) * P],
                                                         ALU.mult, ALU.add)
                        i.then_inc(r_state.handle, 1)
                        dve.wait_ge(r_state.handle, r_state.at(1, l, n + 1))
                    dve.wait_ge(r_squared.handle, r_squared.at(1, l, n + 1))
                    link(dve.tensor_scalar(stat[:, 0:4], ssq[:, 0:4], 1.0 / P, EPS, ALU.mult, ALU.add))
                    rsqrt(stat[:, 0:4], root[:, 0:4], tmp[:, 0:4])
                    if n >= 1:
                        dve.wait_ge(r_back.handle, r_back.at(1, l, n))
                    dve.tensor_tensor(half[:, :].rearrange("p (t e) -> p t e", t=4),
                                      ps[:, 6, :].rearrange("p (t e) -> p t e", t=4),
                                      root[:, 0:4].unsqueeze(2).broadcast_to([P, 4, P]), ALU.mult
                                      ).then_inc(r_headed.handle, 1)

                def r_finish(n):
                    dve.wait_ge(r_back.handle, r_back.at(1, l, n + 1))
                    y = st[:, 0:4, n * P:(n + 1) * P]
                    dve.scalar_tensor_tensor(y, ps[:, 7, :].rearrange("p (c q) -> p c q", c=4), cur[:, C_RN:C_RN + 1], y,
                                             ALU.mult, ALU.mult).then_inc(r_out.handle, 1)

                places = (4, 5, 6, 7, 18, 19, 20, 21, 8, 9)
                for n in range(NB + 2):
                    if 1 <= n < NB + 1:
                        r_next(n - 1)
                    evacuate(1, l, 12 + n, st[:, places[n], :])
                    if n < NB:
                        r_decays(n)
                    if n >= 2:
                        r_finish(n - 2)
                evacuate(1, l, 22, st[:, 14, :])
                evacuate(1, l, 23, st[:, 15, :])

                dve.wait_ge(r_out.handle, r_out.at(1, l, NB))
                split_lo(1, l, 0, lambda c: st[:, c, :], chunks=range(4))
                dve.wait_ge(alibi_in.handle, alibi_in.at(1, l, 16))
                add_to_x(1, l, 24, 0)
                add_to_x(1, l, 25, 1)
                dve.wait_ge(lo_ready.handle, lo_ready.at(1, l, 4))
                steps = attention(1, l, "dif", 0, 0, 0, lambda n, t: space_lo[:, t, S - (n + 1) * P:S], None)
                for c in range(2, KC - 1):
                    for work in share("dif", steps, c - 2):
                        work()
                    add_to_x(1, l, 24 + c, c)
                dve.wait_ge(mixed_out.handle, mixed_out.at(1, l, NB))
                split_lo(1, l, 0, lambda c: st[:, c, :], chunks=range(4, 8))
                add_to_x(1, l, 31, 7)
                gains = lambda c: cur[:, C_FN + c:C_FN + c + 1]
                for c in range(KC):
                    add_to_x(1, l, 32 + c, c)
                    if c >= 2:
                        sum_squares(squared.at(1, l, c), c - 1)
                    if 1 <= c <= 4:
                        split_lo(1, l, 8, lambda c: xt[:, c, :], gains, chunks=[c - 1])
                sum_squares(squared.at(1, l, KC), KC - 1)

                split_lo(1, l, 8, lambda c: xt[:, c, :], gains, chunks=range(4, KC))
                row_factor(stat_ready.at(1, l, 2), D)
                dve.wait_ge(fac_ready.handle, fac_ready.at(1, l, 2))
                n, chunk0 = 40, 0

                def hidden_lo(c, i):
                    dve.wait_ge(hid_hi_ready.handle, hid_hi_ready.at(1, l, i + 1))
                    dve.tensor_tensor(hid_lo[:, c, :], st[:, 16 + c % 2, :], hid_hi[:, c, :].bitcast(F32), ALU.subtract
                                      ).then_inc(hid_lo_ready.handle, 1)

                for group in FFN_GROUPS:
                    for c in range(group):
                        i = chunk0 + c
                        g, t = st[:, 16 + c % 2, :], st[:, 18 + c % 2, :]
                        evacuate(1, l, n + 2 * c, g)
                        if c:
                            hidden_lo(c - 1, i - 1)
                        dve.wait_ge(tanh_ready.handle, tanh_ready.at(1, l, 4 + i + 1))
                        link(dve.scalar_tensor_tensor(t, t, 1.0, g, ALU.add, ALU.mult))
                        up = n + 2 * c + 1
                        dve.wait_ge(done.handle, done.at(1, l, up + 1))
                        dve.scalar_tensor_tensor(g, ps[:, 2 * (up % 2):2 * (up % 2) + 2, :].rearrange("p a b -> p (a b)"),
                                                 0.5, rfac[:, :], ALU.mult, ALU.mult).then_inc(taken.handle, 1)
                        dve.wait_ge(taken.handle, taken.at(1, l, up + 1))
                        dve.tensor_tensor(g, g, t, ALU.mult).then_inc(gated.handle, 1)
                    hidden_lo(group - 1, chunk0 + group - 1)
                    n += 2 * group
                    chunk0 += group
                    for c in range(KC):
                        add_to_x(1, l, n + c, c)
                        if chunk0 == HC and c >= 1:
                            if c >= 2:
                                sum_squares(squared.at(1, l, KC + c), c - 1)
                            split_lo(1, l, 16, lambda c: xt[:, c, :], lambda c: cur[:, C_NEXT + c:C_NEXT + c + 1],
                                     chunks=[c - 1])
                    n += KC
                sum_squares(squared.at(1, l, 2 * KC), KC - 1)
                split_lo(1, l, 16, lambda c: xt[:, c, :], lambda c: cur[:, C_NEXT + c:C_NEXT + c + 1], chunks=[KC - 1])

            own.restart()
            row_factor(stat_ready.end(1), D)
            dve.wait_ge(fac_ready.handle, fac_ready.end(1))
            for c in range(KC):
                dve.scalar_tensor_tensor(xt[:, c, :], xt[:, c, :], par[:, O_FIN2 + c:O_FIN2 + c + 1], rfac[:, :],
                                         ALU.mult, ALU.mult).then_inc(out_ready.handle, 1)


def gammas():
    return (1.0 - np.exp2(-5.0 - np.arange(4, dtype=np.float32))).astype(np.float32)


def chunk_decay(t):
    return float(np.exp(np.float32(P) * np.log(gammas()[t])))


def constants():
    f = np.float32
    eye = np.eye(P, dtype=f)
    inv = (f(10000.0) ** (-np.arange(0, HD, 2, dtype=f) / f(HD))).astype(f)
    ang = (np.arange(S, dtype=f)[None, :] * inv[:, None]).astype(f)
    rope = np.stack([np.tile(np.cos(ang), (4, 1)), np.tile(np.concatenate([-np.sin(ang), np.sin(ang)]), (2, 1))])
    q, k = np.arange(P)[:, None], np.arange(3 * P)[None, :] - P
    gqa = np.where(np.abs(k - q) <= P, 0.0, NEG / SCALE)
    c = np.arange(GRID_W)
    c0 = np.clip(c - KW // 2, 0, GRID_W - KW)
    col = (c[None, :] >= c0[:, None]) & (c[None, :] < c0[:, None] + KW)
    col = np.tile(np.where(col, 0.0, NEG / SCALE), (2, 1))
    row = np.arange(10)[None, :] - np.repeat(np.arange(2), GRID_W)[:, None]
    row = np.where((row >= 0) & (row < KH), 0.0, NEG / SCALE)
    na = np.concatenate([col, np.repeat(row, GRID_W, axis=1)], axis=1)
    lg = np.log(gammas())
    i = np.arange(P, dtype=f)
    rel = i[None, :] - i[:, None]
    decay = [np.where(rel >= 0, np.exp(np.maximum(rel, 0) * lg[t]), 0) * SCALE for t in (0, 2, 1, 3)]
    qd = [np.repeat(np.stack([np.exp((i + 1) * lg[2 * p]), np.exp((i + 1) * lg[2 * p + 1])]), HD, axis=0) for p in range(2)]
    kd = [np.repeat(np.exp((P - 1 - i) * g)[:, None], HD, axis=1) * SCALE for g in lg]
    ret = np.concatenate(decay + qd + kd, axis=1)
    r = np.arange(S)[None, :] - (S - P) - np.arange(P)[:, None]
    alibi = np.stack([np.where(r <= 0, 2.0 ** (-2.0 * (h + 1)) * r / SCALE, NEG / SCALE) for h in range(4)])
    return {"c_ident": eye, "c_rope": rope, "c_gqa": gqa, "c_na": na, "c_ret": ret, "c_alibi": alibi}


def columns(first, count):
    return [np.arange(first + P * c, first + P * (c + 1)) for c in range(count)]


def head_columns(first):
    heads = np.concatenate([np.arange(first + HD * h, first + HD * (h + 1)) for h in GQA_ORDER])
    return [heads[:P], heads[P:]]


def weight_block(w, rows, cols):
    part = w[rows][:, cols]
    k = part.shape[0] // P
    block = np.zeros((P, KC, P), w.dtype)
    block[:, :k] = part.reshape(k, P, P).transpose(1, 0, 2)
    return block.reshape(P, KC * P)


def weight_stream(i):
    blocks = []
    u, v, az, bb, bc, bx, bz = (columns(256 * n, 2) for n in range(7))
    cq, ck, cv, cz = head_columns(1792), columns(2048, 1), columns(2176, 1), head_columns(2304)
    dq, dk, dv, dz = (columns(2560 + 256 * n, 2) for n in range(4))
    every = slice(None)
    for l in range(DEPTH):
        order = cq + ck + cv + [v[0], u[0], v[1], u[1]] + cz + az + bz + dz
        order += [bc[0], bx[0], bb[0], bc[1], bx[1], bb[1]] + dq + dk + dv
        blocks += [weight_block(i["w_in"][l], every, c) for c in order]
        rows = np.concatenate([np.arange(512)] + head_columns(512) + [np.arange(768, 1024)])
        blocks += [weight_block(i["w_out"][l], r, c) for r in (rows[:512], rows[512:]) for c in columns(0, KC)]
    for l in range(DEPTH):
        order = columns(1024, 4) + columns(0, 8) + columns(1536, 12)
        blocks += [weight_block(i["w_in_2"][l], every, c) for c in order]
        blocks += [weight_block(i["w_out_2"][l], r, c) for r in (slice(0, 512), slice(512, 1024)) for c in columns(0, KC)]
        chunk = 0
        for group in FFN_GROUPS:
            for c in columns(P * chunk, group):
                blocks += [weight_block(i["w_gate_2"][l], every, c), weight_block(i["w_up_2"][l], every, c)]
            rows = np.arange(P * chunk, P * (chunk + group))
            blocks += [weight_block(i["w_down_2"][l], rows, c) for c in columns(0, KC)]
            chunk += group
    return np.stack(blocks)


def parameters(i):
    def chunks(v):
        return v.reshape(-1, P).T

    cols = []
    for l in range(DEPTH):
        cols += [chunks(i["norm_g"][l + 1] if l + 1 < DEPTH else i["final_norm_g"])]
        cols += [i["conv_a_w"][l][:, P * c:P * (c + 1)].T for c in range(2)]
        cols += [chunks(i[n][l]) for n in ("conv_a_b", "ln_a_g", "ln_a_b")]
        cols += [i["conv_b_w"][l][:, P * c:P * (c + 1)].T for c in range(2)]
        cols += [np.broadcast_to(i["swa_sink"][l][list(GQA_ORDER)], (P, 4))]
        cols += [np.ones((P, 8), np.float32) if l + 1 < DEPTH else chunks(i["final_norm_g"])]
    for l in range(DEPTH):
        cols += [chunks(i["attn_norm_2"][(l + 1) % DEPTH])]
        cols += [chunks(i[n][l]) for n in ("ffn_norm_2", "ret_norm_2", "diff_norm_2")]
        cols += [np.zeros((P, 1), np.float32)]
    cols += [chunks(v) for v in (i["norm_g"][0], i["attn_norm_2"][0], i["final_norm_g"], i["final_norm_2"])]
    return np.concatenate(cols, axis=1)


def kernel(**inputs):
    import concourse.bacc as bacc
    from concourse.bass_utils import run_bass_kernel_spmd

    i = {k: np.asarray(v) for k, v in inputs.items()}
    lam = np.stack([i[n] for n in ("lambda_q1_2", "lambda_k1_2", "lambda_q2_2", "lambda_k2_2")], axis=1)
    pad = np.pad(i["na_rpb"], ((0, 0), (0, 0), (0, 0), (GRID_W - KW, SKEW - GRID_W - KW + 1)))
    arrays = {
        "x_in": i["x"][0].T.reshape(KC, P, S),
        "w_in": weight_stream(i),
        "par_in": parameters(i),
        "lam_in": np.broadcast_to(lam.reshape(1, -1), (P, DEPTH * 4 * HD)),
        "rpb_in": np.broadcast_to(pad.reshape(DEPTH, 4 * ND, 1, SKEW), (DEPTH, 4 * ND, GRID_W, SKEW)
                                  ).reshape(DEPTH, 4 * ND, GRID_W * SKEW),
        **{k: v.astype(np.float32) for k, v in constants().items()},
    }
    arrays = {k: np.ascontiguousarray(v) for k, v in arrays.items()}
    nc = bacc.Bacc("TRN2", target_bir_lowering=False, num_devices=1, dynamic_dma_scratch_size=1024)
    args = {k: nc.dram_tensor(k, v.shape, F32, kind="ExternalInput").ap() for k, v in arrays.items()}
    out = nc.dram_tensor("out", (KC, P, S), F32, kind="ExternalOutput").ap()
    build(nc, out=out, **args)
    r = run_bass_kernel_spmd(nc, [arrays], core_ids=[0])
    return np.ascontiguousarray(r.results[0]["out"].reshape(D, S).T).reshape(1, S, D)
```
